# Optimizing a Trainium2 kernel written in Bass

```python
import math
import jax, jax.numpy as jnp
from jax import lax
import numpy as np

D_MODEL = 1024
BATCH = 1
SEQ = 128
DEPTH = 4
DEC_BATCH = 1
DEC_SEQ = 512
PAST_LEN = 128

GRID_W = 64
N_MIXERS = 3
N_MLA_LAYERS = (DEPTH + 2) // 3
N_SSD_LAYERS = (DEPTH + 1) // 3
N_MLSTM_LAYERS = DEPTH // 3
NORM_EPS = 1e-6
CONV_W = 4

MLA_HEADS = 16
MLA_NOPE = 64
MLA_ROPE = 32
MLA_V = 64
MLA_Q_RANK = 384
MLA_KV_RANK = 256
MLA_GATE = MLA_HEADS * MLA_V
MLA_IN = MLA_Q_RANK + MLA_KV_RANK + MLA_ROPE + MLA_GATE
MLA_SCALE = (MLA_NOPE + MLA_ROPE) ** -0.5
ROPE_BASE = 10000.0
Q_BLOCK = 128

SSD_INNER = 2 * D_MODEL
SSD_HEADDIM = 64
SSD_HEADS = SSD_INNER // SSD_HEADDIM
SSD_STATE = 128
SSD_GROUPS = 8
SSD_CONV_DIM = SSD_INNER + 2 * SSD_GROUPS * SSD_STATE
SSD_IN = SSD_INNER + SSD_CONV_DIM + 2 * SSD_HEADS
SSD_CHUNK = 128

ML_INNER = 2 * D_MODEL
ML_HEADS = 4
ML_DH = ML_INNER // ML_HEADS
ML_IN = 3 * ML_INNER + 4 * ML_HEADS
ML_CHUNK = 64

kernel_name = 'hybrid_mla_ssd_mlstm_flow_step'

F32 = jnp.float32

def rmsnorm(x, g):
    xf = x.astype(F32)
    y = xf * lax.rsqrt(jnp.mean(xf * xf, axis=-1, keepdims=True) + NORM_EPS)
    return (y * g.astype(F32)).astype(x.dtype)

def headwise_layernorm(h, g):
    hf = h.astype(F32)
    mu = jnp.mean(hf, axis=-1, keepdims=True)
    var = jnp.mean(jnp.square(hf - mu), axis=-1, keepdims=True)
    return ((hf - mu) * lax.rsqrt(var + NORM_EPS) * g.astype(F32)).astype(h.dtype)

def adaln(cond, w, b):
    m = (jax.nn.silu(cond) @ w + b)[:, None, :]
    return jnp.split(m, 3, axis=-1)

def modulate(x, g, shift, scale):
    return rmsnorm(x, g) * (1 + scale) + shift

def centred_dwconv(x, w, b):
    ch = x.shape[-1]
    y = lax.conv_general_dilated(x, w[:, None, :].astype(x.dtype), window_strides=(1,),
                                 padding=[((CONV_W - 1) // 2, CONV_W // 2)],
                                 dimension_numbers=('NWC', 'WIO', 'NWC'), feature_group_count=ch)
    return y + b

def to_chunks(t, size):
    return t.reshape(t.shape[0], t.shape[1] // size, size, *t.shape[2:]).swapaxes(0, 1)

def from_chunks(t):
    t = t.swapaxes(0, 1)
    return t.reshape(t.shape[0], t.shape[1] * t.shape[2], *t.shape[3:])

def flip(t):
    return jnp.flip(t, axis=1)

def axial_rope(n_tokens):
    rows = n_tokens // GRID_W
    row = jnp.repeat(jnp.arange(rows), GRID_W).astype(F32)
    col = jnp.tile(jnp.arange(GRID_W), rows).astype(F32)
    half = MLA_ROPE // 2
    inv = 1.0 / (ROPE_BASE ** (jnp.arange(0, half, 2, dtype=F32) / half))
    ang = jnp.concatenate([row[:, None] * inv, col[:, None] * inv], axis=-1)
    return jnp.cos(ang), jnp.sin(ang)

def apply_rope(x, cos, sin):
    cos = cos.astype(x.dtype)
    sin = sin.astype(x.dtype)
    x1, x2 = x[..., :MLA_ROPE // 2], x[..., MLA_ROPE // 2:]
    return jnp.concatenate([x1 * cos - x2 * sin, x2 * cos + x1 * sin], axis=-1)

def mla_expand(ckv, w_uk, w_uv):
    return (jnp.einsum('blc,chd->blhd', ckv, w_uk), jnp.einsum('blc,chd->blhd', ckv, w_uv))

def mla_attention(q_nope, q_pe, k_nope, k_pe, v):
    b, s, h, _ = q_nope.shape
    nb = s // Q_BLOCK

    def blocks(t):
        return t.reshape(b, nb, Q_BLOCK, *t.shape[2:]).swapaxes(0, 1)

    def one_block(qs):
        qn, qp = qs
        sc = jnp.einsum('bqhd,bkhd->bhqk', qn, k_nope) + jnp.einsum('bqhr,bkr->bhqk', qp, k_pe)
        p = jax.nn.softmax(sc.astype(F32) * MLA_SCALE, axis=-1).astype(v.dtype)
        return jnp.einsum('bhqk,bkhd->bqhd', p, v)

    o = lax.map(one_block, (blocks(q_nope), blocks(q_pe)))
    return o.swapaxes(0, 1).reshape(b, s, h * v.shape[-1])

def mla_mixer(h, w_in, q_norm_g, kv_norm_g, w_uq, w_uk, w_uv, w_out, rope, ctx_ckv, ctx_kpe):
    cq, ckv, kpe, z = jnp.split(h @ w_in, [MLA_Q_RANK, MLA_Q_RANK + MLA_KV_RANK,
                                           MLA_Q_RANK + MLA_KV_RANK + MLA_ROPE], axis=-1)
    q = jnp.einsum('blr,rhd->blhd', rmsnorm(cq, q_norm_g), w_uq)
    q_nope, q_pe = q[..., :MLA_NOPE], q[..., MLA_NOPE:]
    ckv = rmsnorm(ckv, kv_norm_g)
    if rope is not None:
        cos, sin = rope
        q_pe = apply_rope(q_pe, cos[:, None, :], sin[:, None, :])
        kpe_keys = apply_rope(kpe, cos, sin)
    else:
        kpe_keys = kpe
    k_nope, v = mla_expand(ckv, w_uk, w_uv)
    if ctx_ckv is not None:
        kc, vc = mla_expand(ctx_ckv, w_uk, w_uv)
        k_nope = jnp.concatenate([k_nope, kc], axis=1)
        v = jnp.concatenate([v, vc], axis=1)
        kpe_keys = jnp.concatenate([kpe_keys, ctx_kpe], axis=1)
    o = mla_attention(q_nope, q_pe, k_nope, kpe_keys, v)
    return (o * jax.nn.silu(z)) @ w_out, ckv, kpe

def ssd_scan(x, dt, a, bm, cm, h0):
    b, _, nh, p = x.shape
    g = bm.shape[2]
    r = nh // g
    q = SSD_CHUNK
    tri = jnp.tril(jnp.ones((q, q), bool))[None, :, :, None]

    def step(hs, inp):
        xc, dtc, bc, cc = inp
        acs = jnp.cumsum(dtc * a, axis=1)
        seg = acs[:, :, None, :] - acs[:, None, :, :]
        lmat = jnp.exp(jnp.where(tri, seg, -jnp.inf))
        cb = jnp.einsum('bign,bjgn->bijg', cc, bc).astype(F32)
        mm = (cb[..., None] * lmat.reshape(b, q, q, g, r) * dtc.reshape(b, 1, q, g, r)).astype(xc.dtype)
        xg = xc.reshape(b, q, g, r, p)
        y = jnp.einsum('bijgr,bjgrp->bigrp', mm, xg)
        hg = hs.reshape(b, g, r, p, -1)
        y = y + jnp.einsum('bign,bgrpn->bigrp', cc, hg) * jnp.exp(acs).reshape(b, q, g, r, 1).astype(xc.dtype)
        w_end = (jnp.exp(acs[:, -1:, :] - acs) * dtc).reshape(b, q, g, r).astype(xc.dtype)
        h_new = (hs * jnp.exp(acs[:, -1])[:, :, None, None].astype(hs.dtype)
                 + jnp.einsum('bjgn,bjgr,bjgrp->bgrpn', bc, w_end, xg).reshape(hs.shape))
        return h_new.astype(hs.dtype), y.reshape(b, q, nh, p)

    h_t, ys = lax.scan(step, h0, (to_chunks(x, q), to_chunks(dt, q), to_chunks(bm, q), to_chunks(cm, q)))
    return from_chunks(ys), h_t

def ssd_mixer(h, w_in, conv_w, conv_b, dt_bias, a_log, d_skip, norm_g, w_out, h0):
    b, n, _ = h.shape
    z, xbc, dt = jnp.split(h @ w_in, [SSD_INNER, SSD_INNER + SSD_CONV_DIM], axis=-1)
    xbc = jax.nn.silu(centred_dwconv(xbc, conv_w, conv_b))
    xs, bm, cm = jnp.split(xbc, [SSD_INNER, SSD_INNER + SSD_GROUPS * SSD_STATE], axis=-1)
    xs = xs.reshape(b, n, SSD_HEADS, SSD_HEADDIM)
    bm = bm.reshape(b, n, SSD_GROUPS, SSD_STATE)
    cm = cm.reshape(b, n, SSD_GROUPS, SSD_STATE)
    dt = jax.nn.softplus(dt.reshape(b, n, 2, SSD_HEADS).astype(F32) + dt_bias.astype(F32))
    a = -jnp.exp(a_log.astype(F32))
    y_f, h_f = ssd_scan(xs, dt[:, :, 0], a[0], bm, cm, h0[:, 0])
    y_b, h_b = ssd_scan(flip(xs), flip(dt[:, :, 1]), a[1], flip(bm), flip(cm), h0[:, 1])
    y = y_f + flip(y_b) + d_skip[:, None] * xs
    y = rmsnorm(y.reshape(b, n, SSD_INNER) * jax.nn.silu(z), norm_g)
    return y @ w_out, jnp.stack([h_f, h_b], axis=1)

def mlstm_scan(q, k, v, ig, lf, c0, n0, m0):
    ln = ML_CHUNK
    tri = jnp.tril(jnp.ones((ln, ln), bool))

    def step(carry, inp):
        cs, ns, ms = carry
        qc, kc, vc, ic, fc = inp
        ic = ic.swapaxes(1, 2)
        bcum = jnp.cumsum(fc.swapaxes(1, 2), axis=-1)
        mp = ms.astype(F32)
        dmat = jnp.where(tri, bcum[..., :, None] - bcum[..., None, :] + ic[..., None, :], -jnp.inf)
        m_inter = bcum + mp[..., None]
        m_i = jnp.maximum(jnp.max(dmat, axis=-1), m_inter)
        wmat = jnp.exp(dmat - m_i[..., None]).astype(qc.dtype)
        g_inter = jnp.exp(m_inter - m_i)
        s = jnp.einsum('bihk,bjhk->bhij', qc, kc) * wmat
        num = (jnp.einsum('bhij,bjhv->bihv', s, vc).astype(F32)
               + g_inter.swapaxes(1, 2)[..., None] * jnp.einsum('bihk,bhkv->bihv', qc, cs).astype(F32))
        den = jnp.sum(s, axis=-1).astype(F32) + g_inter * jnp.einsum('bihk,bhk->bhi', qc, ns).astype(F32)
        denom = jnp.maximum(jnp.abs(den), jnp.exp(-m_i))
        hc = (num / denom.swapaxes(1, 2)[..., None]).astype(qc.dtype)
        m_new = m_i[..., -1]
        w_end = jnp.exp(bcum[..., -1:] - bcum + ic - m_new[..., None]).astype(kc.dtype)
        decay = jnp.exp(bcum[..., -1] + mp - m_new)
        c_new = decay[..., None, None] * cs.astype(F32) + jnp.einsum('bhj,bjhk,bjhv->bhkv', w_end, kc, vc).astype(F32)
        n_new = decay[..., None] * ns.astype(F32) + jnp.einsum('bhj,bjhk->bhk', w_end, kc).astype(F32)
        return (c_new.astype(cs.dtype), n_new.astype(ns.dtype), m_new.astype(ms.dtype)), hc

    (c_t, n_t, m_t), hs = lax.scan(step, (c0, n0, m0),
                                   (to_chunks(q, ln), to_chunks(k, ln), to_chunks(v, ln),
                                    to_chunks(ig, ln), to_chunks(lf, ln)))
    return from_chunks(hs), c_t, n_t, m_t

def mlstm_mixer(h, w_in, gate_b, conv_w, conv_b, w_q, w_k, w_v, norm_g, skip, w_out, c0, n0, m0):
    b, n, _ = h.shape
    xm, o_pre, z, gates = jnp.split(h @ w_in, [ML_INNER, 2 * ML_INNER, 3 * ML_INNER], axis=-1)
    xc = jax.nn.silu(centred_dwconv(xm, conv_w, conv_b))
    q = jnp.einsum('blhd,hde->blhe', xc.reshape(b, n, ML_HEADS, ML_DH), w_q)
    k = jnp.einsum('blhd,hde->blhe', xc.reshape(b, n, ML_HEADS, ML_DH), w_k) * (ML_DH ** -0.5)
    v = jnp.einsum('blhd,hde->blhe', xm.reshape(b, n, ML_HEADS, ML_DH), w_v)
    gates = gates.reshape(b, n, 2, 2, ML_HEADS).astype(F32) + gate_b.astype(F32)
    ig = gates[:, :, :, 0]
    lf = jax.nn.log_sigmoid(gates[:, :, :, 1])
    h_f, c_f, n_f, m_f = mlstm_scan(q, k, v, ig[:, :, 0], lf[:, :, 0], c0[:, 0], n0[:, 0], m0[:, 0])
    h_b, c_b, n_b, m_b = mlstm_scan(flip(q), flip(k), flip(v), flip(ig[:, :, 1]), flip(lf[:, :, 1]),
                                    c0[:, 1], n0[:, 1], m0[:, 1])
    hh = (h_f + flip(h_b)) * jax.nn.sigmoid(o_pre).reshape(b, n, ML_HEADS, ML_DH)
    hh = headwise_layernorm(hh, norm_g).reshape(b, n, ML_INNER)
    out = ((hh + skip * xc) * jax.nn.silu(z)) @ w_out
    return (out, jnp.stack([c_f, c_b], axis=1), jnp.stack([n_f, n_b], axis=1), jnp.stack([m_f, m_b], axis=1))

def setup_inputs(seed: int = 0) -> dict:
    key = jax.random.key(seed)
    ks = iter(jax.random.split(key, 64))

    def nrm(shape, scale=1.0):
        return jax.random.normal(next(ks), shape, F32) * scale

    def gain(shape):
        return 1.0 + nrm(shape, 0.02)

    D = D_MODEL
    inp = {}
    inp['x_prompt'] = nrm((BATCH, SEQ, D))
    inp['x_sample'] = nrm((DEC_BATCH, DEC_SEQ, D))
    inp['cache_mla_ckv'] = nrm((DEC_BATCH, N_MLA_LAYERS, PAST_LEN, MLA_KV_RANK))
    inp['cache_mla_kpe'] = nrm((DEC_BATCH, N_MLA_LAYERS, PAST_LEN, MLA_ROPE))
    inp['state_ssd'] = nrm((DEC_BATCH, N_SSD_LAYERS, 2, SSD_HEADS, SSD_HEADDIM, SSD_STATE), 0.1)
    inp['state_mlstm_c'] = nrm((DEC_BATCH, N_MLSTM_LAYERS, 2, ML_HEADS, ML_DH, ML_DH), 0.05)
    inp['state_mlstm_n'] = nrm((DEC_BATCH, N_MLSTM_LAYERS, 2, ML_HEADS, ML_DH), 0.05)
    inp['state_mlstm_m'] = jax.random.uniform(next(ks), (DEC_BATCH, N_MLSTM_LAYERS, 2, ML_HEADS), F32, 0.0, 4.0)
    inp['c'] = nrm((DEC_BATCH, D))
    inp['c_ctx'] = nrm((D,))
    inp['ada_w'] = nrm((DEPTH, D, 3 * D), 0.5 * D ** -0.5)
    inp['ada_b'] = nrm((DEPTH, 3 * D), 0.02)
    inp['norm_g'] = gain((DEPTH, D))
    inp['final_norm_g'] = gain((D,))
    nm = N_MLA_LAYERS
    inp['mla_w_in'] = nrm((nm, D, MLA_IN), D ** -0.5)
    inp['mla_q_norm_g'] = gain((nm, MLA_Q_RANK))
    inp['mla_kv_norm_g'] = gain((nm, MLA_KV_RANK))
    inp['mla_w_uq'] = nrm((nm, MLA_Q_RANK, MLA_HEADS, MLA_NOPE + MLA_ROPE), MLA_Q_RANK ** -0.5)
    inp['mla_w_uk'] = nrm((nm, MLA_KV_RANK, MLA_HEADS, MLA_NOPE), MLA_KV_RANK ** -0.5)
    inp['mla_w_uv'] = nrm((nm, MLA_KV_RANK, MLA_HEADS, MLA_V), MLA_KV_RANK ** -0.5)
    inp['mla_w_out'] = nrm((nm, MLA_GATE, D), MLA_GATE ** -0.5)
    ns_ = N_SSD_LAYERS
    inp['ssd_w_in'] = nrm((ns_, D, SSD_IN), D ** -0.5)
    inp['ssd_conv_w'] = nrm((ns_, CONV_W, SSD_CONV_DIM), CONV_W ** -0.5)
    inp['ssd_conv_b'] = nrm((ns_, SSD_CONV_DIM), 0.02)
    u = jax.random.uniform(next(ks), (ns_, 2, SSD_HEADS), F32)
    dt0 = jnp.exp(u * (math.log(0.1) - math.log(0.001)) + math.log(0.001))
    inp['ssd_dt_bias'] = dt0 + jnp.log(-jnp.expm1(-dt0))
    inp['ssd_a_log'] = jnp.log(jax.random.uniform(next(ks), (ns_, 2, SSD_HEADS), F32, 1.0, 16.0))
    inp['ssd_d'] = 1.0 + nrm((ns_, SSD_HEADS), 0.1)
    inp['ssd_norm_g'] = gain((ns_, SSD_INNER))
    inp['ssd_w_out'] = nrm((ns_, SSD_INNER, D), SSD_INNER ** -0.5)
    nl = N_MLSTM_LAYERS
    inp['ml_w_in'] = nrm((nl, D, ML_IN), D ** -0.5)
    ib = nrm((nl, 2, 1, ML_HEADS), 0.1)
    fb = jnp.linspace(3.0, 6.0, ML_HEADS, dtype=F32) + nrm((nl, 2, 1, ML_HEADS), 0.1)
    inp['ml_gate_b'] = jnp.concatenate([ib, fb], axis=2)
    inp['ml_conv_w'] = nrm((nl, CONV_W, ML_INNER), CONV_W ** -0.5)
    inp['ml_conv_b'] = nrm((nl, ML_INNER), 0.02)
    inp['ml_w_q'] = nrm((nl, ML_HEADS, ML_DH, ML_DH), ML_DH ** -0.5)
    inp['ml_w_k'] = nrm((nl, ML_HEADS, ML_DH, ML_DH), ML_DH ** -0.5)
    inp['ml_w_v'] = nrm((nl, ML_HEADS, ML_DH, ML_DH), ML_DH ** -0.5)
    inp['ml_norm_g'] = gain((nl, ML_HEADS, ML_DH))
    inp['ml_skip'] = 1.0 + nrm((nl, ML_INNER), 0.1)
    inp['ml_w_out'] = nrm((nl, ML_INNER, D), ML_INNER ** -0.5)
    return inp

def reference(x_prompt, x_sample, cache_mla_ckv, cache_mla_kpe, state_ssd, state_mlstm_c, state_mlstm_n,
              state_mlstm_m, c, c_ctx, ada_w, ada_b, norm_g, final_norm_g,
              mla_w_in, mla_q_norm_g, mla_kv_norm_g, mla_w_uq, mla_w_uk, mla_w_uv, mla_w_out,
              ssd_w_in, ssd_conv_w, ssd_conv_b, ssd_dt_bias, ssd_a_log, ssd_d, ssd_norm_g, ssd_w_out,
              ml_w_in, ml_gate_b, ml_conv_w, ml_conv_b, ml_w_q, ml_w_k, ml_w_v, ml_norm_g, ml_skip, ml_w_out):
    bp = x_prompt.shape[0]
    rope = axial_rope(x_sample.shape[1])
    xp, xs = x_prompt, x_sample
    new_ckv, new_kpe, new_ssd, new_c, new_n, new_m = [], [], [], [], [], []
    for i in range(DEPTH):
        kind, j = i % N_MIXERS, i // N_MIXERS
        sh_p, sc_p, g_p = adaln(c_ctx[None, :], ada_w[i], ada_b[i])
        sh_s, sc_s, g_s = adaln(c, ada_w[i], ada_b[i])
        hp = modulate(xp, norm_g[i], sh_p, sc_p)
        hs = modulate(xs, norm_g[i], sh_s, sc_s)
        if kind == 0:
            wts = (mla_w_in[j], mla_q_norm_g[j], mla_kv_norm_g[j], mla_w_uq[j], mla_w_uk[j], mla_w_uv[j], mla_w_out[j])
            out_p, ckv, kpe = mla_mixer(hp, *wts, None, None, None)
            out_s, _, _ = mla_mixer(hs, *wts, rope, cache_mla_ckv[:, j], cache_mla_kpe[:, j])
            new_ckv.append(ckv)
            new_kpe.append(kpe)
        elif kind == 1:
            wts = (ssd_w_in[j], ssd_conv_w[j], ssd_conv_b[j], ssd_dt_bias[j], ssd_a_log[j], ssd_d[j],
                   ssd_norm_g[j], ssd_w_out[j])
            h0 = jnp.zeros((bp, 2, SSD_HEADS, SSD_HEADDIM, SSD_STATE), xp.dtype)
            out_p, st = ssd_mixer(hp, *wts, h0)
            out_s, _ = ssd_mixer(hs, *wts, state_ssd[:, j])
            new_ssd.append(st)
        else:
            wts = (ml_w_in[j], ml_gate_b[j], ml_conv_w[j], ml_conv_b[j], ml_w_q[j], ml_w_k[j], ml_w_v[j],
                   ml_norm_g[j], ml_skip[j], ml_w_out[j])
            c0 = jnp.zeros((bp, 2, ML_HEADS, ML_DH, ML_DH), xp.dtype)
            n0 = jnp.zeros((bp, 2, ML_HEADS, ML_DH), xp.dtype)
            m0 = jnp.zeros((bp, 2, ML_HEADS), xp.dtype)
            out_p, cc, nn_, mm = mlstm_mixer(hp, *wts, c0, n0, m0)
            out_s, _, _, _ = mlstm_mixer(hs, *wts, state_mlstm_c[:, j], state_mlstm_n[:, j], state_mlstm_m[:, j])
            new_c.append(cc)
            new_n.append(nn_)
            new_m.append(mm)
        xp = xp + g_p * out_p
        xs = xs + g_s * out_s
    y_prompt = rmsnorm(xp, final_norm_g)
    y_sample = rmsnorm(xs, final_norm_g)
    return (y_prompt, y_sample, jnp.stack(new_ckv, axis=1), jnp.stack(new_kpe, axis=1), jnp.stack(new_ssd, axis=1),
            jnp.stack(new_c, axis=1), jnp.stack(new_n, axis=1), jnp.stack(new_m, axis=1))


_drawn_inputs = setup_inputs


def setup_inputs(seed=0):
    import zlib

    import numpy as np

    out = dict(_drawn_inputs(seed))
    spreads = {}
    factors = {'cache_mla_ckv': 6.316,
     'cache_mla_kpe': 8.0,
     'state_mlstm_n': 3.829,
     'final_norm_g': 2.731,
     'mla_q_norm_g': 8.0,
     'mla_kv_norm_g': 2.803,
     'ssd_d': 2.691,
     'ssd_norm_g': 5.291,
     'ml_norm_g': 8.0,
     'ml_skip': 4.702}
    for name, (base, spread) in spreads.items():
        noise = np.random.default_rng([zlib.crc32(name.encode()), seed]).standard_normal(out[name].shape)
        drawn = base * np.exp(spread * noise) if base else spread * noise
        out[name] = __import__('jax').numpy.asarray(drawn.astype(out[name].dtype))
    for name, factor in factors.items():
        out[name] = (out[name] * factor).astype(out[name].dtype)
    return out
```

```python
from contextlib import ExitStack, nullcontext

import numpy as np

import concourse.bass as bass
from concourse import mybir

F32 = mybir.dt.float32
ACT = mybir.ActivationFunctionType
ALU = mybir.AluOpType
X = mybir.AxisListType.X

P = 128
D_MODEL, DEPTH = 1024, 4
LAT, CTX, PAST = 512, 128, 128
TOK = LAT + CTX
NT = TOK // P
KD = D_MODEL // P
EPS = 1e-6
BIG = 1e30
SLAB = 4096
HEADS, NOPE, ROPE, VDIM = 16, 64, 32, 64
QK = NOPE + ROPE
Q_RANK, KV_RANK = 384, 256
MLA_SCALE = QK ** -0.5
PAIRS = HEADS // 2
KEYS = LAT + PAST + CTX
INNER = 2 * D_MODEL
KI = INNER // P
GROUPS, GH, HD, STATE = 8, 4, 64, 128
SH = GROUPS * GH
GX = GH * HD
CW = 4
ML_HEADS, DH = 4, 512
KH = DH // P
RAW = 648
RAW_LAT, RAW_CTX = 1, LAT + 4
CONV = LAT + 3 + CTX
C_CTX = LAT + 3

COL = {}


def _columns():
    at = 0
    for block in ((("ada_b", 96), ("norm_g", 32)),
                  (("c", 8), ("c_ctx", 8), ("final_norm_g", 8), ("mla_q_norm_g", 6), ("mla_kv_norm_g", 4),
                   ("ssd_conv_b", 32), ("ssd_norm_g", 16), ("ml_conv_b", 16), ("ml_norm_g", 16)),
                  (("ssd_conv_w", 128),),
                  (("ml_conv_w", 64), ("ml_skip", 16), ("state_mlstm_n", 32))):
        row = 0
        for name, n in block:
            COL[name] = (at, row, n)
            row += n
        at += P
    return at // P


PARAM_BLOCKS = _columns()


def col(name, k=0):
    block, row, _ = COL[name]
    return block + row + k


class Slabs:

    def __init__(self):
        self.n, self.got, self.i, self.dn, self.dg = 0, [0, 0], 0, 0, [0, 0]

    def enter(self, i, dmas):
        assert len(dmas) % 2 == 0
        self.i, self.dn = i, len(dmas)
        self.dg = [0, 0]
        for k, d in enumerate(dmas):
            self.dg[(self.n + k) % 2] += 16 * d

    def leave(self, trips):
        self.n += self.dn * (trips - 1)
        self.got = [g + d * (trips - 1) for g, d in zip(self.got, self.dg)]
        self.i, self.dn, self.dg = 0, 0, [0, 0]

    def take(self, dmas=1):
        slot = self.n % 2
        free = self.n + 1 + self.dn * self.i
        self.n += 1
        self.got[slot] += 16 * dmas
        return slot, free, self.got[slot] + self.dg[slot] * self.i


class Tally:

    def __init__(self, eng, sem):
        self.eng, self.sem, self.n, self.i, self.per = eng, sem, 0, 0, 0

    def enter(self, i, per):
        self.i, self.per, self.n0 = i, per, self.n

    def leave(self, trips):
        assert self.n - self.n0 == self.per, (self.n - self.n0, self.per)
        self.n += self.per * (trips - 1)
        self.i, self.per = 0, 0

    def mark(self, ins):
        ins.then_inc(self.sem, 1)
        self.n += 1
        return self.n + self.per * self.i

    def after(self, ins):
        self.eng.wait_ge(self.sem, self.mark(ins))


def rope_table():
    grid_w, half = 64, ROPE // 2
    pos = np.arange(LAT)
    inv = (1.0 / (np.float32(10000.0) ** (np.arange(0, half, 2, dtype=np.float32) / np.float32(half)))).astype(np.float32)
    ang = np.concatenate([(pos // grid_w).astype(np.float32)[:, None] * inv,
                          (pos % grid_w).astype(np.float32)[:, None] * inv], axis=-1)
    table = np.zeros((2 * ROPE, TOK), np.float32)
    table[0:ROPE] = 1.0
    cos, sin = np.cos(ang).T, np.sin(ang).T
    table[0:ROPE, 0:LAT] = np.concatenate([cos, cos])
    table[ROPE:, 0:LAT] = np.concatenate([-sin, sin])
    return table


def hybrid_flow_step(nc, t, out, layers=DEPTH):
    with ExitStack() as ctx:
        def sb(name, shape):
            return ctx.enter_context(nc.sbuf_tensor(name, shape, F32))

        def sem(name):
            return ctx.enter_context(nc.semaphore(name))

        xT = sb("xT", [P, KD, TOK])
        hT = sb("hT", [P, KD, TOK])
        ring = sb("ring", [P, 2, SLAB])
        yT = sb("yT", [P, KI, TOK])
        ident, ones = sb("ident", [P, P]), sb("ones", [P, P])
        tri = sb("tri", [P, 2, P])
        neg = sb("neg", [P, 2, P])
        cols = sb("cols", [P, PARAM_BLOCKS * P])
        cond = sb("cond", [P, KD, 2])
        mod = sb("mod", [P, 24, 2])
        gain = sb("gain", [P, KD, 2])
        small = sb("small", [P, 64])
        ROOM = 53215 - (2 * KD * TOK + 2 * SLAB + KI * TOK + 6 * P + PARAM_BLOCKS * P + 16 + 48 + 16 + 64) - 64
        room = sb("room", [P, ROOM])

        class Room:

            def __init__(self):
                self.at = 0

            def __call__(self, *shape):
                n = 1
                for s in shape:
                    n *= s
                a = room[:, self.at:self.at + n]
                self.at += n
                assert self.at <= ROOM, (self.at, ROOM)
                if len(shape) == 2:
                    a = a.rearrange("p (a b) -> p a b", b=shape[1])
                if len(shape) == 4:
                    a = a.rearrange("p (a b c d) -> p a b c d", b=shape[1], c=shape[2], d=shape[3])
                if len(shape) == 3:
                    a = a.rearrange("p (a b c) -> p a b c", b=shape[1], c=shape[2])
                return a

        ps = ctx.enter_context(nc.psum_tensor("ps", [P, 8, 512], F32))

        def big(n):
            n %= 3
            return ps[:, 2 * n:2 * n + 2, :].rearrange("p a b -> p (a b)")

        def bank(n):
            return ps[:, n, :]

        def slab_through(pe, product, own, done):
            product.then_inc(w_used, 1)
            pe.matmul(own, cond[:, 0, :], cond[:, 0, :], start=True, stop=True).then_inc(done, 1)

        def last_cols(n):
            return big(n)[0:2, 1020:1022]

        acs_rows = nc.dram_tensor("acs_rows", (2 * SH, TOK), F32).ap()
        max_rows = nc.dram_tensor("max_rows", (ML_HEADS, 2 * TOK), F32).ap()

        w_loaded = [sem("w_loaded0"), sem("w_loaded1")]
        w_used = sem("w_used")
        stage_done = sem("stage_done")
        pe_steps, act_steps, dve_steps, pool_steps = (sem("pe_steps"), sem("act_steps"), sem("dve_steps"),
                                                      sem("pool_steps"))
        masks_made = sem("masks_made")
        x_loaded, rows_loaded, zeros_made = sem("x_loaded"), sem("rows_loaded"), sem("zeros_made")
        stored = sem("stored")
        in_turned, in_copied, in_copied_v = sem("in_turned"), sem("in_copied"), sem("in_copied_v")
        cond_ready = sem("cond_ready")
        ada_done, ada_read = sem("ada_done"), sem("ada_read")
        gain_ready = sem("gain_ready")
        squared, summed, sums_read, rooted = sem("squared"), sem("summed"), sem("sums_read"), sem("rooted")
        scaled, h_ready = sem("scaled"), sem("h_ready")
        out_done, out_read = sem("out_done"), sem("out_read")

        S = {}

        def sems(*names):
            for n in names:
                S[n] = sem(n)

        MASKS = 9
        passed = sem("passed")

        def apart(eng):
            eng.sem_inc(passed, 1)

        engines = 4
        fences = {}

        def fence(eng, name):
            fences[name] = fences.get(name, 0) + 1
            eng.drain().then_inc(stage_done, 1)
            eng.wait_ge(stage_done, engines * fences[name])

        def seg(s):
            return slice(0, LAT) if s == 0 else slice(LAT, TOK)

        def bcast(a, n):
            return a.unsqueeze(2).broadcast_to([a.shape[0], a.shape[1], n])

        def trips(eng, n):
            return eng.Fori(0, n) if n > 1 else nullcontext(0)

        x_in = yT[:, 0:KD, :].rearrange("p a b -> p (a b)").rearrange("p (t d) -> p t d", d=D_MODEL)
        rows_in = room[:, 0:PARAM_BLOCKS * P].rearrange("p (b c) -> p b c", c=P)
        param_dmas = len(COL)
        block_rows = [0] * PARAM_BLOCKS
        for at, row, n in COL.values():
            block_rows[at // P] = max(block_rows[at // P], row + n)

        def setup_sync(sp):
            sp.dma_start(x_in[:, 0:LAT // P, :], t["x_sample"][0].rearrange("(t p) d -> p t d", p=P)
                         ).then_inc(x_loaded, 16)
            sp.dma_start(x_in[:, LAT // P, :], t["x_prompt"][0]).then_inc(x_loaded, 16)

        def setup_act_loads(act):
            for name, (at, row, n) in COL.items():
                src = t[name]
                dims = "abcdef"[:len(src.shape)]
                flat = src.rearrange(f"{' '.join(dims)} -> ({' '.join(dims)})") if len(dims) > 1 else src
                act.dma_start(rows_in[row:row + n, at // P, :], flat.rearrange("(r c) -> r c", c=P)
                              ).then_inc(rows_loaded, 16)

        def setup_pool(pool):
            n = 0
            for a, v in ((ident[:], 0.0), (ones[:], 1.0), (tri[:], 1.0), (neg[:], 0.0)):
                pool.memset(a, v).then_inc(masks_made, 1)
                n += 1
            pool.wait_ge(masks_made, n)
            pool.affine_select(out=ident[:], in_=ident[:], compare_op=ALU.not_equal, fill=1.0, base=0,
                               pattern=[[-1, P]], channel_multiplier=1).then_inc(masks_made, 1)
            for d in range(2):
                s = 1 - 2 * d
                for m, fill in ((tri, 0.0), (neg, -BIG)):
                    pool.affine_select(out=m[:, d], in_=m[:, d], compare_op=ALU.is_ge, fill=fill, base=0,
                                       pattern=[[s, P]], channel_multiplier=-s).then_inc(masks_made, 1)

        def setup_pe(pe):
            pe.wait_ge(masks_made, MASKS)
            pe.wait_ge(rows_loaded, 16 * param_dmas)
            for b in range(PARAM_BLOCKS):
                n = block_rows[b]
                mm = pe.transpose(bank(6)[:, b * P:b * P + n], rows_in[0:n, b, :], ident[0:n, 0:n])
            mm.then_inc(in_turned, 1)
            pe.wait_ge(x_loaded, 32)
            for k in range(KD):
                if k >= 3:
                    pe.wait_ge(in_copied if k % 2 else in_copied_v, (k - 3) // 2 + 1)
                for tt in range(NT):
                    mm = pe.transpose(big(k)[:, tt * P:(tt + 1) * P], x_in[:, tt, k * P:(k + 1) * P], ident[:])
                mm.then_inc(in_turned, 1)

        def setup_act(act):
            act.wait_ge(in_turned, 1)
            for b in range(PARAM_BLOCKS):
                n = block_rows[b]
                ins = act.activation(cols[:, b * P:b * P + n], bank(6)[:, b * P:b * P + n], ACT.Copy)
                act_t.mark(ins)
            act.wait_ge(act_steps, act_t.n)
            act.activation(cond[:, :, 0], cols[:, col("c"):col("c") + KD], ACT.Silu).then_inc(cond_ready, 1)
            act.activation(cond[:, :, 1], cols[:, col("c_ctx"):col("c_ctx") + KD], ACT.Silu).then_inc(cond_ready, 1)
            for k in range(0, KD, 2):
                act.wait_ge(in_turned, k + 2)
                act.activation(xT[:, k], big(k)[:, 0:TOK], ACT.Copy).then_inc(in_copied, 1)

        def setup_dve(dve):
            for k in range(1, KD, 2):
                dve.wait_ge(in_turned, k + 2)
                dve.tensor_copy(xT[:, k], big(k)[:, 0:TOK]).then_inc(in_copied_v, 1)

        def ada_sync(sp, l):
            w = t["ada_w"][l].rearrange("(k p) n -> p k n", p=P)
            with trips(sp, 3) as i:
                slabs.enter(i, [1, 1])
                for u in range(2):
                    slot, free, _ = slabs.take()
                    sp.wait_ge(w_used, free)
                    sp.dma_start(ring[:, slot].rearrange("p (k n) -> p k n", n=512),
                                 w[:, :, bass.ds((2 * i + u) * 512, 512)]).then_inc(w_loaded[slot], 16)
            slabs.leave(3)

        def ada_pe(pe, l):
            pe.wait_ge(cond_ready, 2)
            with trips(pe, 3) as i:
                slabs.enter(i, [1, 1])
                for u in range(2):
                    slot, _, full = slabs.take()
                    w = ring[:, slot].rearrange("p (k n) -> p k n", n=512)
                    pe.wait_ge(w_loaded[slot], full)
                    pe.wait_ge(ada_read, 6 * l + 2 * i + u + 1)
                    for m in range(4):
                        for k in range(KD):
                            mm = pe.matmul(bank(6 + u)[:, 2 * m:2 * m + 2], w[:, k, m * P:(m + 1) * P], cond[:, k, :],
                                           start=(k == 0), stop=(k == KD - 1))
                    slab_through(pe, mm, bank(6 + u)[0:2, 8:10], ada_done)
            slabs.leave(3)

        def ada_dve(dve, l):
            with trips(dve, 3) as i:
                for u in range(2):
                    s = 2 * i + u
                    dve.wait_ge(ada_done, 6 * l + s + 1)
                    b = cols[:, bass.ds(col("ada_b", 24 * l) + 4 * s, 4)]
                    dve.tensor_tensor(mod[:, bass.ds(4 * s, 4), :],
                                      bank(6 + u)[:, 0:8].rearrange("p (m c) -> p m c", c=2),
                                      bcast(b, 2), ALU.add).then_inc(ada_read, 1)
            dve.wait_ge(ada_read, 6 * l + 8)
            dve.scalar_tensor_tensor(out=gain[:], in0=mod[:, KD:2 * KD, :], scalar=1.0,
                                     in1=bcast(cols[:, col("norm_g", KD * l):col("norm_g", KD * l) + KD], 2),
                                     op0=ALU.add, op1=ALU.mult).then_inc(gain_ready, 1)

        n_sq, n_rstd, n_tmp = yT[:, KD:KD + 2], yT[:, KD + 2], yT[:, KD + 3]

        def norm_act(act, l):
            for k in range(KD):
                n = KD * l + k
                if n >= 2:
                    act.wait_ge(summed, n - 1)
                act.activation(n_sq[:, k % 2], xT[:, k], ACT.Square).then_inc(squared, 1)
            act.wait_ge(sums_read, 2 * l + 1)
            act.activation(n_tmp, n_tmp, ACT.Sqrt).then_inc(rooted, 1)
            if l < layers:
                for k in range(KD):
                    act.wait_ge(scaled, KD * l + k + 1)
                    for s in range(2):
                        ins = act.activation(hT[:, k, seg(s)], hT[:, k, seg(s)], ACT.Identity, bias=mod[:, k, s:s + 1])
                    ins.then_inc(h_ready, 1)

        def norm_pe(pe, l):
            for k in range(KD):
                pe.wait_ge(squared, KD * l + k + 1)
                pe.matmul(big(0)[:, 0:512], ones[:], n_sq[:, k % 2, 0:512], start=(k == 0), stop=(k == KD - 1))
                pe.matmul(big(0)[:, 512:TOK], ones[:], n_sq[:, k % 2, 512:TOK], start=(k == 0), stop=(k == KD - 1)
                          ).then_inc(summed, 1)

        def norm_dve(dve, l):
            dve.wait_ge(summed, KD * (l + 1))
            dve.tensor_scalar(n_tmp, big(0)[:, 0:TOK], 1.0 / D_MODEL, EPS, ALU.mult, ALU.add).then_inc(sums_read, 1)
            dve.wait_ge(rooted, l + 1)
            dve.reciprocal(n_rstd, n_tmp).then_inc(sums_read, 1)
            dve.wait_ge(sums_read, 2 * l + 2)
            for k in range(KD):
                if l < layers:
                    for s in range(2):
                        ins = dve.scalar_tensor_tensor(out=hT[:, k, seg(s)], in0=xT[:, k, seg(s)],
                                                       scalar=gain[:, k, s:s + 1], in1=n_rstd[:, seg(s)],
                                                       op0=ALU.mult, op1=ALU.mult)
                else:
                    ins = dve.scalar_tensor_tensor(out=hT[:, k], in0=xT[:, k],
                                                   scalar=cols[:, col("final_norm_g", k):col("final_norm_g", k) + 1],
                                                   in1=n_rstd, op0=ALU.mult, op1=ALU.mult)
                ins.then_inc(scaled, 1)

        def out_sync(sp, w_out, kt):
            n = SLAB // kt
            w = w_out.rearrange("(k p) n -> p k n", p=P)
            tr = D_MODEL // n // 2
            with trips(sp, tr) as i:
                slabs.enter(i, [1, 1])
                for u in range(2):
                    slot, free, _ = slabs.take()
                    sp.wait_ge(w_used, free)
                    sp.dma_start(ring[:, slot].rearrange("p (k n) -> p k n", n=n),
                                 w[:, :, bass.ds((2 * i + u) * n, n)]).then_inc(w_loaded[slot], 16)
            slabs.leave(tr)

        def out_pe(pe, l, kt):
            n = SLAB // kt
            tr = D_MODEL // n // 2
            with trips(pe, tr) as i:
                slabs.enter(i, [1, 1])
                for u in range(2):
                    slot, _, full = slabs.take()
                    w = ring[:, slot].rearrange("p (k n) -> p k n", n=n)
                    pe.wait_ge(w_loaded[slot], full)
                    for m in range(n // P):
                        at = u * (n // P) + m
                        pe.wait_ge(out_read, KD * l + 2 * (n // P) * i + at + 1)
                        for k in range(kt):
                            pe.matmul(big(at % 2)[:, 0:512], w[:, k, m * P:(m + 1) * P], yT[:, k, 0:512],
                                      start=(k == 0), stop=(k == kt - 1))
                            mm = pe.matmul(big(at % 2)[:, 512:TOK], w[:, k, m * P:(m + 1) * P], yT[:, k, 512:TOK],
                                           start=(k == 0), stop=(k == kt - 1))
                        if m < n // P - 1:
                            mm.then_inc(out_done, 1)
                        else:
                            slab_through(pe, mm, last_cols(at % 2), out_done)
            slabs.leave(tr)

        def out_dve(dve, l, kt, rstd=None, tmp=None):
            n = SLAB // kt
            tr, per = D_MODEL // n // 2, 2 * (n // P)
            with trips(dve, tr) as i:
                if rstd is not None:
                    dve_t.enter(i, per)
                for at in range(per):
                    m = per * i + at
                    dve.wait_ge(out_done, KD * l + m + 1)
                    src = big(at % 2)[:, 0:TOK]
                    if rstd is not None:
                        dve_t.after(dve.tensor_tensor(tmp[:, at % 2], src, rstd, ALU.mult))
                        src = tmp[:, at % 2]
                    for s in range(2):
                        xm = xT[:, bass.ds(m, 1), seg(s)].rearrange("p a b -> p (a b)")
                        g = mod[:, bass.ds(2 * KD + m, 1), s:s + 1].rearrange("p a b -> p (a b)")
                        ins = dve.scalar_tensor_tensor(out=xm, in0=src[:, seg(s)], scalar=g, in1=xm,
                                                       op0=ALU.mult, op1=ALU.add)
                    ins.then_inc(out_read, 1)
            if rstd is not None:
                dve_t.leave(tr)

        y_out = yT[:, 0:KD, :].rearrange("p a b -> p (a b)").rearrange("p (t d) -> p t d", d=D_MODEL)

        def final_pe(pe):
            pe.wait_ge(scaled, KD * (layers + 1))
            for tt in range(NT):
                if tt >= 3:
                    pe.wait_ge(S["y_copied_a"], tt - 2)
                    pe.wait_ge(S["y_copied_v"], tt - 2)
                for k in range(KD):
                    mm = pe.transpose(big(tt)[:, k * P:(k + 1) * P], hT[:, k, tt * P:(tt + 1) * P], ident[:])
                mm.then_inc(S["y_turned"], 1)

        def final_copy(eng, half):
            a = slice(half * 512, half * 512 + 512)
            for tt in range(NT):
                eng.wait_ge(S["y_turned"], tt + 1)
                if half:
                    eng.tensor_copy(y_out[:, tt, a], big(tt)[:, a]).then_inc(S["y_copied_v"], 1)
                else:
                    eng.activation(y_out[:, tt, a], big(tt)[:, a], ACT.Copy).then_inc(S["y_copied_a"], 1)

        def final_sync(sp):
            for tt in range(NT):
                sp.wait_ge(S["y_copied_a"], tt + 1)
                sp.wait_ge(S["y_copied_v"], tt + 1)
                dst = out["y_sample"][0, tt * P:(tt + 1) * P, :] if tt < LAT // P else out["y_prompt"][0]
                sp.dma_start(dst, y_out[:, tt]).then_inc(stored, 16)

        a_ = Room()
        cq, keyc = a_(Q_RANK // P, TOK), a_(KV_RANK // P, KEYS)
        q_h, k_h = a_(2, TOK), a_(2, KEYS)
        v_h = a_(KEYS // P, P)
        prob = a_(2, 4 * (LAT + PAST) + P)
        probT = a_(5 * LAT + P)
        rope_tab, rope_tmps = a_(TOK), a_(2, TOK)
        rope_tmp = rope_tmps[:, 0]
        nmax, rsum, rinv = a_(16), a_(16), a_(16)
        kpe = prob[:, 0, 0:TOK]
        ckv_raw = prob[:, 0, TOK:3 * TOK].rearrange("p (a b) -> p a b", b=TOK)
        m_sq = probT[:, 0:3 * TOK].rearrange("p (a b) -> p a b", b=TOK)
        kv_sq = prob[:, 1, 0:2 * TOK].rearrange("p (a b) -> p a b", b=TOK)
        cache_in = q_h[:, 0, 0:KV_RANK + ROPE]
        new_rows = v_h.rearrange("p a b -> p (a b)")[:, 0:KV_RANK + ROPE]
        q_rstd, kv_rstd = q_h[:, 1], probT[:, 3 * TOK:4 * TOK]
        rank_tiles = Q_RANK // P + KV_RANK // P
        IN_TILES = 14
        PD = PAIRS

        sems("lat_done", "lat_read", "cache_loaded", "cache_turned", "cache_copied", "rank_squared", "rank_summed",
             "rank_rooted", "rank_ready", "new_turned", "new_copied", "new_stored",
             "q_done", "k_done", "v_done", "q_copied", "q_turned", "k_copied", "v_copied",
             "score_done", "max_done", "exp_done", "sum_done", "prob_ready",
             "probT_done", "probT_a", "probT_v", "attn_done", "attn_read",
             "y_turned", "y_copied_a", "y_copied_v")

        def mla_misc_loads(pool, r):
            pool.dma_start(rope_tab[2 * ROPE:4 * ROPE], t["rope"]).then_inc(S["cache_loaded"], 16)
            pool.dma_start(cache_in[:, 0:KV_RANK], t["cache_mla_ckv"][0, r]).then_inc(S["cache_loaded"], 16)
            pool.dma_start(cache_in[:, KV_RANK:], t["cache_mla_kpe"][0, r]).then_inc(S["cache_loaded"], 16)

        def mla_sync(sp, r):
            w = t["mla_w_in"][r].rearrange("(k p) n -> p k n", p=P)
            for s in range(4):
                dmas = 7 if s == 1 else 1
                slot, free, _ = slabs.take(dmas)
                sp.wait_ge(w_used, free)
                v = ring[:, slot].rearrange("p (k n) -> p k n", n=512)
                if s != 1:
                    at = 0 if s == 0 else 672 + 512 * (s - 2)
                    sp.dma_start(v, w[:, :, at:at + 512]).then_inc(w_loaded[slot], 16)
                    continue
                sp.dma_start(v[:, :, 0:P], w[:, :, 512:640]).then_inc(w_loaded[slot], 16)
                for c in range(2):
                    for at, src, n in ((0, 640, 32), (32, 656, 16), (48, 640, 16)):
                        at += P + 64 * c
                        sp.dma_start(v[:, :, at:at + n], w[:, :, src:src + n]).then_inc(w_loaded[slot], 16)
            wq = t["mla_w_uq"][r].rearrange("(k p) h d -> p k h d", p=P)
            wk = t["mla_w_uk"][r].rearrange("(k p) h d -> p k (h d)", p=P)
            wv = t["mla_w_uv"][r].rearrange("(k p) h d -> p k (h d)", p=P)
            with sp.Fori(0, PD // 2) as i:
                slabs.enter(i, [11, 11])
                for u in range(2):
                    slot, free, _ = slabs.take(11)
                    q, k, v = pair_weights(slot)
                    sp.wait_ge(w_used, free)
                    for c in range(3):
                        h = bass.ds(4 * i + 2 * u, 2)
                        for at, src, n in ((0, 0, QK), (QK, QK - 16, 16), (QK + 16, NOPE, 16)):
                            sp.dma_start(q[:, c, :, at:at + n], wq[:, c, h, src:src + n]).then_inc(w_loaded[slot], 16)
                    for dst, src in ((k, wk), (v, wv)):
                        sp.dma_start(dst, src[:, :, bass.ds((2 * i + u) * P, P)]).then_inc(w_loaded[slot], 16)
            slabs.leave(PD // 2)

        def pair_weights(slot):
            q = ring[:, slot, 0:768].rearrange("p (k h d) -> p k h d", k=3, h=2)
            k = ring[:, slot, 768:1024].rearrange("p (k n) -> p k n", k=2)
            v = ring[:, slot, 1024:1280].rearrange("p (k n) -> p k n", k=2)
            return q, k, v

        def mla_in_pe(pe, r):
            n = 0
            for s in range(4):
                slot, _, full = slabs.take(7 if s == 1 else 1)
                w = ring[:, slot].rearrange("p (k n) -> p k n", n=512)
                pe.wait_ge(w_loaded[slot], full)
                if s == 0:
                    pe.wait_ge(h_ready, KD * (3 * r + 1))
                for m in range(2 if s == 1 else 4):
                    if n >= 3:
                        pe.wait_ge(S["lat_read"], IN_TILES * r + n - 2)
                    for k in range(KD):
                        pe.matmul(big(n)[:, 0:512], w[:, k, m * P:(m + 1) * P], hT[:, k, 0:512],
                                  start=(k == 0), stop=(k == KD - 1))
                        mm = pe.matmul(big(n)[:, 512:TOK], w[:, k, m * P:(m + 1) * P], hT[:, k, 512:TOK],
                                       start=(k == 0), stop=(k == KD - 1))
                    if m == (1 if s == 1 else 3):
                        slab_through(pe, mm, last_cols(n), S["lat_done"])
                    else:
                        mm.then_inc(S["lat_done"], 1)
                    n += 1
            pe.wait_ge(S["cache_loaded"], 48 * (r + 1))
            for c in range(2):
                pe.transpose(bank(6)[:, c * P:(c + 1) * P], cache_in[:, c * P:(c + 1) * P], ident[:])
            pe.transpose(bank(6)[0:ROPE, 2 * P:3 * P], cache_in[:, KV_RANK:], ident[:]).then_inc(S["cache_turned"], 1)
            pe.wait_ge(S["lat_read"], IN_TILES * (r + 1))
            pe.wait_ge(S["rank_squared"], rank_tiles * (r + 1))
            for b, sq, tiles in ((0, m_sq, 3), (1, kv_sq, 2)):
                for k in range(tiles):
                    pe.matmul(big(b)[:, 0:512], ones[:], sq[:, k, 0:512], start=(k == 0), stop=(k == tiles - 1))
                    mm = pe.matmul(big(b)[:, 512:TOK], ones[:], sq[:, k, 512:TOK], start=(k == 0), stop=(k == tiles - 1))
                mm.then_inc(S["rank_summed"], 1)
            pe.wait_ge(S["rank_ready"], 2 * (r + 1))
            for c in range(2):
                pe.transpose(bank(7)[:, c * P:(c + 1) * P], keyc[:, c, LAT + PAST:], ident[:])
            pe.transpose(bank(7)[:, KV_RANK:KV_RANK + ROPE], kpe[0:ROPE, LAT:TOK], ident[0:ROPE, 0:ROPE]
                         ).then_inc(S["new_turned"], 1)

        def mla_in_act(act, r):
            for n in range(IN_TILES):
                act.wait_ge(S["lat_done"], IN_TILES * r + n + 1)
                dst, f = ((cq[:, n], ACT.Copy) if n < 3 else (ckv_raw[:, n - 3], ACT.Copy) if n < 5 else
                          (kpe, ACT.Copy) if n == 5 else (yT[:, n - 6], ACT.Silu))
                act.activation(dst, big(n)[:, 0:TOK], f).then_inc(S["lat_read"], 1)
            act.wait_ge(S["cache_turned"], r + 1)
            act.activation(keyc[:, :, LAT:LAT + PAST], bank(6)[:, 0:2 * P].rearrange("p (a b) -> p a b", b=P), ACT.Copy)
            for h in range(2):
                act.activation(k_h[NOPE:QK, h, LAT:LAT + PAST], bank(6)[0:ROPE, 2 * P:3 * P], ACT.Copy)
            act.wait_ge(S["rank_summed"], 2 * r + 2)
            act.wait_ge(S["rank_rooted"], 4 * r + 2)
            for n, a in enumerate((q_rstd, kv_rstd)):
                act.activation(a, a, ACT.Sqrt).then_inc(S["rank_rooted"], 1)
            act.wait_ge(S["new_turned"], r + 1)
            act.activation(new_rows, bank(7)[:, 0:KV_RANK + ROPE], ACT.Copy).then_inc(S["new_copied"], 1)

        def mla_in_dve(dve, r):
            for n in range(rank_tiles):
                dve.wait_ge(S["lat_read"], IN_TILES * r + n + 1)
                src, dst = (cq[:, n], m_sq[:, n]) if n < 3 else (ckv_raw[:, n - 3], kv_sq[:, n - 3])
                dve.tensor_tensor(dst, src, src, ALU.mult).then_inc(S["rank_squared"], 1)
            dve.wait_ge(S["lat_read"], IN_TILES * r + 6)
            dve.wait_ge(S["cache_loaded"], 48 * (r + 1))
            rot = slice(NOPE, QK)
            dve_t.mark(dve.tensor_tensor(k_h[rot, 0, 0:LAT], kpe[rot, 0:LAT], rope_tab[rot, 0:LAT], ALU.mult))
            dve_t.after(dve.tensor_tensor(rope_tmp[rot, 0:LAT], kpe[QK:P, 0:LAT], rope_tab[QK:P, 0:LAT], ALU.mult))
            dve_t.after(dve.tensor_tensor(k_h[rot, 0, 0:LAT], k_h[rot, 0, 0:LAT], rope_tmp[rot, 0:LAT], ALU.add))
            dve.tensor_copy(k_h[rot, 1, 0:LAT], k_h[rot, 0, 0:LAT])
            for h in range(2):
                dve.tensor_copy(k_h[rot, h, LAT + PAST:], kpe[rot, LAT:TOK])
            dve.wait_ge(S["rank_summed"], 2 * r + 2)
            for b, a, n in ((0, q_rstd, Q_RANK), (1, kv_rstd, KV_RANK)):
                dve.tensor_scalar(a, big(b)[:, 0:TOK], 1.0 / n, EPS, ALU.mult, ALU.add).then_inc(S["rank_rooted"], 1)
            dve.wait_ge(S["rank_rooted"], 4 * r + 4)
            dve_t.mark(dve.reciprocal(q_rstd, q_rstd))
            dve_t.after(dve.reciprocal(kv_rstd, kv_rstd))
            dve_t.after(dve.tensor_scalar(q_rstd, q_rstd, MLA_SCALE, None, ALU.mult))
            for c in range(3):
                g = col("mla_q_norm_g", 3 * r + c)
                dve.scalar_tensor_tensor(out=cq[:, c], in0=cq[:, c], scalar=cols[:, g:g + 1], in1=q_rstd,
                                         op0=ALU.mult, op1=ALU.mult)
            for c in range(2):
                g = col("mla_kv_norm_g", 2 * r + c)
                for src, dst in ((slice(0, LAT), slice(0, LAT)), (slice(LAT, TOK), slice(LAT + PAST, KEYS))):
                    ins = dve.scalar_tensor_tensor(out=keyc[:, c, dst], in0=ckv_raw[:, c, src],
                                                   scalar=cols[:, g:g + 1], in1=kv_rstd[:, src],
                                                   op0=ALU.mult, op1=ALU.mult)
                ins.then_inc(S["rank_ready"], 1)

        def mla_new_store(pool, r):
            pool.wait_ge(S["new_copied"], r + 1)
            pool.dma_start(out["new_mla_ckv"][0, r], new_rows[:, 0:KV_RANK]).then_inc(S["new_stored"], 16)
            pool.dma_start(out["new_mla_kpe"][0, r], new_rows[:, KV_RANK:]).then_inc(S["new_stored"], 16)
            pool.wait_ge(S["new_stored"], 32 * (r + 1))

        NS = 10

        def prob_tile(n):
            h, c = divmod(n, 5)
            return prob[:, h, 640 * c:640 * c + 640] if c < 4 else prob[:, h, 2560:2560 + P]

        def mla_pe(pe, r):
            with pe.Fori(0, PD // 2) as i:
                slabs.enter(i, [11, 11])
                for u in range(2):
                    p = PD * r + u + 2 * i
                    slot, _, full = slabs.take(11)
                    wq, wk, wv = pair_weights(slot)
                    pe.wait_ge(w_loaded[slot], full)
                    pe.wait_ge(S["exp_done"], NS * p + 10)
                    for h in range(2):
                        for k in range(3):
                            pe.matmul(big(h)[:, 0:512], wq[:, k, h], cq[:, k, 0:512], start=(k == 0), stop=(k == 2))
                            mm = pe.matmul(big(h)[:, 512:TOK], wq[:, k, h], cq[:, k, 512:TOK],
                                           start=(k == 0), stop=(k == 2))
                        mm.then_inc(S["q_done"], 1)
                    pe.wait_ge(S["attn_read"], p + 1)
                    for k in range(2):
                        pe.matmul(big(2)[:, 0:512], wk[:, k], keyc[:, k, 0:512], start=(k == 0), stop=(k == 1))
                        mm = pe.matmul(big(2)[:, 512:KEYS], wk[:, k], keyc[:, k, 512:KEYS], start=(k == 0), stop=(k == 1))
                    mm.then_inc(S["k_done"], 1)
                    pe.wait_ge(S["q_copied"], 2 * p + 1)
                    pe.wait_ge(S["q_turned"], 2 * p + 1)
                    for kt in range(KEYS // P):
                        for k in range(2):
                            mm = pe.matmul(big(3)[:, kt * P:(kt + 1) * P], keyc[:, k, kt * P:(kt + 1) * P], wv[:, k],
                                           start=(k == 0), stop=(k == 1))
                    slab_through(pe, mm, last_cols(3), S["v_done"])
                    for n in range(NS):
                        h, c = divmod(n, 5)
                        b = big(4 + n)
                        if c == 0:
                            pe.wait_ge(S["q_copied"], 2 * p + h + 1)
                            pe.wait_ge(S["q_turned"], 2 * p + h + 1)
                            pe.wait_ge(S["k_copied"], 2 * p + h + 1)
                        if n == 0:
                            pe.wait_ge(S["q_copied"], 2 * p + 2)
                            pe.wait_ge(S["q_turned"], 2 * p + 2)
                        if n == 1:
                            pe.wait_ge(S["k_copied"], 2 * p + 2)
                        if n == 2:
                            pe.wait_ge(S["v_copied"], p + 1)
                        if n >= 3:
                            pe.wait_ge(S["exp_done"], NS * p + NS + n - 2)
                        if c < 4:
                            q = q_h[0:QK, h, c * P:(c + 1) * P]
                            pe.matmul(b[:, 0:512], q, k_h[0:QK, h, 0:512], start=True, stop=True)
                            pe.matmul(b[:, 512:640], q, k_h[0:QK, h, 512:640], start=True, stop=True
                                      ).then_inc(S["score_done"], 1)
                        else:
                            pe.matmul(b[:, 0:P], q_h[0:QK, h, LAT:TOK], k_h[0:QK, h, LAT + PAST:KEYS],
                                      start=True, stop=True).then_inc(S["score_done"], 1)
                    for h in range(2):
                        at = slice(VDIM * h, VDIM * h + VDIM)
                        for kt in range(6):
                            pe.wait_ge(S["probT_a" if kt % 2 else "probT_v"], 6 * p + 3 * h + kt // 2 + 3)
                            if kt < 5:
                                for c in range(4):
                                    if kt == 0:
                                        pe.wait_ge(S["prob_ready"], NS * p + 5 * h + c + 1)
                                    mm = pe.transpose(bank(6 + kt % 2)[:, c * P:(c + 1) * P],
                                                      prob_tile(5 * h + c)[:, kt * P:(kt + 1) * P], ident[:])
                            else:
                                pe.wait_ge(S["prob_ready"], NS * p + 5 * h + 5)
                                mm = pe.transpose(bank(7)[:, 0:P], prob_tile(5 * h + 4), ident[:])
                            mm.then_inc(S["probT_done"], 1)
                        for kt in range(5):
                            pe.wait_ge(S["probT_a" if kt % 2 else "probT_v"], 6 * p + 3 * h + kt // 2 + 4)
                            pe.matmul(big(2)[at, 0:512], v_h[:, kt, at], probT[:, kt * LAT:(kt + 1) * LAT],
                                      start=(kt == 0), stop=(kt == 4))
                        pe.wait_ge(S["probT_a"], 6 * p + 3 * h + 6)
                        mm = pe.matmul(big(2)[at, 512:TOK], v_h[:, 5, at], probT[:, 5 * LAT:], start=True, stop=True)
                    mm.then_inc(S["attn_done"], 1)
            slabs.leave(PD // 2)

        def mla_act(act, r):
            with act.Fori(0, PD // 2) as i:
                for u in range(2):
                    p = PD * r + u + 2 * i
                    for h in range(2):
                        act.wait_ge(S["q_done"], 2 * p + h + 1)
                        act.activation(q_h[0:NOPE, h], big(h)[0:NOPE, 0:TOK], ACT.Copy).then_inc(S["q_copied"], 1)
                    act.wait_ge(S["k_done"], p + 1)
                    for h in range(2):
                        act.activation(k_h[0:NOPE, h], big(2)[NOPE * h:NOPE * h + NOPE, 0:KEYS], ACT.Copy
                                       ).then_inc(S["k_copied"], 1)
                    act.wait_ge(S["v_done"], p + 1)
                    act.activation(v_h, big(3)[:, 0:KEYS].rearrange("p (a b) -> p a b", b=P), ACT.Copy
                                   ).then_inc(S["v_copied"], 1)
                    for n in range(NS):
                        act.wait_ge(S["max_done"], NS * p + n + 1)
                        a = prob_tile(n)
                        act.activation(a, big(4 + n)[:, 0:a.shape[1]], ACT.Exp, bias=nmax[:, n:n + 1],
                                       accum_out=rsum[:, n:n + 1]).then_inc(S["exp_done"], 1)
                    for h in range(2):
                        for kt in (1, 3, 5):
                            act.wait_ge(S["probT_done"], 12 * p + 6 * h + kt + 1)
                            n = LAT if kt < 5 else P
                            act.activation(probT[:, kt * LAT:kt * LAT + n], bank(7)[:, 0:n], ACT.Copy
                                           ).then_inc(S["probT_a"], 1)

        def mla_dve(dve, r):
            rot = slice(NOPE, QK)
            with dve.Fori(0, PD // 2) as i:
                dve_t.enter(i, 8)
                for u in range(2):
                    p = PD * r + u + 2 * i
                    for h in range(2):
                        dve.wait_ge(S["q_done"], 2 * p + h + 1)
                        dve_t.mark(dve.tensor_tensor(q_h[rot, h], big(h)[rot, 0:TOK], rope_tab[rot], ALU.mult))
                        dve_t.after(dve.tensor_tensor(rope_tmps[rot, h], big(h)[QK:P, 0:TOK], rope_tab[QK:P], ALU.mult))
                        dve.tensor_tensor(q_h[rot, h], q_h[rot, h], rope_tmps[rot, h], ALU.add).then_inc(S["q_turned"], 1)
                    for n in range(NS + 1):
                        if n < NS:
                            dve.wait_ge(S["score_done"], NS * p + n + 1)
                            w = prob_tile(n).shape[1]
                            dve.tensor_reduce(nmax[:, n:n + 1], big(4 + n)[:, 0:w], X, ALU.max, negate=True
                                              ).then_inc(S["max_done"], 1)
                        if n:
                            dve.wait_ge(S["exp_done"], NS * p + NS + n)
                            dve.reciprocal(rinv[:, n - 1:n], rsum[:, n - 1:n]).then_inc(S["sum_done"], 1)
                    for h in range(2):
                        for kt in (0, 2, 4):
                            dve.wait_ge(S["probT_done"], 12 * p + 6 * h + kt + 1)
                            dve.tensor_copy(probT[:, kt * LAT:(kt + 1) * LAT], bank(6)).then_inc(S["probT_v"], 1)
                    dve.wait_ge(S["attn_done"], p + 1)
                    y = yT[:, bass.ds(2 * i + u, 1), :].rearrange("p a b -> p (a b)")
                    dve.tensor_tensor(y, big(2)[:, 0:TOK], y, ALU.mult).then_inc(S["attn_read"], 1)
            dve_t.leave(PD // 2)

        def mla_pool(pool, r):
            with pool.Fori(0, PD // 2) as i:
                for u in range(2):
                    p = PD * r + u + 2 * i
                    for n in range(NS):
                        pool.wait_ge(S["sum_done"], NS * p + n + 1)
                        a = prob_tile(n)
                        pool.tensor_tensor(a, a, rinv[:, n:n + 1].broadcast_to([P, a.shape[1]]), ALU.mult).then_inc(S["prob_ready"], 1)

        def mla_credits_act(act):
            act.sem_inc(S["exp_done"], NS)
            act.sem_inc(S["probT_a"], 3)

        def credits_dve(dve):
            dve.sem_inc(S["probT_v"], 3)
            dve.sem_inc(S["attn_read"], 1)
            dve.sem_inc(ada_read, 2)
            dve.sem_inc(out_read, 2)

        LC = LAT // P
        b_ = Room()
        s_dt, s_nacs, s_eacs = b_(NT, 2 * SH), b_(NT, 2 * SH), b_(NT, 2 * SH)
        s_etot, s_wend = b_(NT, 2 * SH), b_(NT, 2 * SH)
        s_a, s_bias, s_d = b_(2 * SH), b_(2 * SH), b_(SH)
        s_ssq, s_one = b_(NT, GROUPS), b_(NT)
        s_raw, s_xc = b_(4, RAW), b_(4, CONV)
        s_tmp, s_rstd = s_raw[:, 0:2, 0:TOK], s_xc[:, 0, 0:TOK]
        s_xb = b_(NT, 3 * P)
        s_xe, s_xd = b_(NT, 2, GX), b_(2, 2, GX)
        s_m = b_(3, 8, P)
        s_h = b_(LC, 2, GX)
        s_z, s_y, s_t = b_(NT, GX), b_(NT, GX), b_(2, 2 * GX)
        s_cb, s_in, s_fin = b_(TOK), b_(4, P), b_(4, P)
        s_t2 = s_in.rearrange("p (a b) n -> p a (b n)", a=2)
        s_dump = s_z
        s_dtmp = s_m[:, 0].rearrange("p a b -> p (a b)")
        s_dA = s_m[:, 1].rearrange("p a b -> p (a b)")[:, 0:NT * 2 * SH].rearrange("p (a b) -> p a b", b=2 * SH)
        s_rows = s_h.rearrange("p a b c -> p (a b c)")[0:SH, 0:2 * TOK].rearrange("p (d n) -> p d n", d=2)
        s_v, s_e = s_dtmp[:, 0:320], s_dtmp[:, 320:640]

        sems("s_small_loaded", "s_dt_summed", "s_v_ready", "s_abs", "s_dA_ready", "s_acs_done", "s_acs_read",
             "s_rows_copied", "s_rows_stored", "s_cols_ready", "s_cols_exp", "s_zeroed",
             "s_pj_done", "s_pj_read", "s_tap0", "s_conved", "s_x_ready", "s_state_loaded", "s_state_turned",
             "s_state_copied", "s_in_turned", "s_in_copied", "s_cb_done", "s_cb_copied", "s_xe_ready", "s_upd_done",
             "s_h_ready", "s_fin_done", "s_fin_copied", "s_fin_stored", "s_xd_ready", "s_m_ready",
             "s_y_done", "s_y_read", "s_y_ready", "s_y_squared", "s_y_turned", "s_y_copied",
             "s_rows_loaded0", "s_rows_loaded1", "s_rows_loaded2", "s_masked", "s_decayed", "s_rms_done", "s_rms_diag",
             "s_rms_root")

        def ssd_sync(sp):
            w = t["ssd_w_in"][0].rearrange("(k p) n -> p k n", p=P)
            slot, free, _ = slabs.take()
            sp.wait_ge(w_used, free)
            sp.dma_start(ring[:, slot, 0:KD * 2 * SH].rearrange("p (k n) -> p k n", n=2 * SH),
                         w[:, :, 3 * INNER:3 * INNER + 2 * SH]).then_inc(w_loaded[slot], 16)
            with sp.Fori(0, GROUPS) as g:
                slabs.enter(g, [3, 1])
                slot, free, _ = slabs.take(3)
                v = ring[:, slot].rearrange("p (k n) -> p k n", n=512)
                sp.wait_ge(w_used, free)
                apart(sp)
                for at, src, n in ((0, INNER + GX * g, GX), (GX, 2 * INNER + P * g, P),
                                   (GX + P, 2 * INNER + GROUPS * STATE + P * g, P)):
                    sp.dma_start(v[:, :, at:at + n], w[:, :, bass.ds(src, n)]).then_inc(w_loaded[slot], 16)
                slot, free, _ = slabs.take()
                sp.wait_ge(w_used, free)
                apart(sp)
                sp.dma_start(ring[:, slot, 0:KD * GX].rearrange("p (k n) -> p k n", n=GX),
                             w[:, :, bass.ds(GX * g, GX)]).then_inc(w_loaded[slot], 16)
            slabs.leave(GROUPS)

        def ssd_in_pe(pe):
            slot, _, full = slabs.take()
            w = ring[:, slot, 0:KD * 2 * SH].rearrange("p (k n) -> p k n", n=2 * SH)
            pe.wait_ge(w_loaded[slot], full)
            pe.wait_ge(h_ready, KD * 2)
            for tt in range(NT):
                for k in range(KD):
                    mm = pe.matmul(bank(6)[:, tt * 64:(tt + 1) * 64], hT[:, k, tt * P:(tt + 1) * P], w[:, k],
                                   start=(k == 0), stop=(k == KD - 1))
            slab_through(pe, mm, bank(6)[0:2, 510:512], S["s_dt_summed"])
            pe.wait_ge(S["s_dA_ready"], 1)
            for tt in range(NT):
                for d in range(2):
                    pe.matmul(bank(7)[:, tt * 64 + d * SH:tt * 64 + d * SH + SH], tri[:, d],
                              s_dA[:, tt, d * SH:(d + 1) * SH], start=True, stop=True)
            for d in range(2):
                for tt in range(NT):
                    pe.matmul(big(d)[0:SH, tt * P:(tt + 1) * P], s_dA[:, tt, d * SH:(d + 1) * SH], tri[:, d],
                              start=True, stop=True)
            pe.matmul(bank(6)[:, 0:320], ones[:], s_dA.rearrange("p a b -> p (a b)"), start=True, stop=True
                      ).then_inc(S["s_acs_done"], 1)
            pe.wait_ge(S["s_rows_copied"], 2)
            pe.wait_ge(S["s_acs_read"], 1)

        def ssd_in_dve(dve):
            dve.wait_ge(S["s_small_loaded"], 48)
            dve.wait_ge(S["s_dt_summed"], 1)
            bias = s_bias.unsqueeze(1).broadcast_to([P, NT, 2 * SH])
            dve.tensor_tensor(s_v.rearrange("p (a b) -> p a b", b=64),
                              bank(6)[:, 0:320].rearrange("p (a b) -> p a b", b=64), bias, ALU.add
                              ).then_inc(S["s_v_ready"], 1)
            dve.wait_ge(S["s_abs"], 4)
            dt2 = s_dt.rearrange("p a b -> p (a b)")
            dve_t.after(dve.scalar_tensor_tensor(out=dt2, in0=s_v, scalar=0.0, in1=s_e, op0=ALU.max, op1=ALU.add))
            dve.scalar_tensor_tensor(out=s_dA, in0=s_dt, scalar=-1.0, in1=s_a.unsqueeze(1).broadcast_to([P, NT, 2 * SH]),
                                     op0=ALU.mult, op1=ALU.mult).then_inc(S["s_dA_ready"], 1)
            dve.wait_ge(S["s_acs_done"], 1)
            acs, tot = bank(7)[:, 0:320], bank(6)[:, 0:320]
            fl = lambda a: a.rearrange("p a b -> p (a b)")
            dve_t.mark(dve.tensor_scalar(fl(s_nacs), acs, -1.0, None, ALU.mult))
            dve_t.after(dve.tensor_copy(fl(s_etot), tot))
            dve.tensor_tensor(fl(s_wend), fl(s_etot), fl(s_nacs), ALU.add).then_inc(S["s_acs_read"], 1)
            dve.wait_ge(S["s_cols_exp"], 3)
            dve.tensor_tensor(fl(s_wend), fl(s_wend), fl(s_dt), ALU.mult).then_inc(S["s_cols_ready"], 1)
            dve.wait_ge(S["s_cols_ready"], 1)

        def ssd_in_act(act):
            act.wait_ge(S["s_zeroed"], 1)
            act.wait_ge(S["s_small_loaded"], 48)
            act.activation(s_a, s_a, ACT.Exp).then_inc(S["s_abs"], 1)
            act.wait_ge(S["s_v_ready"], 1)
            act.activation(s_e, s_v, ACT.Abs).then_inc(S["s_abs"], 1)
            act.wait_ge(S["s_abs"], 2)
            act.activation(s_e, s_e, ACT.Exp, scale=-1.0).then_inc(S["s_abs"], 1)
            act.wait_ge(S["s_abs"], 3)
            act.activation(s_e, s_e, ACT.Ln, bias=1.0).then_inc(S["s_abs"], 1)
            act.wait_ge(S["s_acs_done"], 1)
            for d in range(2):
                act.activation(s_rows[:, d], big(d)[0:SH, 0:TOK], ACT.Copy).then_inc(S["s_rows_copied"], 1)
            act.wait_ge(S["s_acs_read"], 1)
            act.activation(s_eacs, s_nacs, ACT.Exp, scale=-1.0).then_inc(S["s_cols_exp"], 1)
            act.activation(s_etot, s_etot, ACT.Exp).then_inc(S["s_cols_exp"], 1)
            act.activation(s_wend, s_wend, ACT.Exp).then_inc(S["s_cols_exp"], 1)

        def conv_tile(n, g):
            return 2 * g + n if n < 2 else (16 + g if n == 2 else 24 + g)

        def pcol(c):
            return cols[:, bass.ds(c, 1)]

        def xc_tile(n, tt):
            at = tt * P if tt < LC else C_CTX
            return s_xc[:, n, at:at + P]

        def ssd_pe(pe):
            with pe.Fori(0, GROUPS) as g:
                slabs.enter(g, [3, 1])
                for n in range(9):
                    if n in (0, 4):
                        slot, _, full = slabs.take(3 if n == 0 else 1)
                        pe.wait_ge(w_loaded[slot], full)
                        w = ring[:, slot, 0:SLAB if n == 0 else KD * GX].rearrange("p (k n) -> p k n", k=KD)
                    pe.wait_ge(S["s_pj_read"], 9 * g + 9 + max(n - 1, 0))
                    b = big(n % 2)
                    for k in range(KD):
                        if n < 4:
                            pe.matmul(b[:, 0:512], w[:, k, n * P:(n + 1) * P], hT[:, k, 0:512],
                                      start=(k == 0), stop=(k == KD - 1))
                            mm = pe.matmul(b[:, 512:TOK], w[:, k, n * P:(n + 1) * P], hT[:, k, 512:TOK],
                                           start=(k == 0), stop=(k == KD - 1))
                        else:
                            mm = pe.matmul(b[:, 0:GX], hT[:, k, (n - 4) * P:(n - 3) * P], w[:, k],
                                           start=(k == 0), stop=(k == KD - 1))
                    if n in (3, 8):
                        slab_through(pe, mm, big(n % 2)[0:2, 1020:1022] if n == 3 else b[0:2, 510:512], S["s_pj_done"])
                    else:
                        mm.then_inc(S["s_pj_done"], 1)
                pe.wait_ge(S["s_state_loaded"], 32 * g + 32)
                pe.wait_ge(S["s_y_copied"], 2 * g + 2)
                for c in range(4):
                    mm = pe.transpose(bank(5)[:, c * P:(c + 1) * P], s_in[:, c], ident[:])
                mm.then_inc(S["s_state_turned"], 1)
                pe.wait_ge(S["s_x_ready"], 4 * g + 4)
                for tt in range(NT):
                    if tt == 1:
                        pe.wait_ge(S["s_state_copied"], g + 1)
                    if tt >= 2:
                        pe.wait_ge(S["s_in_copied"], NT * g + tt - 1)
                    for n in range(3):
                        mm = pe.transpose(bank(4 + tt % 2)[:, n * P:(n + 1) * P], xc_tile(n, tt), ident[:])
                    mm.then_inc(S["s_in_turned"], 1)
                pe.wait_ge(S["s_y_read"], NT * g + NT)
                for tt in range(NT):
                    b = bank(6)[:, tt * P:(tt + 1) * P] if tt < LC else bank(7)[:, 0:P]
                    mm = pe.matmul(b, xc_tile(2, tt), xc_tile(3, tt), start=True, stop=True)
                mm.then_inc(S["s_cb_done"], 1)
                pe.wait_ge(S["s_in_copied"], NT * g + NT)
                pe.wait_ge(S["s_xe_ready"], NT * g + NT)
                for s in range(LC - 1):
                    if s == 2:
                        pe.wait_ge(S["s_h_ready"], 3 * g + 1)
                    for d, tt in ((0, s), (1, LC - 1 - s)):
                        mm = pe.matmul(bank(4 + s % 2)[:, d * GX:(d + 1) * GX], s_xb[:, tt, 2 * P:], s_xe[:, tt, d],
                                       start=True, stop=True)
                    mm.then_inc(S["s_upd_done"], 1)
                pe.wait_ge(S["s_h_ready"], 3 * g + 2)
                for d in range(2):
                    for c in range(2):
                        mm = pe.matmul(bank(5)[:, (2 * d + c) * P:(2 * d + c + 1) * P], s_xe[:, LC, d, c * P:(c + 1) * P],
                                       s_xb[:, LC, 2 * P:], start=True, stop=True)
                mm.then_inc(S["s_fin_done"], 1)
                pe.wait_ge(S["s_cb_copied"], g + 1)
                for tt in range(NT):
                    pe.wait_ge(S["s_xd_ready"], NT * g + tt + 1)
                    pe.wait_ge(S["s_m_ready"], NT * g + tt + 1)
                    if tt:
                        pe.wait_ge(S["s_y_read"], NT * g + tt + NT)
                    for h in range(GH):
                        for d in range(2):
                            mm = pe.matmul(bank(6)[:, h * HD:(h + 1) * HD], s_m[:, tt % 3, d * GH + h],
                                           s_xd[:, tt % 2, d, h * HD:(h + 1) * HD], start=(d == 0), stop=(d == 1))
                    if tt < LC:
                        if tt == 0:
                            pe.wait_ge(S["s_h_ready"], 3 * g + 3)
                        mm = pe.matmul(bank(7), xc_tile(3, tt), s_h[:, tt].rearrange("p a b -> p (a b)"),
                                       start=True, stop=True)
                    mm.then_inc(S["s_y_done"], 1)
                for c in range(2):
                    if c == 0:
                        pe.wait_ge(S["s_y_ready"], NT * g + NT)
                        pe.wait_ge(S["s_fin_copied"], g + 1)
                    else:
                        pe.wait_ge(S["s_y_copied"], 2 * g + 3)
                    for tt in range(NT):
                        mm = pe.transpose(big(2)[:, tt * P:(tt + 1) * P], s_y[:, tt, c * P:(c + 1) * P], ident[:])
                    mm.then_inc(S["s_y_turned"], 1)
            slabs.leave(GROUPS)
            pe.wait_ge(S["s_rms_diag"], 1)
            for tt in range(NT):
                mm = pe.matmul(big(0)[:, tt * P:(tt + 1) * P], ones[:], s_m[:, 0:2].rearrange("p a b c -> p (a b) c")[:, tt],
                               start=True, stop=True)
            mm.then_inc(S["s_rms_done"], 1)

        def ssd_act(act):
            def exps(g, tt):
                act.wait_ge(S["s_masked"], NT * g + tt + 1)
                for c in range(8):
                    d, h = divmod(c, GH)
                    nac = s_nacs[:, tt, bass.ds(d * SH + GH * g + h, 1)]
                    ins = act.activation(s_m[:, tt % 3, c], s_m[:, tt % 3, c], ACT.Exp, bias=nac)
                ins.then_inc(S["s_decayed"], 1)

            with act.Fori(0, GROUPS) as g:
                act_t.enter(g, 4)
                for n in range(9):
                    act.wait_ge(S["s_pj_done"], 9 * g + n + 1)
                    if n < 4:
                        if n == 0:
                            act.wait_ge(S["s_conved"], 4 * g + 4)
                            act.wait_ge(S["s_y_done"], NT * g + NT)
                        b = big(n % 2)
                        act_t.mark(act.activation(s_raw[:, n, RAW_LAT:RAW_LAT + LAT], b[:, 0:LAT], ACT.Copy))
                        act.activation(s_raw[:, n, RAW_CTX:RAW_CTX + CTX], b[:, LAT:TOK], ACT.Copy
                                       ).then_inc(S["s_pj_read"], 1)
                        act.wait_ge(S["s_pj_read"], 9 * g + 9 + n + 1)
                        act.activation(s_xc[:, n], s_raw[:, n, 0:CONV], ACT.Identity,
                                       bias=pcol(col("ssd_conv_b") + conv_tile(n, g)),
                                       scale=pcol(col("ssd_conv_w") + conv_tile(n, g))).then_inc(S["s_tap0"], 1)
                    else:
                        act.activation(s_z[:, n - 4], big(n % 2)[:, 0:GX], ACT.Silu).then_inc(S["s_pj_read"], 1)
                        if n < 8:
                            act.wait_ge(S["s_conved"], 4 * g + 4 + n - 3)
                            act.activation(s_xc[:, n - 4], s_xc[:, n - 4], ACT.Silu).then_inc(S["s_x_ready"], 1)
                act.wait_ge(S["s_state_turned"], g + 1)
                act.activation(s_h[:, 0, 0], bank(5)[:, 0:GX], ACT.Copy)
                act.activation(s_h[:, LC - 1, 1], bank(5)[:, GX:2 * GX], ACT.Copy).then_inc(S["s_state_copied"], 1)
                for tt in range(NT):
                    act.wait_ge(S["s_in_turned"], NT * g + tt + 1)
                    act.activation(s_xb[:, tt], bank(4 + tt % 2)[:, 0:3 * P], ACT.Copy).then_inc(S["s_in_copied"], 1)
                act.wait_ge(S["s_cb_done"], g + 1)
                act.activation(s_cb[:, 0:LAT], bank(6), ACT.Copy)
                act.activation(s_cb[:, LAT:TOK], bank(7)[:, 0:P], ACT.Copy).then_inc(S["s_cb_copied"], 1)
                for tt in range(3):
                    exps(g, tt)
                act.wait_ge(S["s_fin_done"], g + 1)
                act.activation(s_fin, bank(5).rearrange("p (a b) -> p a b", b=P), ACT.Copy).then_inc(S["s_fin_copied"], 1)
                for tt in range(3, NT):
                    exps(g, tt)
                for tt in range(NT):
                    act.wait_ge(S["s_y_ready"], NT * g + tt + 1)
                    act.activation(s_dump[:, tt], s_y[:, tt], ACT.Square,
                                   accum_out=s_ssq[:, tt, bass.ds(g, 1)]).then_inc(S["s_y_squared"], 1)
                for c in range(2):
                    act.wait_ge(S["s_y_turned"], 2 * g + c + 1)
                    act.activation(yT[:, bass.ds(2 * g + c, 1), :].rearrange("p a b -> p (a b)"), big(2)[:, 0:TOK],
                                   ACT.Copy, scale=pcol(col("ssd_norm_g") + 2 * g + c)).then_inc(S["s_y_copied"], 1)
            act_t.leave(GROUPS)
            act.wait_ge(S["s_rms_root"], 1)
            act.activation(s_rstd, s_rstd, ACT.Sqrt).then_inc(S["s_rms_root"], 1)

        def ssd_dve(dve):
            with dve.Fori(0, GROUPS) as g:
                dve_t.enter(g, 25)
                for n in range(4):
                    dve.wait_ge(S["s_tap0"], 4 * g + n + 1)
                    for k in range(1, CW):
                        ins = dve.scalar_tensor_tensor(out=s_xc[:, n], in0=s_raw[:, n, k:k + CONV],
                                                       scalar=pcol(col("ssd_conv_w", 32 * k) + conv_tile(n, g)),
                                                       in1=s_xc[:, n], op0=ALU.mult, op1=ALU.add)
                        if k < CW - 1:
                            dve_t.after(ins)
                        else:
                            ins.then_inc(S["s_conved"], 1)

                def weigh(dst, tt, by):
                    x = s_xb[:, tt, 0:GX].rearrange("p (h w) -> p h w", w=HD).unsqueeze(1).broadcast_to([P, 2, GH, HD])
                    f = by[:, tt].rearrange("p (d h) -> p d h", d=2)[:, :, bass.ds(GH * g, GH)]
                    return dve.tensor_tensor(dst.rearrange("p d (h w) -> p d h w", w=HD), x,
                                             f.unsqueeze(3).broadcast_to([P, 2, GH, HD]), ALU.mult)

                for tt in range(NT):
                    dve.wait_ge(S["s_in_copied"], NT * g + tt + 1)
                    weigh(s_xe[:, tt], tt, s_wend).then_inc(S["s_xe_ready"], 1)

                for s in range(LC - 1):
                    for d, tt, nx in ((0, s, s + 1), (1, LC - 1 - s, LC - 2 - s)):
                        f = s_etot[:, tt, bass.ds(d * SH + GH * g, GH)].unsqueeze(2).broadcast_to([P, GH, HD])
                        ins = dve.tensor_tensor(s_h[:, nx, d].rearrange("p (h w) -> p h w", w=HD),
                                                s_h[:, tt, d].rearrange("p (h w) -> p h w", w=HD), f, ALU.mult)
                        if d:
                            dve_t.after(ins)
                        else:
                            dve_t.mark(ins)
                    dve.wait_ge(S["s_upd_done"], 3 * g + s + 1)
                    for d, nx in ((0, s + 1), (1, LC - 2 - s)):
                        ins = dve.tensor_tensor(s_h[:, nx, d], s_h[:, nx, d], bank(4 + s % 2)[:, d * GX:(d + 1) * GX],
                                                ALU.add)
                        if d:
                            ins.then_inc(S["s_h_ready"], 1)
                        else:
                            dve_t.mark(ins)
                    dve.wait_ge(S["s_h_ready"], 3 * g + s + 1)
                dve.wait_ge(S["s_cb_copied"], g + 1)
                for tt in range(NT):
                    weigh(s_xd[:, tt % 2], tt, s_dt).then_inc(S["s_xd_ready"], 1)
                    dve.wait_ge(S["s_decayed"], NT * g + tt + 1)
                    m = s_m[:, tt % 3]
                    dve.tensor_tensor(m, m, s_cb[:, tt * P:(tt + 1) * P].unsqueeze(1).broadcast_to([P, 8, P]), ALU.mult
                                      ).then_inc(S["s_m_ready"], 1)
                    dve.wait_ge(S["s_y_done"], NT * g + tt + 1 + NT)
                    y = s_y[:, tt]
                    if tt < LC:
                        tmp = s_t[:, tt % 2]
                        f = s_eacs[:, tt].rearrange("p (d h) -> p d h", d=2)[:, :, bass.ds(GH * g, GH)]
                        dve_t.after(dve.tensor_tensor(tmp.rearrange("p (d h w) -> p d h w", d=2, w=HD),
                                                      bank(7).rearrange("p (d h w) -> p d h w", d=2, w=HD),
                                                      f.unsqueeze(3).broadcast_to([P, 2, GH, HD]), ALU.mult))
                        dve_t.after(dve.tensor_tensor(y, bank(6)[:, 0:GX], tmp[:, 0:GX], ALU.add))
                        dve.tensor_tensor(y, y, tmp[:, GX:], ALU.add).then_inc(S["s_y_read"], 1)
                    else:
                        dve.tensor_copy(y, bank(6)[:, 0:GX]).then_inc(S["s_y_read"], 1)
            dve_t.leave(GROUPS)
            dve.wait_ge(S["s_y_squared"], NT * GROUPS)
            dve_t.after(dve.tensor_reduce(s_one, s_ssq, X, ALU.add))
            diag = s_m[:, 0:2].rearrange("p a b c -> p (a b) c")
            for tt in range(NT):
                ins = dve.tensor_scalar(diag[:, tt], ident[:], s_one[:, tt:tt + 1], None, ALU.mult)
            ins.then_inc(S["s_rms_diag"], 1)
            dve.wait_ge(S["s_rms_done"], 1)
            dve.tensor_scalar(s_rstd, big(0)[:, 0:TOK], 1.0 / INNER, EPS, ALU.mult, ALU.add).then_inc(S["s_rms_root"], 1)

        def ssd_out_scale(dve):
            dve.wait_ge(S["s_rms_root"], 2)
            dve_t.after(dve.reciprocal(s_rstd, s_rstd))

        def ssd_pool(pool):
            for n, (dst, src) in enumerate(((s_bias, t["ssd_dt_bias"]), (s_a, t["ssd_a_log"]), (s_d, t["ssd_d"]))):
                v = src.rearrange("a d h -> a (d h)") if len(src.shape) == 3 else src
                pool.dma_start(dst, v.broadcast_to([P, v.shape[1]])).then_inc(S["s_small_loaded"], 16)
            pool.memset(s_raw, 0.0).then_inc(S["s_zeroed"], 1)
            pool.wait_ge(S["s_rows_copied"], 2)
            for d in range(2):
                pool.dma_start(acs_rows[d * SH:(d + 1) * SH], s_rows[:, d]).then_inc(S["s_rows_stored"], 16)
            pool.wait_ge(S["s_rows_stored"], 32)
            rows = acs_rows.rearrange("(d h) n -> d h n", d=2)

            def load_rows(g, tt):
                for d in range(2):
                    src = rows[d, bass.ds(GH * g, GH), tt * P:(tt + 1) * P].unsqueeze(0)
                    pool.dma_start(s_m[:, tt % 3, d * GH:(d + 1) * GH], src.broadcast_to([P, GH, P])
                                   ).then_inc(S[f"s_rows_loaded{tt % 3}"], 16)

            def mask(g, tt):
                per = 64 if tt % 3 < 2 else 32
                pool.wait_ge(S[f"s_rows_loaded{tt % 3}"], per * g + 32 * (tt // 3) + 32)
                m = s_m[:, tt % 3].rearrange("p (d h) i -> p d h i", d=2)
                for d in range(2):
                    ins = pool.tensor_tensor(m[:, d], m[:, d], neg[:, d].unsqueeze(1).broadcast_to([P, GH, P]), ALU.add)
                    if d == 0:
                        pool_t.mark(ins)
                ins.then_inc(S["s_masked"], 1)

            with pool.Fori(0, GROUPS) as g:
                pool_t.enter(g, 15)
                pool.wait_ge(S["s_y_done"], NT * g + NT)
                apart(pool)
                for d in range(2):
                    src = t["state_ssd"][0, 0, d, bass.ds(GH * g, GH)].rearrange("(a h) w n -> (h w) a n", a=2)
                    pool.dma_start(s_in[:, 2 * d:2 * d + 2], src).then_inc(S["s_state_loaded"], 16)
                for tt in range(3):
                    load_rows(g, tt)
                for tt in range(3):
                    mask(g, tt)
                pool.wait_ge(S["s_fin_copied"], g + 1)
                apart(pool)
                for d in range(2):
                    dst = out["new_ssd"][0, 0, d, bass.ds(GH * g, GH)].rearrange("(a h) w n -> (h w) a n", a=2)
                    pool.dma_start(dst, s_fin[:, 2 * d:2 * d + 2]).then_inc(S["s_fin_stored"], 16)
                for tt in range(NT):
                    pool.wait_ge(S["s_y_read"], NT * g + NT + tt + 1)
                    apart(pool)
                    if tt < 2:
                        load_rows(g, tt + 3)
                    y, x = s_y[:, tt], s_xb[:, tt, 0:GX]
                    xd = s_t2[:, tt % 2]
                    f = s_d[:, bass.ds(GH * g, GH)].unsqueeze(2).broadcast_to([P, GH, HD])
                    pool_t.after(pool.tensor_tensor(xd.rearrange("p (h w) -> p h w", w=HD),
                                                    x.rearrange("p (h w) -> p h w", w=HD), f, ALU.mult))
                    pool_t.after(pool.tensor_tensor(y, y, xd, ALU.add))
                    pool.tensor_tensor(y, y, s_z[:, tt], ALU.mult).then_inc(S["s_y_ready"], 1)
                    if tt < 2:
                        mask(g, tt + 3)
                pool.wait_ge(S["s_fin_stored"], 32 * g + 32)
            pool_t.leave(GROUPS)

        def ssd_credits_act(act):
            act.sem_inc(S["s_pj_read"], 9)
            act.sem_inc(S["s_y_copied"], 2)

        def ssd_credits_dve(dve):
            dve.sem_inc(S["s_conved"], 4)
            dve.sem_inc(S["s_y_read"], 5)

        def ssd_credits_pe(pe):
            pe.sem_inc(S["s_y_done"], 5)


        c_ = Room()
        m_raw, m_xc = c_(KH, RAW), c_(KH, CONV)
        m_wide = c_(16, TOK)
        m_q = m_wide[:, 0:4]
        m_k = m_wide[:, 4:8]
        m_v = m_wide[:, 8:12].rearrange("p a b -> p (a b)").rearrange("p (t n) -> p t n", n=DH)
        m_hh = m_wide[:, 12:16].rearrange("p a b -> p (a b)").rearrange("p (t n) -> p t n", n=DH)
        m_sw, m_swc = c_(LC, TOK), c_(2, P)
        m_row, m_diag = c_(2, TOK), c_(2, TOK)
        m_t = c_(2, DH)
        m_gt, m_lf, m_gb = c_(NT, 16), c_(NT, 16), c_(16)
        m_c = c_(P)
        m_den, m_r, m_rg = c_(8), c_(2, 2), c_(2, 2)
        m_stat, m_mv, m_sd = c_(NT, 6), c_(NT, 2), c_(NT)
        m_m0, m_new = c_(2), c_(2)
        m_kw = m_sw.rearrange("p a b -> p (a b)")[:, 0:2 * DH].rearrange("p (d n) -> p d n", d=2)
        m_cst = m_t
        m_nst = m_diag.rearrange("p a b -> p (a b)")[0:1, 0:2 * DH]
        m_zero = m_raw[0:ML_HEADS, 0, 0:LAT]
        R_IG, R_LF, R_BC, R_G, R_M, R_GI, R_EN, R_WE = range(0, 16, 2)
        PJ = 26
        kinds = ["xm"] * 4 + ["o"] * NT + ["z"] * 4 + ["q"] * 4 + ["k"] * 4 + ["v"] * NT
        by_dve = [k in ("q", "v") for k in kinds]
        N_V = sum(by_dve)
        N_A = PJ - N_V

        sems("m_small_loaded", "m_zeroed", "m_gates_done", "m_gates_read", "m_softplus", "m_lf_ready", "m_rows_turned", "m_rows_copied",
             "m_scanned", "m_rows_exp", "m_rows_stored", "m_cols_turned", "m_cols_copied",
             "m_pj_done", "m_rd_a", "m_rd_v", "m_tap0", "m_conved", "m_x_ready", "m_row_loaded", "m_masked", "m_w_ready",
             "m_s_done", "m_sw_ready", "m_num_done", "m_i_read", "m_r_ready", "m_t_ready", "m_h_ready",
             "m_var_ready", "m_sd_ready", "m_ln_ready", "m_kt_done", "m_kw_ready", "m_c_done", "m_c_copied_a",
             "m_c_copied_v", "m_c_stored_a", "m_c_stored_v", "m_n_done", "m_n_copied", "m_n_stored", "m_sk_ready",
             "m_h_turned", "m_a_ready", "m_y_ready")

        def pair(n):
            return ps[:, 2 * n:2 * n + 2, :].rearrange("p a b -> p (a b)")

        def ml_sync(sp):
            w = t["ml_w_in"][0].rearrange("(k p) n -> p k n", p=P)
            slot, free, _ = slabs.take()
            sp.wait_ge(w_used, free)
            sp.dma_start(ring[:, slot, 0:KD * 16].rearrange("p (k n) -> p k n", n=16),
                         w[:, :, 3 * INNER:3 * INNER + 16]).then_inc(w_loaded[slot], 16)
            with sp.Fori(0, ML_HEADS) as h:
                slabs.enter(h, [1, 1, 1, 2, 1, 2])
                for c in range(3):
                    slot, free, _ = slabs.take()
                    sp.wait_ge(w_used, free)
                    apart(sp)
                    sp.dma_start(ring[:, slot].rearrange("p (k n) -> p k n", n=DH),
                                 w[:, :, bass.ds(INNER * c + DH * h, DH)]).then_inc(w_loaded[slot], 16)
                for group in (("ml_w_q", "ml_w_k"), ("ml_w_v",), (0, 1)):
                    slot, free, _ = slabs.take(len(group))
                    sp.wait_ge(w_used, free)
                    apart(sp)
                    for c, name in enumerate(group):
                        src = t["state_mlstm_c"][0, 0, name] if isinstance(name, int) else t[name][0]
                        src = src[bass.ds(h, 1)].rearrange("a (k p) n -> p (a k) n", p=P)
                        sp.dma_start(ring[:, slot, 2048 * c:2048 * c + 2048].rearrange("p (k n) -> p k n", n=DH), src
                                     ).then_inc(w_loaded[slot], 16)
            slabs.leave(ML_HEADS)

        def ml_in_pe(pe):
            slot, _, full = slabs.take()
            w = ring[:, slot, 0:KD * 16].rearrange("p (k n) -> p k n", n=16)
            pe.wait_ge(w_loaded[slot], full)
            pe.wait_ge(h_ready, KD * 3)
            for tt in range(NT):
                for k in range(KD):
                    mm = pe.matmul(bank(6)[:, tt * 16:(tt + 1) * 16], hT[:, k, tt * P:(tt + 1) * P], w[:, k],
                                   start=(k == 0), stop=(k == KD - 1))
            slab_through(pe, mm, bank(6)[0:2, 510:512], S["m_gates_done"])
            pe.wait_ge(S["m_lf_ready"], 1)
            for q in range(4):
                src = m_gt if q < 2 else m_lf
                at = 8 * (q % 2) + (0 if q < 2 else 4)
                for tt in range(NT):
                    mm = pe.transpose(pair(q)[0:4, tt * P:(tt + 1) * P], src[:, tt, at:at + 4], ident[:])
            mm.then_inc(S["m_rows_turned"], 1)
            pe.wait_ge(S["m_rows_copied"], 4)
            pe.wait_ge(S["m_rows_exp"], 9)
            for tt in range(NT):
                for n, q in enumerate((R_G, R_GI, R_EN)):
                    for d in range(2):
                        at = 24 * tt + 8 * n + 4 * d
                        pe.transpose(bank(6)[:, at:at + 4], m_wide[0:4, q + d, tt * P:(tt + 1) * P], ident[0:4, 0:4])
            for d in range(2):
                mm = pe.transpose(bank(6)[:, 120 + 4 * d:124 + 4 * d], m_wide[0:4, R_WE + d, 0:P], ident[0:4, 0:4])
            mm.then_inc(S["m_cols_turned"], 1)
            fence(pe, "pe")

        def ml_in_dve(dve):
            fl = lambda a: a.rearrange("p a b -> p (a b)")
            dve.wait_ge(S["m_small_loaded"], 32)
            dve.wait_ge(S["m_zeroed"], 1)
            dve.wait_ge(S["m_gates_done"], 1)
            dve.tensor_tensor(m_gt, bank(6)[:, 0:80].rearrange("p (a b) -> p a b", b=16),
                              m_gb.unsqueeze(1).broadcast_to([P, NT, 16]), ALU.add).then_inc(S["m_gates_read"], 1)
            dve.wait_ge(S["m_softplus"], 3)
            dve.wait_ge(S["m_gates_read"], 1)
            dve.scalar_tensor_tensor(out=fl(m_lf), in0=fl(m_gt), scalar=0.0, in1=fl(m_lf), op0=ALU.min,
                                     op1=ALU.subtract).then_inc(S["m_lf_ready"], 1)
            dve.wait_ge(S["m_rows_copied"], 4)

            def run(a, d):
                return a if d == 0 else a[:, ::-1]

            last = {}
            for d in range(2):
                for s in range(2):
                    c = seg(s)
                    n = c.stop - c.start
                    lf, ig, bc, g, mx = (m_wide[0:4, q + d, c] for q in (R_LF, R_IG, R_BC, R_G, R_M))
                    dve_t.after(dve.tensor_tensor_scan(run(bc, d), run(lf, d), m_zero[:, 0:n], 0.0, ALU.add, ALU.add))
                    dve_t.after(dve.tensor_tensor(g, ig, bc, ALU.subtract))
                    dve_t.after(dve.tensor_tensor_scan(run(mx, d), run(g, d), run(g, d),
                                                       m_m0[0:4, d:d + 1] if s == 0 else 0.0, ALU.max, ALU.max))
                dve_t.mark(dve.scalar_tensor_tensor(out=m_wide[0:4, R_EN + d], in0=m_wide[0:4, R_BC + d], scalar=-1.0,
                                                    in1=m_wide[0:4, R_M + d], op0=ALU.mult, op1=ALU.subtract))
                e = TOK - 1 if d == 0 else LAT
                dve_t.mark(dve.tensor_tensor(m_new[0:4, d:d + 1], m_wide[0:4, R_BC + d, e:e + 1],
                                             m_wide[0:4, R_M + d, e:e + 1], ALU.add))
                dve.tensor_scalar(m_wide[0:4, R_WE + d, 0:P], m_wide[0:4, R_G + d, LAT:TOK],
                                  m_wide[0:4, R_M + d, e:e + 1], None, ALU.subtract).then_inc(S["m_scanned"], 1)
            fence(dve, "dve")

        def ml_in_act(act):
            act.wait_ge(S["m_gates_read"], 1)
            act.activation(m_lf, m_gt, ACT.Abs).then_inc(S["m_softplus"], 1)
            act.wait_ge(S["m_softplus"], 1)
            act.activation(m_lf, m_lf, ACT.Exp, scale=-1.0).then_inc(S["m_softplus"], 1)
            act.wait_ge(S["m_softplus"], 2)
            act.activation(m_lf, m_lf, ACT.Ln, bias=1.0).then_inc(S["m_softplus"], 1)
            act.wait_ge(S["m_rows_turned"], 1)
            for q in range(4):
                act.activation(m_wide[0:4, q], pair(q)[0:4, 0:TOK], ACT.Copy).then_inc(S["m_rows_copied"], 1)
            act.wait_ge(S["m_scanned"], 2)
            for d in range(2):
                act.activation(m_wide[0:4, R_GI + d, 0:LAT], m_wide[0:4, R_M + d, 0:LAT], ACT.Exp, scale=-1.0,
                               bias=m_m0[0:4, d:d + 1]).then_inc(S["m_rows_exp"], 1)
                act.activation(m_wide[0:4, R_GI + d, LAT:TOK], m_wide[0:4, R_M + d, LAT:TOK], ACT.Exp, scale=-1.0
                               ).then_inc(S["m_rows_exp"], 1)
                act.activation(m_wide[0:4, R_WE + d, 0:P], m_wide[0:4, R_WE + d, 0:P], ACT.Exp).then_inc(S["m_rows_exp"], 1)
            for d in range(2):
                act.activation(m_wide[0:4, R_EN + d], m_wide[0:4, R_EN + d], ACT.Exp).then_inc(S["m_rows_exp"], 1)
            act.activation(m_den[0:4, 0:1], m_new[0:4, 0:1], ACT.Copy).then_inc(S["m_rows_exp"], 1)
            act.wait_ge(S["m_cols_turned"], 1)
            act.activation(m_c, bank(6)[:, 0:P], ACT.Copy).then_inc(S["m_cols_copied"], 1)
            fence(act, "act")

        def ml_in_pool(pool):
            pool.memset(m_raw, 0.0).then_inc(S["m_zeroed"], 1)
            pool.dma_start(m_gb, t["ml_gate_b"].rearrange("a d g h -> a (d g h)").broadcast_to([P, 16])
                           ).then_inc(S["m_small_loaded"], 16)
            pool.dma_start(m_m0[0:4], t["state_mlstm_m"][0, 0].rearrange("d h -> h d"), allow_slow_non_contiguous=True).then_inc(S["m_small_loaded"], 16)
            pool.wait_ge(S["m_scanned"], 2)
            pool.dma_start(max_rows, m_wide[0:4, R_M:R_M + 2].rearrange("p a b -> p (a b)")
                           ).then_inc(S["m_rows_stored"], 16)
            pool.dma_start(out["new_mlstm_m"][0, 0].rearrange("d h -> h d"), m_new[0:4],
                           allow_slow_non_contiguous=True).then_inc(S["m_rows_stored"], 16)
            pool.wait_ge(S["m_rows_stored"], 32)
            fence(pool, "pool")

        def tokens(a, k, tt, lat, ctx_at):
            at = lat + tt * P if tt < LC else ctx_at
            return a[:, k, at:at + P]

        def ml_pe(pe):
            with pe.Fori(0, ML_HEADS) as h:
                slabs.enter(h, [1, 1, 1, 2, 1, 2])
                for n, kind in enumerate(kinds):
                    first = n == 0 or kinds[n - 1] != kind
                    if first and kind != "k":
                        slot, _, full = slabs.take(2 if kind == "q" else 1)
                        pe.wait_ge(w_loaded[slot], full)
                    kt = KD if kind in ("xm", "o", "z") else KH
                    at = 2048 if kind == "k" else 0
                    w = ring[:, slot, at:at + kt * DH].rearrange("p (k n) -> p k n", n=DH)
                    i = n - kinds.index(kind)
                    if n < 2:
                        pe.wait_ge(S["m_c_copied_a"], 4 * h + 4)
                        pe.wait_ge(S["m_c_copied_v"], 4 * h + 4)
                    elif by_dve[n - 2]:
                        pe.wait_ge(S["m_rd_v"], N_V * h + sum(by_dve[:n - 1]))
                    else:
                        pe.wait_ge(S["m_rd_a"], N_A * h + (n - 1) - sum(by_dve[:n - 1]))
                    if first and kind == "q":
                        pe.wait_ge(S["m_x_ready"], 4 * h + 4)
                    b = big(n % 2)
                    for k in range(kt):
                        st = dict(start=(k == 0), stop=(k == kt - 1))
                        if kind in ("xm", "z"):
                            pe.matmul(b[:, 0:512], w[:, k, i * P:(i + 1) * P], hT[:, k, 0:512], **st)
                            mm = pe.matmul(b[:, 512:TOK], w[:, k, i * P:(i + 1) * P], hT[:, k, 512:TOK], **st)
                        elif kind in ("q", "k"):
                            pe.matmul(b[:, 0:512], w[:, k, i * P:(i + 1) * P], m_xc[:, k, 0:LAT], **st)
                            mm = pe.matmul(b[:, 512:TOK], w[:, k, i * P:(i + 1) * P], m_xc[:, k, C_CTX:CONV], **st)
                        elif kind == "o":
                            mm = pe.matmul(b[:, 0:DH], hT[:, k, i * P:(i + 1) * P], w[:, k], **st)
                        else:
                            mm = pe.matmul(b[:, 0:DH], tokens(m_raw, k, i, RAW_LAT, RAW_CTX), w[:, k], **st)
                    if n == PJ - 1 or (kinds[n + 1] != kind and kind != "q"):
                        slab_through(pe, mm, last_cols(n % 2), S["m_pj_done"])
                    else:
                        mm.then_inc(S["m_pj_done"], 1)
                for j in range(NT):
                    if j == 0:
                        pe.wait_ge(S["m_rd_v"], N_V * h + 4)
                        pe.wait_ge(S["m_rd_a"], N_A * h + N_A)
                        pe.wait_ge(S["m_a_ready"], 4 * h + 4)
                    if j >= 2:
                        pe.wait_ge(S["m_sw_ready"], NT * h + j - 1)
                    n = LAT if j < LC else P
                    for k in range(KH):
                        mm = pe.matmul(bank(4 + j % 2)[:, 0:n], m_k[:, k, j * P:(j + 1) * P],
                                       m_q[:, k, 0:LAT] if j < LC else m_q[:, k, LAT:TOK],
                                       start=(k == 0), stop=(k == KH - 1))
                    mm.then_inc(S["m_s_done"], 1)
                pe.wait_ge(S["m_sw_ready"], NT * h + NT)
                pe.wait_ge(S["m_rd_v"], N_V * h + N_V)
                slot, _, full = slabs.take(2)
                c0 = ring[:, slot].rearrange("p (d k n) -> p d k n", d=2, k=KH)
                pe.wait_ge(w_loaded[slot], full)
                for i in range(NT):
                    if i:
                        pe.wait_ge(S["m_i_read"], NT * h + i)
                    sets = []
                    for d in range(2):
                        js = [LC] if i == LC else (range(0, i + 1) if d == 0 else range(i, LC))
                        for j in js:
                            if i == LC:
                                a = m_swc[:, d]
                            elif d == 0:
                                a = m_sw[:, j, (i - j) * P:(i - j + 1) * P]
                            else:
                                a = m_sw[:, j, LAT - j * P + i * P:LAT - j * P + (i + 1) * P]
                            sets.append((d, a, j, j == js[0], j == js[-1]))
                    for d, a, j, st, sp_ in sets:
                        pe.matmul(bank(6)[:, d:d + 1], a, ones[:, 0:1], start=st, stop=sp_)
                    if i < LC:
                        for k in range(KH):
                            n0 = cols[:, bass.ds(col("state_mlstm_n", k) + KH * h, 17)][:, ::16]
                            pe.matmul(bank(6)[:, 2:4], m_q[:, k, i * P:(i + 1) * P], n0,
                                      start=(k == 0), stop=(k == KH - 1))
                    for d, a, j, st, sp_ in sets:
                        mm = pe.matmul(bank(d), a, m_v[:, j], start=st, stop=sp_)
                    if i < LC:
                        for d in range(2):
                            for k in range(KH):
                                mm = pe.matmul(bank(2 + d), m_q[:, k, i * P:(i + 1) * P], c0[:, d, k],
                                               start=(k == 0), stop=(k == KH - 1))
                    if i == LC - 1:
                        slab_through(pe, mm, bank(6)[0:2, 510:512], S["m_num_done"])
                    else:
                        mm.then_inc(S["m_num_done"], 1)
                for k in range(KH):
                    mm = pe.transpose(bank(7)[:, k * P:(k + 1) * P], m_k[:, k, LAT:TOK], ident[:])
                mm.then_inc(S["m_kt_done"], 1)
                pe.wait_ge(S["m_i_read"], NT * h + NT)
                pe.wait_ge(S["m_kw_ready"], h + 1)
                for d in range(2):
                    mm = pe.matmul(bank(4 + d)[0:1, :], ones[:, 0:1], m_kw[:, d], start=True, stop=True)
                mm.then_inc(S["m_n_done"], 1)
                for n in range(8):
                    d, m = divmod(n, KH)
                    if n >= 4:
                        pe.wait_ge(S["m_c_copied_v" if n % 2 else "m_c_copied_a"], 4 * h + 4 + (n - 4) // 2 + 1)
                    pe.matmul(bank(n % 4), m_kw[:, d, m * P:(m + 1) * P], m_v[:, LC], start=True, stop=True
                              ).then_inc(S["m_c_done"], 1)
                pe.wait_ge(S["m_ln_ready"], h + 1)
                pe.wait_ge(S["m_n_copied"], h + 1)
                for m in range(KH):
                    if m >= 2:
                        pe.wait_ge(S["m_a_ready"], 4 * h + 4 + m - 1)
                    for tt in range(NT):
                        mm = pe.transpose(pair(2 + m % 2)[:, tt * P:(tt + 1) * P], m_hh[:, tt, m * P:(m + 1) * P], ident[:])
                    mm.then_inc(S["m_h_turned"], 1)
            slabs.leave(ML_HEADS)

        def ml_act(act):
            with act.Fori(0, ML_HEADS) as h:
                done = 0
                for n, kind in enumerate(kinds):
                    i = n - kinds.index(kind)
                    b = big(n % 2)
                    if by_dve[n]:
                        continue
                    act.wait_ge(S["m_pj_done"], PJ * h + n + 1)
                    done += 1
                    if kind == "xm":
                        if i == 0:
                            act.wait_ge(S["m_y_ready"], 4 * h + 4)
                        act.activation(m_raw[:, i, RAW_LAT:RAW_LAT + LAT], b[:, 0:LAT], ACT.Copy)
                        act.activation(m_raw[:, i, RAW_CTX:RAW_CTX + CTX], b[:, LAT:TOK], ACT.Copy
                                       ).then_inc(S["m_rd_a"], 1)
                        act.wait_ge(S["m_rd_a"], N_A * h + done)
                        act.activation(m_xc[:, i], m_raw[:, i, 0:CONV], ACT.Identity,
                                       bias=pcol(col("ml_conv_b") + KH * h + i), scale=pcol(col("ml_conv_w") + KH * h + i)
                                       ).then_inc(S["m_tap0"], 1)
                    elif kind == "o":
                        act.activation(m_hh[:, i], b[:, 0:DH], ACT.Sigmoid).then_inc(S["m_rd_a"], 1)
                    elif kind == "z":
                        act.activation(yT[:, bass.ds(KH * h + i, 1), :].rearrange("p a b -> p (a b)"), b[:, 0:TOK], ACT.Silu
                                       ).then_inc(S["m_rd_a"], 1)
                        act.wait_ge(S["m_conved"], 4 * h + i + 1)
                        act.activation(m_xc[:, i], m_xc[:, i], ACT.Silu).then_inc(S["m_x_ready"], 1)
                    else:
                        act.activation(m_k[:, i], b[:, 0:TOK], ACT.Copy, scale=DH ** -0.5).then_inc(S["m_rd_a"], 1)
                act.wait_ge(S["m_masked"], h + 1)
                for j in range(NT):
                    for d in range(2):
                        g = m_c[:, bass.ds(24 * j + 4 * d + h, 1)]
                        if j == LC:
                            parts = [(m_swc[:, d], m_diag[:, d, LAT:TOK])]
                        elif d == 0:
                            parts = [(m_sw[:, j, 0:P], m_diag[:, 0, j * P:(j + 1) * P]),
                                     (m_sw[:, j, P:LAT - j * P], m_row[:, 0, (j + 1) * P:LAT])]
                        else:
                            parts = [(m_sw[:, j, LAT - j * P:LAT], m_row[:, 1, 0:j * P]),
                                     (m_sw[:, j, LAT:TOK], m_diag[:, 1, j * P:(j + 1) * P])]
                        for dst, src in parts:
                            if dst.shape[1]:
                                ins = act.activation(dst, src, ACT.Exp, scale=-1.0, bias=g)
                    ins.then_inc(S["m_w_ready"], 1)
                for i in range(LC):
                    act.wait_ge(S["m_r_ready"], NT * h + i + 1)
                    if i:
                        act.wait_ge(S["m_h_ready"], NT * h + i)
                    for d in range(2):
                        ins = act.activation(m_t[:, d], bank(2 + d), ACT.Copy, scale=m_rg[:, i % 2, d:d + 1])
                    ins.then_inc(S["m_t_ready"], 1)
                for k in range(KH):
                    act.activation(m_xc[:, k], m_xc[:, k], ACT.Copy, scale=pcol(col("ml_skip") + KH * h + k)
                                   ).then_inc(S["m_sk_ready"], 1)
                act.wait_ge(S["m_kt_done"], h + 1)
                for d in range(2):
                    ins = act.activation(m_kw[:, d], bank(7), ACT.Copy, scale=m_c[:, bass.ds(120 + 4 * d + h, 1)])
                ins.then_inc(S["m_kw_ready"], 1)
                act.wait_ge(S["m_n_done"], h + 1)
                for d in range(2):
                    ins = act.activation(m_nst[:, d * DH:(d + 1) * DH], bank(4 + d)[0:1, :], ACT.Copy)
                ins.then_inc(S["m_n_copied"], 1)
                act.wait_ge(S["m_var_ready"], h + 1)
                act.activation(m_sd, m_sd, ACT.Sqrt).then_inc(S["m_sd_ready"], 1)
                for n in range(0, 8, 2):
                    act.wait_ge(S["m_c_done"], 8 * h + n + 1)
                    if n == 0:
                        act.wait_ge(S["m_h_ready"], NT * h + NT)
                    else:
                        act.wait_ge(S["m_c_stored_a"], 64 * h + 8 * n)
                    act.activation(m_cst[:, 0], bank(n % 4), ACT.Copy).then_inc(S["m_c_copied_a"], 1)

        def ml_dve(dve):
            with dve.Fori(0, ML_HEADS) as h:
                dve_t.enter(h, ML_DVE)
                for n in range(KH):
                    dve.wait_ge(S["m_tap0"], 4 * h + n + 1)
                    for k in range(1, CW):
                        ins = dve.scalar_tensor_tensor(out=m_xc[:, n], in0=m_raw[:, n, k:k + CONV],
                                                       scalar=pcol(col("ml_conv_w", KI * k) + KH * h + n),
                                                       in1=m_xc[:, n], op0=ALU.mult, op1=ALU.add)
                        if k < CW - 1:
                            dve_t.after(ins)
                        else:
                            ins.then_inc(S["m_conved"], 1)
                for n, kind in enumerate(kinds):
                    if not by_dve[n]:
                        continue
                    i = n - kinds.index(kind)
                    dve.wait_ge(S["m_pj_done"], PJ * h + n + 1)
                    if kind == "q":
                        ins = dve.tensor_copy(m_q[:, i], big(n % 2)[:, 0:TOK])
                    else:
                        ins = dve.tensor_copy(m_v[:, i], big(n % 2)[:, 0:DH])
                    ins.then_inc(S["m_rd_v"], 1)
                for j in range(NT):
                    dve.wait_ge(S["m_s_done"], NT * h + j + 1)
                    dve.wait_ge(S["m_w_ready"], NT * h + NT + j + 1)
                    s = bank(4 + j % 2)
                    for d in range(2):
                        if j == LC:
                            a, b = m_swc[:, d], s[:, 0:P]
                        elif d == 0:
                            a, b = m_sw[:, j, 0:LAT - j * P], s[:, j * P:LAT]
                        else:
                            a, b = m_sw[:, j, LAT - j * P:TOK], s[:, 0:(j + 1) * P]
                        ins = dve.tensor_tensor(a, a, b, ALU.mult)
                        if d == 0:
                            dve_t.mark(ins)
                    ins.then_inc(S["m_sw_ready"], 1)
                for i in range(NT):
                    dve.wait_ge(S["m_num_done"], NT * h + i + 1)
                    gi, en = (m_c[:, bass.ds(24 * i + at + h, 5)][:, ::4] for at in (8, 16))
                    den, r, rg = m_den[:, 4 * (i % 2):4 * (i % 2) + 2], m_r[:, i % 2], m_rg[:, i % 2]
                    if i < LC:
                        dve_t.after(dve.tensor_tensor(den, bank(6)[:, 2:4], gi, ALU.mult))
                        dve_t.after(dve.tensor_tensor(den, bank(6)[:, 0:2], den, ALU.add))
                    else:
                        dve_t.after(dve.tensor_copy(den, bank(6)[:, 0:2]))
                    dve_t.after(dve.scalar_tensor_tensor(out=den, in0=den, scalar=-1.0, in1=den, op0=ALU.mult,
                                                         op1=ALU.max))
                    dve_t.after(dve.tensor_tensor(den, den, en, ALU.max))
                    dve_t.after(dve.reciprocal(r, den))
                    if i < LC:
                        dve.tensor_tensor(rg, r, gi, ALU.mult).then_inc(S["m_r_ready"], 1)
                        dve.wait_ge(S["m_t_ready"], LC * h + i + 1)
                        for d in range(2):
                            ins = dve.scalar_tensor_tensor(out=m_t[:, d], in0=bank(d), scalar=r[:, d:d + 1],
                                                           in1=m_t[:, d], op0=ALU.mult, op1=ALU.add)
                            if d == 0:
                                dve_t.mark(ins)
                    else:
                        dve.tensor_tensor(rg, r, gi, ALU.mult).then_inc(S["m_r_ready"], 1)
                        dve.wait_ge(S["m_h_ready"], NT * h + i)
                        for d in range(2):
                            ins = dve.tensor_scalar(m_t[:, d], bank(d), r[:, d:d + 1], None, ALU.mult)
                            if d == 0:
                                dve_t.mark(ins)
                    ins.then_inc(S["m_i_read"], 1)
                for i in range(NT):
                    dve.wait_ge(S["m_h_ready"], NT * h + i + 1)
                    ins = dve.bn_stats(m_stat[:, i], m_hh[:, i])
                    if i < NT - 1:
                        dve_t.mark(ins)
                    else:
                        dve_t.after(ins)
                apart(dve)
                for i in range(NT):
                    ins = dve.bn_aggr(m_mv[:, i], m_stat[:, i])
                    if i < NT - 1:
                        dve_t.mark(ins)
                    else:
                        dve_t.after(ins)
                dve.tensor_scalar(m_sd, m_mv[:, :, 1], EPS, None, ALU.add).then_inc(S["m_var_ready"], 1)
                dve.wait_ge(S["m_sd_ready"], h + 1)
                dve_t.after(dve.reciprocal(m_sd, m_sd))
                for i in range(NT):
                    ins = dve.tensor_scalar(m_hh[:, i], m_hh[:, i], m_mv[:, i, 0:1], m_sd[:, i:i + 1], ALU.subtract,
                                            ALU.mult)
                    if i < NT - 1:
                        dve_t.mark(ins)
                ins.then_inc(S["m_ln_ready"], 1)
                for n in range(1, 8, 2):
                    dve.wait_ge(S["m_c_done"], 8 * h + n + 1)
                    if n > 1:
                        dve.wait_ge(S["m_c_stored_v"], 64 * h + 8 * (n - 1))
                    dve.tensor_copy(m_cst[:, 1], bank(n % 4)).then_inc(S["m_c_copied_v"], 1)
                for m in range(KH):
                    dve.wait_ge(S["m_h_turned"], 4 * h + m + 1)
                    dve.wait_ge(S["m_sk_ready"], 4 * h + m + 1)
                    for s, c in ((0, slice(0, LAT)), (1, slice(C_CTX, CONV))):
                        ins = dve.scalar_tensor_tensor(out=m_xc[:, m, c], in0=pair(2 + m % 2)[:, seg(s)],
                                                       scalar=pcol(col("ml_norm_g") + KH * h + m), in1=m_xc[:, m, c],
                                                       op0=ALU.mult, op1=ALU.add)
                        if s == 0:
                            dve_t.mark(ins)
                    ins.then_inc(S["m_a_ready"], 1)
            dve_t.leave(ML_HEADS)

        ML_DVE = 8 + 5 + 4 * 5 + 4 + 5 + 10 + 1 + 4 + 4

        def ml_pool(pool):
            ml_in_pool(pool)
            with pool.Fori(0, ML_HEADS) as h:
                pool_t.enter(h, 1 + NT + KH)
                pool.wait_ge(S["m_w_ready"], NT * h + NT)
                apart(pool)
                pool.dma_start(m_row.rearrange("p a b -> p (a b)"), max_rows[bass.ds(h, 1)].broadcast_to([P, 2 * TOK])
                               ).then_inc(S["m_row_loaded"], 16)
                pool.wait_ge(S["m_row_loaded"], 16 * h + 16)
                for d in range(2):
                    ins = pool.tensor_tensor(m_diag[:, d].rearrange("p (t i) -> p t i", i=P),
                                             m_row[:, d].rearrange("p (t i) -> p t i", i=P),
                                             neg[:, d].unsqueeze(1).broadcast_to([P, NT, P]), ALU.subtract)
                    if d == 0:
                        pool_t.mark(ins)
                ins.then_inc(S["m_masked"], 1)
                for i in range(NT):
                    pool.wait_ge(S["m_i_read"], NT * h + i + 1)
                    pool_t.after(pool.tensor_tensor(m_t[:, 0], m_t[:, 0], m_t[:, 1], ALU.add))
                    pool.tensor_tensor(m_hh[:, i], m_hh[:, i], m_t[:, 0], ALU.mult).then_inc(S["m_h_ready"], 1)
                pool.wait_ge(S["m_n_copied"], h + 1)
                apart(pool)
                for d in range(2):
                    pool.dma_start(out["new_mlstm_n"][0, 0, d, bass.ds(h, 1)], m_nst[:, d * DH:(d + 1) * DH]
                                   ).then_inc(S["m_n_stored"], 16)
                for n in range(8):
                    d, m = divmod(n, KH)
                    odd = n % 2
                    pool.wait_ge(S["m_c_copied_v" if odd else "m_c_copied_a"], 4 * h + 4 + n // 2 + 1)
                    apart(pool)
                    dst = out["new_mlstm_c"][0, 0, d, bass.ds(h, 1), m * P:(m + 1) * P].rearrange("a p n -> p (a n)")
                    pool.dma_start(dst, m_cst[:, odd]).then_inc(S["m_c_stored_v" if odd else "m_c_stored_a"], 16)
                for m in range(KH):
                    pool.wait_ge(S["m_a_ready"], 4 * h + 4 + m + 1)
                    apart(pool)
                    for s, c in ((0, slice(0, LAT)), (1, slice(C_CTX, CONV))):
                        y = yT[:, bass.ds(KH * h + m, 1), seg(s)].rearrange("p a b -> p (a b)")
                        ins = pool.tensor_tensor(y, y, m_xc[:, m, c], ALU.mult)
                        if s == 0:
                            pool_t.mark(ins)
                    ins.then_inc(S["m_y_ready"], 1)
                pool.wait_ge(S["m_n_stored"], 32 * h + 32)
                pool.wait_ge(S["m_c_stored_a"], 64 * h + 64)
                pool.wait_ge(S["m_c_stored_v"], 64 * h + 64)
            pool_t.leave(ML_HEADS)

        slabs = None
        act_t = dve_t = pool_t = None
        block = ctx.enter_context(nc.Block())

        @block.sync
        def _(sp):
            nonlocal slabs
            slabs = Slabs()
            setup_sync(sp)
            for l in range(layers):
                ada_sync(sp, l)
                if l % 3 == 0:
                    mla_sync(sp, l // 3)
                    out_sync(sp, t["mla_w_out"][l // 3], KD)
                elif l % 3 == 1:
                    ssd_sync(sp)
                    out_sync(sp, t["ssd_w_out"][0], KI)
                else:
                    ml_sync(sp)
                    out_sync(sp, t["ml_w_out"][0], KI)
            final_sync(sp)
            sp.wait_ge(stored, 16 * NT)

        @block.tensor
        def _(pe):
            nonlocal slabs
            slabs = Slabs()
            pe.sem_inc(w_used, 2)
            ssd_credits_pe(pe)
            setup_pe(pe)
            for l in range(layers):
                ada_pe(pe, l)
                fence(pe, "pe")
                norm_pe(pe, l)
                if l % 3 == 0:
                    mla_in_pe(pe, l // 3)
                    fence(pe, "pe")
                    mla_pe(pe, l // 3)
                    fence(pe, "pe")
                    out_pe(pe, l, KD)
                elif l % 3 == 1:
                    ssd_in_pe(pe)
                    ssd_pe(pe)
                    fence(pe, "pe")
                    out_pe(pe, l, KI)
                else:
                    ml_in_pe(pe)
                    ml_pe(pe)
                    fence(pe, "pe")
                    out_pe(pe, l, KI)
            fence(pe, "pe")
            norm_pe(pe, layers)
            final_pe(pe)

        @block.scalar
        def _(act):
            nonlocal act_t
            act_t = Tally(act, act_steps)
            setup_act_loads(act)
            mla_credits_act(act)
            ssd_credits_act(act)
            act.sem_inc(S["m_c_copied_a"], 4)
            act.sem_inc(S["m_w_ready"], NT)
            setup_act(act)
            for l in range(layers):
                fence(act, "act")
                norm_act(act, l)
                if l % 3 == 0:
                    mla_in_act(act, l // 3)
                    fence(act, "act")
                    mla_act(act, l // 3)
                elif l % 3 == 1:
                    ssd_in_act(act)
                    ssd_act(act)
                else:
                    ml_in_act(act)
                    ml_act(act)
                fence(act, "act")
            fence(act, "act")
            norm_act(act, layers)
            final_copy(act, 0)

        @block.vector
        def _(dve):
            nonlocal dve_t
            dve_t = Tally(dve, dve_steps)
            credits_dve(dve)
            ssd_credits_dve(dve)
            dve.sem_inc(S["m_c_copied_v"], 4)
            dve.sem_inc(S["m_a_ready"], 4)
            setup_dve(dve)
            for l in range(layers):
                ada_dve(dve, l)
                fence(dve, "dve")
                norm_dve(dve, l)
                if l % 3 == 0:
                    mla_in_dve(dve, l // 3)
                    fence(dve, "dve")
                    mla_dve(dve, l // 3)
                    fence(dve, "dve")
                    out_dve(dve, l, KD)
                elif l % 3 == 1:
                    ssd_in_dve(dve)
                    ssd_dve(dve)
                    fence(dve, "dve")
                    ssd_out_scale(dve)
                    out_dve(dve, l, KI, s_rstd, s_tmp)
                else:
                    ml_in_dve(dve)
                    ml_dve(dve)
                    fence(dve, "dve")
                    out_dve(dve, l, KI)
            fence(dve, "dve")
            norm_dve(dve, layers)
            final_copy(dve, 1)

        @block.gpsimd
        def _(pool):
            nonlocal pool_t
            pool_t = Tally(pool, pool_steps)
            pool.sem_inc(S["m_y_ready"], 4)
            setup_pool(pool)
            for l in range(layers):
                fence(pool, "pool")
                if l % 3 == 0:
                    mla_misc_loads(pool, l // 3)
                    mla_new_store(pool, l // 3)
                    fence(pool, "pool")
                    mla_pool(pool, l // 3)
                elif l % 3 == 1:
                    ssd_pool(pool)
                else:
                    ml_pool(pool)
                fence(pool, "pool")
            fence(pool, "pool")


_INS = ['x_prompt', 'x_sample', 'cache_mla_ckv', 'cache_mla_kpe', 'state_ssd', 'state_mlstm_c', 'state_mlstm_n',
        'state_mlstm_m', 'c', 'c_ctx', 'ada_w', 'ada_b', 'norm_g', 'final_norm_g', 'mla_w_in', 'mla_q_norm_g',
        'mla_kv_norm_g', 'mla_w_uq', 'mla_w_uk', 'mla_w_uv', 'mla_w_out', 'ssd_w_in', 'ssd_conv_w', 'ssd_conv_b',
        'ssd_dt_bias', 'ssd_a_log', 'ssd_d', 'ssd_norm_g', 'ssd_w_out', 'ml_w_in', 'ml_gate_b', 'ml_conv_w',
        'ml_conv_b', 'ml_w_q', 'ml_w_k', 'ml_w_v', 'ml_norm_g', 'ml_skip', 'ml_w_out']
_OUTS = [('y_prompt', (1, 128, 1024)), ('y_sample', (1, 512, 1024)), ('new_mla_ckv', (1, 2, 128, 256)),
         ('new_mla_kpe', (1, 2, 128, 32)), ('new_ssd', (1, 1, 2, 32, 64, 128)),
         ('new_mlstm_c', (1, 1, 2, 4, 512, 512)), ('new_mlstm_n', (1, 1, 2, 4, 512)), ('new_mlstm_m', (1, 1, 2, 4))]


def kernel(**inputs):
    import numpy as _np
    import concourse.bacc as _bacc
    from concourse import mybir as _mybir
    from concourse.bass_utils import run_bass_kernel_spmd as _run

    nc = _bacc.Bacc("TRN2", target_bir_lowering=False, num_devices=1)
    arrays, ins, outs = {}, {}, {}
    for name in _INS:
        a = _np.ascontiguousarray(inputs[name])
        arrays[f"in_{name}_dram"] = a
        ins[name] = nc.dram_tensor(f"in_{name}_dram", a.shape, _mybir.dt.from_np(a.dtype), kind="ExternalInput").ap()
    ins["rope"] = nc.inline_tensor(rope_table(), "rope_table").ap()
    for name, shape in _OUTS:
        outs[name] = nc.dram_tensor(f"out_{name}_dram", shape, _mybir.dt.float32, kind="ExternalOutput").ap()
    hybrid_flow_step(nc, ins, outs)
    r = _run(nc, [arrays], core_ids=[0])
    return tuple(r.results[0][f"out_{name}_dram"] for name, _ in _OUTS)
```

```python
from contextlib import ExitStack, nullcontext

import numpy as np

import concourse.bass as bass
from concourse import mybir

F32 = mybir.dt.float32
F32R = mybir.dt.float32r
ACT = mybir.ActivationFunctionType
ALU = mybir.AluOpType
X = mybir.AxisListType.X

P = 128
D_MODEL, DEPTH = 1024, 4
LAT, CTX, PAST = 512, 128, 128
TOK = LAT + CTX
NT = TOK // P
KD = D_MODEL // P
EPS = 1e-6
BIG = 1e30
SLAB = 2048
HALF = SLAB // 2
WHOLE, HALVES = (1, 0), (1, 1)
HEADS, NOPE, ROPE, VDIM = 16, 64, 32, 64
QK = NOPE + ROPE
Q_RANK, KV_RANK = 384, 256
RANK_TILES = (Q_RANK + KV_RANK) // P
MLA_SCALE = QK ** -0.5
PAIRS = HEADS // 2
KEYS = LAT + PAST + CTX
INNER = 2 * D_MODEL
KI = INNER // P
GROUPS, GH, HD, STATE = 8, 4, 64, 128
SH = GROUPS * GH
GX = GH * HD
CW = 4
ML_HEADS, DH = 4, 512
KH = DH // P
RAW = 648
RAW_LAT, RAW_CTX = 1, LAT + 4
CONV = LAT + 3 + CTX
C_CTX = LAT + 3

COL = {}


def _columns():
    at = 0
    for block in ((("ada_b", 96), ("norm_g", 32)),
                  (("c", 8), ("c_ctx", 8), ("final_norm_g", 8), ("mla_q_norm_g", 6), ("mla_kv_norm_g", 4),
                   ("ssd_conv_b", 32), ("ssd_norm_g", 16), ("ml_conv_b", 16), ("ml_norm_g", 16)),
                  (("ssd_conv_w", 128),),
                  (("ml_conv_w", 64), ("ml_skip", 16), ("state_mlstm_n", 32))):
        row = 0
        for name, n in block:
            COL[name] = (at, row, n)
            row += n
        at += P
    return at // P


PARAM_BLOCKS = _columns()


def col(name, k=0):
    block, row, _ = COL[name]
    return block + row + k


class Slabs:

    def __init__(self):
        self.n, self.got, self.parts = 0, [[0, 0], [0, 0]], 0
        self.i, self.dn, self.dgot, self.dparts = 0, 0, [[0, 0], [0, 0]], 0

    def enter(self, i, slabs):
        assert len(slabs) % 2 == 0
        self.i, self.dn = i, len(slabs)
        self.dgot, self.dparts = [[0, 0], [0, 0]], 0
        for k, d in enumerate(slabs):
            d = d or (0, 0)
            for h in range(2):
                self.dgot[(self.n + k) % 2][h] += 16 * d[h]
            self.dparts += 2 if d[1] else 0

    def leave(self, trips):
        self.n += self.dn * (trips - 1)
        self.parts += self.dparts * (trips - 1)
        for s in range(2):
            for h in range(2):
                self.got[s][h] += self.dgot[s][h] * (trips - 1)
        self.i, self.dn, self.dgot, self.dparts = 0, 0, [[0, 0], [0, 0]], 0

    def take(self, dmas=WHOLE):
        slot = self.n % 2
        free = self.n + 1 + self.dn * self.i
        self.n += 1
        d = dmas or (0, 0)
        full = []
        for h in range(2):
            self.got[slot][h] += 16 * d[h]
            full.append(self.got[slot][h] + self.dgot[slot][h] * self.i)
        split = [self.parts + h + 1 + self.dparts * self.i for h in range(2)]
        self.parts += 2 if d[1] else 0
        return slot, free, full, split


class Tally:

    def __init__(self, eng, sem):
        self.eng, self.sem, self.n, self.i, self.per = eng, sem, 0, 0, 0

    def enter(self, i, per):
        self.i, self.per, self.n0 = i, per, self.n

    def leave(self, trips):
        assert self.n - self.n0 == self.per, (self.n - self.n0, self.per)
        self.n += self.per * (trips - 1)
        self.i, self.per = 0, 0

    def mark(self, ins):
        ins.then_inc(self.sem, 1)
        self.n += 1
        return self.n + self.per * self.i

    def after(self, ins):
        self.eng.wait_ge(self.sem, self.mark(ins))


def rope_table():
    grid_w, half = 64, ROPE // 2
    pos = np.arange(LAT)
    inv = (1.0 / (np.float32(10000.0) ** (np.arange(0, half, 2, dtype=np.float32) / np.float32(half)))).astype(np.float32)
    ang = np.concatenate([(pos // grid_w).astype(np.float32)[:, None] * inv,
                          (pos % grid_w).astype(np.float32)[:, None] * inv], axis=-1)
    table = np.zeros((2 * ROPE, TOK), np.float32)
    table[0:ROPE] = 1.0
    cos, sin = np.cos(ang).T, np.sin(ang).T
    table[0:ROPE, 0:LAT] = np.concatenate([cos, cos])
    table[ROPE:, 0:LAT] = np.concatenate([-sin, sin])
    return table


def hybrid_flow_step(nc, t, out, layers=DEPTH):
    with ExitStack() as ctx:
        def sb(name, shape, dtype=F32):
            return ctx.enter_context(nc.sbuf_tensor(name, shape, dtype))

        def sem(name):
            return ctx.enter_context(nc.semaphore(name))

        def twice(name, name_r, shape):
            with nc.sbuf_tensor(name, shape, F32) as plain:
                pass
            return plain, ctx.enter_context(nc.sbuf_tensor(name_r, shape, F32R))

        xT, h_lo = twice("xT", "h_lo", [P, KD, TOK])
        hT, h_hi = twice("hT", "h_hi", [P, KD, TOK])
        ring, w_lo = twice("ring", "w_lo", [P, 2, SLAB])
        w_hi = sb("w_hi", [P, 2, SLAB], F32R)
        yT = sb("yT", [P, KI, TOK])
        ident, ones = sb("ident", [P, P]), sb("ones", [P, P])
        tri = sb("tri", [P, 2, P])
        neg = sb("neg", [P, 2, P])
        cols = sb("cols", [P, PARAM_BLOCKS * P])
        cond = sb("cond", [P, KD, 2])
        mod = sb("mod", [P, DEPTH, 24, 2])
        gain = sb("gain", [P, KD, 2])
        small = sb("small", [P, 64])
        ROOM = 53215 - (2 * KD * TOK + 4 * SLAB + KI * TOK + 6 * P + PARAM_BLOCKS * P + 16 + 48 * DEPTH + 16 + 64) - 64
        room, room_r = twice("room", "room_r", [P, ROOM])
        y_hi, y_lo = (room_r[:, n * KI * TOK:(n + 1) * KI * TOK].rearrange("p (k n) -> p k n", n=TOK)
                      for n in range(2))

        class Room:

            def __init__(self):
                self.at = 0

            def __call__(self, *shape):
                n = 1
                for s in shape:
                    n *= s
                a = room[:, self.at:self.at + n]
                self.at += n
                assert self.at <= ROOM, (self.at, ROOM)
                if len(shape) == 2:
                    a = a.rearrange("p (a b) -> p a b", b=shape[1])
                if len(shape) == 4:
                    a = a.rearrange("p (a b c d) -> p a b c d", b=shape[1], c=shape[2], d=shape[3])
                if len(shape) == 3:
                    a = a.rearrange("p (a b c) -> p a b c", b=shape[1], c=shape[2])
                return a

        ps = ctx.enter_context(nc.psum_tensor("ps", [P, 8, 512], F32))

        def big(n):
            n %= 3
            return ps[:, 2 * n:2 * n + 2, :].rearrange("p a b -> p (a b)")

        def wide(b):
            return b[:, 512 - TOK // 2:512 + TOK // 2]

        def bank(n):
            return ps[:, n, :]

        def slab_through(pe, product, own, done, empty=False):
            product.then_inc(w_used, 1)
            if empty:
                slabs.take(None)
                pe.matmul(own, cond[:, 0, :], cond[:, 0, :], start=True, stop=True).then_inc(w_used, 1)
            pe.matmul(own, cond[:, 0, :], cond[:, 0, :], start=True, stop=True).then_inc(done, 1)

        def last_cols(n):
            return big(n)[0:2, 1020:1022]

        def split3(pe, dst, a_hi, a_lo, b_hi, b_lo, start, stop):
            pe.matmul(dst, a_hi, b_hi, start=start, stop=False)
            pe.matmul(dst, a_hi, b_lo, start=False, stop=False)
            return pe.matmul(dst, a_lo, b_hi, start=False, stop=stop)

        def split3_tile(pe, b, hi, lo, x_hi, x_lo, start, stop):
            for c in (slice(0, TOK // 2), slice(TOK // 2, TOK)):
                mm = split3(pe, wide(b)[:, c], hi, lo, x_hi[:, c], x_lo[:, c], start, stop)
            return mm

        def split_slab(pool, dmas=HALVES, n=None):
            slot, _, full, _ = slabs.take(dmas)
            for h in range(2):
                split_half(pool, slot, full, h, n)

        def split_half(pool, slot, full, h, n=None):
            raw, hi, lo = (a[:, slot, h * HALF:(h + 1) * HALF] for a in (ring, w_hi, w_lo))
            if n is not None:
                raw, hi, lo = (a.rearrange("p (k n) -> p k n", n=2 * P)[:, :, 0:n] for a in (raw, hi, lo))
            one = ones[:, 0:1] if n is None else ones[:, 0:1].unsqueeze(2)
            pool.wait_ge(w_loaded[slot][h], full[h])
            pool_t.after(pool.tensor_tensor(hi, raw, one.broadcast_to(raw.shape), ALU.mult))
            pool.tensor_tensor(lo, raw, hi.bitcast(F32), ALU.subtract).then_inc(w_split, 1)

        def load_halves(sp, slot, v, src, kt):
            for h in range(2):
                k = slice(h * kt // 2, (h + 1) * kt // 2)
                sp.dma_start(v[:, k], src[:, k]).then_inc(w_loaded[slot][h], 16)

        def columns(a, slot, n):
            return a[:, slot].rearrange("p (k n) -> p k n", n=n)

        x_rows = nc.dram_tensor("x_rows", (P, KD * TOK), F32).ap()
        acs_rows = nc.dram_tensor("acs_rows", (2 * SH, TOK), F32).ap()
        max_rows = nc.dram_tensor("max_rows", (ML_HEADS, 2 * TOK), F32).ap()

        w_loaded = [[sem("w_loaded0a"), sem("w_loaded0b")], [sem("w_loaded1a"), sem("w_loaded1b")]]
        w_split = sem("w_split")
        x_moved = sem("x_moved")
        h_high = sem("h_high")
        y_high, y_split = sem("y_high"), sem("y_split")
        w_used = sem("w_used")
        stage_done = sem("stage_done")
        act_steps, dve_steps, pool_steps = sem("act_steps"), sem("dve_steps"), sem("pool_steps")
        masks_made = sem("masks_made")
        x_loaded, rows_loaded = sem("x_loaded"), sem("rows_loaded")
        stored = sem("stored")
        in_turned, in_copied, in_copied_v = sem("in_turned"), sem("in_copied"), sem("in_copied_v")
        cond_ready = sem("cond_ready")
        ada_done, ada_read = sem("ada_done"), sem("ada_read")
        squared, summed, sums_read, rooted = sem("squared"), sem("summed"), sem("sums_read"), sem("rooted")
        scaled, h_ready = sem("scaled"), sem("h_ready")
        out_done, out_read = sem("out_done"), sem("out_read")

        S = {}

        def sems(*names):
            for n in names:
                S[n] = sem(n)

        MASKS = 9
        passed = sem("passed")

        def apart(eng):
            eng.sem_inc(passed, 1)

        engines = 4
        fences = {}

        def fence(eng, name):
            fences[name] = fences.get(name, 0) + 1
            eng.drain().then_inc(stage_done, 1)
            eng.wait_ge(stage_done, engines * fences[name])

        def seg(s):
            return slice(0, LAT) if s == 0 else slice(LAT, TOK)

        def bcast(a, n):
            return a.unsqueeze(2).broadcast_to([a.shape[0], a.shape[1], n])

        def trips(eng, n):
            return eng.Fori(0, n) if n > 1 else nullcontext(0)

        x_in = yT[:, 0:KD, :].rearrange("p a b -> p (a b)").rearrange("p (t d) -> p t d", d=D_MODEL)
        rows_in = room[:, 0:PARAM_BLOCKS * P].rearrange("p (b c) -> p b c", c=P)
        param_dmas = len(COL)
        block_rows = [0] * PARAM_BLOCKS
        for at, row, n in COL.values():
            block_rows[at // P] = max(block_rows[at // P], row + n)

        def setup_sync(sp):
            sp.dma_start(x_in[:, 0:LAT // P, :], t["x_sample"][0].rearrange("(t p) d -> p t d", p=P)
                         ).then_inc(x_loaded, 16)
            sp.dma_start(x_in[:, LAT // P, :], t["x_prompt"][0]).then_inc(x_loaded, 16)

        def setup_act_loads(act):
            for name, (at, row, n) in COL.items():
                src = t[name]
                dims = "abcdef"[:len(src.shape)]
                flat = src.rearrange(f"{' '.join(dims)} -> ({' '.join(dims)})") if len(dims) > 1 else src
                act.dma_start(rows_in[row:row + n, at // P, :], flat.rearrange("(r c) -> r c", c=P)
                              ).then_inc(rows_loaded, 16)

        def setup_pool(pool):
            n = 0
            for a, v in ((ident[:], 0.0), (ones[:], 1.0), (tri[:], 1.0), (neg[:], 0.0)):
                pool.memset(a, v).then_inc(masks_made, 1)
                n += 1
            pool.wait_ge(masks_made, n)
            pool.affine_select(out=ident[:], in_=ident[:], compare_op=ALU.not_equal, fill=1.0, base=0,
                               pattern=[[-1, P]], channel_multiplier=1).then_inc(masks_made, 1)
            for d in range(2):
                s = 1 - 2 * d
                for m, fill in ((tri, 0.0), (neg, -BIG)):
                    pool.affine_select(out=m[:, d], in_=m[:, d], compare_op=ALU.is_ge, fill=fill, base=0,
                                       pattern=[[s, P]], channel_multiplier=-s).then_inc(masks_made, 1)

        def setup_pe(pe):
            pe.wait_ge(masks_made, MASKS)
            pe.wait_ge(rows_loaded, 16 * param_dmas)
            for b in range(PARAM_BLOCKS):
                n = block_rows[b]
                mm = pe.transpose(bank(6)[:, b * P:b * P + n], rows_in[0:n, b, :], ident[0:n, 0:n])
            mm.then_inc(in_turned, 1)
            pe.wait_ge(x_loaded, 32)
            for k in range(KD):
                if k >= 3:
                    pe.wait_ge(in_copied if k % 2 else in_copied_v, (k - 3) // 2 + 1)
                for tt in range(NT):
                    mm = pe.transpose(big(k)[:, tt * P:(tt + 1) * P], x_in[:, tt, k * P:(k + 1) * P], ident[:])
                mm.then_inc(in_turned, 1)

        def setup_act(act):
            act.wait_ge(in_turned, 1)
            for b in range(PARAM_BLOCKS):
                n = block_rows[b]
                ins = act.activation(cols[:, b * P:b * P + n], bank(6)[:, b * P:b * P + n], ACT.Copy)
                act_t.mark(ins)
            act.wait_ge(act_steps, act_t.n)
            act.activation(cond[:, :, 0], cols[:, col("c"):col("c") + KD], ACT.Silu).then_inc(cond_ready, 1)
            act.activation(cond[:, :, 1], cols[:, col("c_ctx"):col("c_ctx") + KD], ACT.Silu).then_inc(cond_ready, 1)
            for k in range(0, KD, 2):
                act.wait_ge(in_turned, k + 2)
                act.activation(xT[:, k], big(k)[:, 0:TOK], ACT.Copy).then_inc(in_copied, 1)

        def setup_dve(dve):
            for k in range(1, KD, 2):
                dve.wait_ge(in_turned, k + 2)
                dve.tensor_copy(xT[:, k], big(k)[:, 0:TOK]).then_inc(in_copied_v, 1)

        ADA = 3 * D_MODEL // (2 * P)
        ADA_AHEAD = 2

        def ada_sync(sp, l):
            w = t["ada_w"][l].rearrange("(k p) n -> p k n", p=P)
            with trips(sp, ADA // 2) as i:
                slabs.enter(i, [WHOLE, WHOLE])
                for u in range(2):
                    slot, free, _, _ = slabs.take()
                    sp.wait_ge(w_used, free)
                    sp.dma_start(columns(ring, slot, 2 * P), w[:, :, bass.ds((2 * i + u) * 2 * P, 2 * P)]
                                 ).then_inc(w_loaded[slot][0], 16)
            slabs.leave(ADA // 2)

        def ada_pe(pe, l):
            pe.wait_ge(cond_ready, 2)
            with trips(pe, ADA // 2) as i:
                slabs.enter(i, [WHOLE, WHOLE])
                for u in range(2):
                    slot, _, full, _ = slabs.take()
                    w = columns(ring, slot, 2 * P)
                    pe.wait_ge(w_loaded[slot][0], full[0])
                    pe.wait_ge(ada_read, ADA * l + 2 * i + u + 1)
                    for m in range(2):
                        for k in range(KD):
                            mm = pe.matmul(bank(6 + u)[:, 2 * m:2 * m + 2], w[:, k, m * P:(m + 1) * P], cond[:, k, :],
                                           start=(k == 0), stop=(k == KD - 1))
                    slab_through(pe, mm, bank(6 + u)[0:2, 8:10], ada_done)
            slabs.leave(ADA // 2)

        def ada_dve(dve, l):
            if l >= ADA_AHEAD:
                dve.wait_ge(ada_read, ADA * ADA_AHEAD + 2 + GROUPS)
                gain_dve(dve, l)
                return
            with trips(dve, ADA // 2) as i:
                for u in range(2):
                    s = 2 * i + u
                    dve.wait_ge(ada_done, ADA * l + s + 1)
                    b = cols[:, bass.ds(col("ada_b", 24 * l) + 2 * s, 2)]
                    dve.tensor_tensor(mod[:, l, bass.ds(2 * s, 2), :],
                                      bank(6 + u)[:, 0:4].rearrange("p (m c) -> p m c", c=2),
                                      bcast(b, 2), ALU.add).then_inc(ada_read, 1)
            dve.wait_ge(ada_read, ADA * (l + 1) + 2)
            gain_dve(dve, l)

        def gain_dve(dve, l):
            dve.scalar_tensor_tensor(out=gain[:], in0=mod[:, l, KD:2 * KD, :], scalar=1.0,
                                     in1=bcast(cols[:, col("norm_g", KD * l):col("norm_g", KD * l) + KD], 2),
                                     op0=ALU.add, op1=ALU.mult)

        n_sq, n_rstd, n_tmp = yT[:, 0:KD], yT[:, KD], yT[:, KD + 1]

        def norm_squares(act, l):
            if l == 0:
                act.wait_ge(in_copied, KD // 2)
                act.wait_ge(in_copied_v, KD // 2)
            else:
                act.wait_ge(y_split, y_before(l - 1) + (KD if (l - 1) % 3 == 0 else KI))
            for k in range(KD):
                if l:
                    act.wait_ge(out_read, 2 + KD * (l - 1) + k + 1)
                act.activation(n_sq[:, k], xT[:, k], ACT.Square).then_inc(squared, 1)
                if l < layers and k % (KD // 2) == KD // 2 - 1:
                    half = slice(k + 1 - KD // 2, k + 1)
                    act.dma_start(x_rows[:, half.start * TOK:half.stop * TOK],
                                  xT[:, half].rearrange("p a b -> p (a b)")).then_inc(x_moved, 16)

        def norm_act(act, l):
            act.wait_ge(sums_read, 2 * l + 1)
            act.activation(n_tmp, n_tmp, ACT.Sqrt).then_inc(rooted, 1)
            if l < layers:
                for k in range(KD):
                    act.wait_ge(scaled, KD * l + k + 1)
                    for s in range(2):
                        ins = act.activation(h_hi[:, k, seg(s)], xT[:, k, seg(s)], ACT.Identity, bias=mod[:, l, k, s:s + 1])
                    ins.then_inc(h_high, 1)

        def norm_pe(pe, l):
            for k in range(KD):
                pe.wait_ge(squared, KD * l + k + 1)
                pe.matmul(big(2)[:, 0:512], ones[:], n_sq[:, k, 0:512], start=(k == 0), stop=(k == KD - 1))
                pe.matmul(big(2)[:, 512:TOK], ones[:], n_sq[:, k, 512:TOK], start=(k == 0), stop=(k == KD - 1)
                          ).then_inc(summed, 1)

        def norm_dve(dve, l):
            dve.wait_ge(summed, KD * (l + 1))
            dve.tensor_scalar(n_tmp, big(2)[:, 0:TOK], 1.0 / D_MODEL, EPS, ALU.mult, ALU.add).then_inc(sums_read, 1)
            dve.wait_ge(rooted, l + 1)
            dve.reciprocal(n_rstd, n_tmp).then_inc(sums_read, 1)
            dve.wait_ge(sums_read, 2 * l + 2)
            if l < layers:
                dve.wait_ge(x_moved, 48 * l + 32)
                for k in range(KD + 1):
                    if k < KD:
                        for s in range(2):
                            ins = dve.scalar_tensor_tensor(out=xT[:, k, seg(s)], in0=xT[:, k, seg(s)],
                                                           scalar=gain[:, k, s:s + 1], in1=n_rstd[:, seg(s)],
                                                           op0=ALU.mult, op1=ALU.mult)
                        ins.then_inc(scaled, 1)
                    if k:
                        dve.wait_ge(h_high, KD * l + k)
                        for s in range(2):
                            ins = dve.scalar_tensor_tensor(out=h_lo[:, k - 1, seg(s)], in0=xT[:, k - 1, seg(s)],
                                                           scalar=mod[:, l, k - 1, s:s + 1],
                                                           in1=h_hi[:, k - 1, seg(s)].bitcast(F32),
                                                           op0=ALU.add, op1=ALU.subtract)
                        ins.then_inc(h_ready, 1)
            else:
                for k in range(KD):
                    dve.scalar_tensor_tensor(out=hT[:, k], in0=xT[:, k],
                                             scalar=cols[:, col("final_norm_g", k):col("final_norm_g", k) + 1],
                                             in1=n_rstd, op0=ALU.mult, op1=ALU.mult).then_inc(scaled, 1)

        def tiles_before(l):
            return sum((KD + RANK_TILES, KI, 2 * KI)[m % 3] for m in range(l))

        def y_before(l):
            return tiles_before(l) + (RANK_TILES, 0, KI)[l % 3]

        def out_sync(sp, w_out, kt):
            n = SLAB // kt
            w = w_out.rearrange("(k p) n -> p k n", p=P)
            tr = D_MODEL // n // 2
            with trips(sp, tr) as i:
                slabs.enter(i, [HALVES, HALVES])
                for u in range(2):
                    slot, free, _, _ = slabs.take(HALVES)
                    sp.wait_ge(w_used, free)
                    apart(sp)
                    load_halves(sp, slot, columns(ring, slot, n), w[:, :, bass.ds((2 * i + u) * n, n)], kt)
            slabs.leave(tr)

        def out_pool(pool, kt, done=0):
            tr = D_MODEL // (SLAB // kt) // 2
            if done:
                tr -= 1
            with trips(pool, tr) as i:
                slabs.enter(i, [HALVES, HALVES])
                pool_t.enter(i, 4)
                for u in range(2):
                    split_slab(pool)
            pool_t.leave(tr)
            slabs.leave(tr)

        def out_act(act, l, kt):
            act.dma_start(xT[:].rearrange("p a b -> p (a b)"), x_rows).then_inc(x_moved, 16)
            for k in range(kt):
                act.activation(y_hi[:, k], yT[:, k], ACT.Copy).then_inc(y_high, 1)

        def out_pe(pe, l, kt):
            n = SLAB // kt
            tr = D_MODEL // n // 2
            with trips(pe, tr) as i:
                slabs.enter(i, [HALVES, HALVES])
                for u in range(2):
                    slot, _, _, split = slabs.take(HALVES)
                    hi, lo = columns(w_hi, slot, n), columns(w_lo, slot, n)
                    for m in range(n // P):
                        at = u * (n // P) + m
                        c = slice(m * P, (m + 1) * P)
                        pe.wait_ge(out_read, KD * l + 2 * (n // P) * i + at + 1)
                        for k in range(kt):
                            if m == 0 and k % (kt // 2) == 0:
                                pe.wait_ge(w_split, split[k // (kt // 2)])
                            if at == 0:
                                pe.wait_ge(y_split, y_before(l) + k + 1)
                            st = dict(start=(k == 0), stop=(k == kt - 1))
                            mm = split3_tile(pe, big(at % 2), hi[:, k, c], lo[:, k, c], y_hi[:, k], y_lo[:, k], **st)
                        if m < n // P - 1:
                            mm.then_inc(out_done, 1)
                        else:
                            slab_through(pe, mm, last_cols(at % 2), out_done)
            slabs.leave(tr)

        def out_dve(dve, l, kt, rstd=None, tmp=None):
            for k in range(kt):
                dve.wait_ge(y_high, y_before(l) + k + 1)
                dve.tensor_tensor(y_lo[:, k], yT[:, k], y_hi[:, k].bitcast(F32), ALU.subtract).then_inc(y_split, 1)
            dve.wait_ge(x_moved, 48 * l + 48)
            n = SLAB // kt
            tr, per = D_MODEL // n // 2, 2 * (n // P)
            if rstd is not None:
                ssd_out_scale(dve)
            with trips(dve, tr) as i:
                if rstd is not None:
                    dve_t.enter(i, per)
                for at in range(per):
                    m = per * i + at
                    dve.wait_ge(out_done, KD * l + m + 1)
                    src = wide(big(at % 2))
                    if rstd is not None:
                        dve_t.after(dve.tensor_tensor(tmp[:, at % 2], src, rstd, ALU.mult))
                        src = tmp[:, at % 2]
                    for s in range(2):
                        xm = xT[:, bass.ds(m, 1), seg(s)].rearrange("p a b -> p (a b)")
                        g = mod[:, l, bass.ds(2 * KD + m, 1), s:s + 1].rearrange("p a b -> p (a b)")
                        ins = dve.scalar_tensor_tensor(out=xm, in0=src[:, seg(s)], scalar=g, in1=xm,
                                                       op0=ALU.mult, op1=ALU.add)
                    ins.then_inc(out_read, 1)
            if rstd is not None:
                dve_t.leave(tr)

        y_out = yT[:, 0:KD, :].rearrange("p a b -> p (a b)").rearrange("p (t d) -> p t d", d=D_MODEL)

        def final_pe(pe):
            pe.wait_ge(scaled, KD * (layers + 1))
            for tt in range(NT):
                if tt >= 3:
                    pe.wait_ge(S["y_copied_a"], tt - 2)
                    pe.wait_ge(S["y_copied_v"], tt - 2)
                for k in range(KD):
                    mm = pe.transpose(big(tt)[:, k * P:(k + 1) * P], hT[:, k, tt * P:(tt + 1) * P], ident[:])
                mm.then_inc(S["y_turned"], 1)

        def final_copy(eng, half):
            a = slice(half * 512, half * 512 + 512)
            for tt in range(NT):
                eng.wait_ge(S["y_turned"], tt + 1)
                if half:
                    eng.tensor_copy(y_out[:, tt, a], big(tt)[:, a]).then_inc(S["y_copied_v"], 1)
                else:
                    eng.activation(y_out[:, tt, a], big(tt)[:, a], ACT.Copy).then_inc(S["y_copied_a"], 1)

        def final_sync(sp):
            for tt in range(NT):
                sp.wait_ge(S["y_copied_a"], tt + 1)
                sp.wait_ge(S["y_copied_v"], tt + 1)
                dst = out["y_sample"][0, tt * P:(tt + 1) * P, :] if tt < LAT // P else out["y_prompt"][0]
                sp.dma_start(dst, y_out[:, tt]).then_inc(stored, 16)

        a_ = Room()
        QT, KT = Q_RANK // P, KV_RANK // P
        cq_lo = room_r[:, 0:QT * TOK].rearrange("p (k n) -> p k n", n=TOK)
        cq, keyc = a_(QT, TOK), a_(KT, KEYS)
        cq_hi = room_r[:, a_.at:a_.at + QT * TOK].rearrange("p (k n) -> p k n", n=TOK)
        a_(QT, TOK)
        keyc_hi, keyc_lo = (room_r[:, a_.at + n * KT * KEYS:a_.at + (n + 1) * KT * KEYS
                                   ].rearrange("p (k n) -> p k n", n=KEYS) for n in range(2))
        a_(2 * KT, KEYS)
        q_h, k_h = a_(2, TOK), a_(2, KEYS)
        v_h = a_(KEYS // P, P)
        prob = a_(2, 4 * (LAT + PAST) + P)
        probT = a_(5 * LAT + P)
        rope_tab, rope_tmps = a_(TOK), a_(2, TOK)
        rope_tmp = rope_tmps[:, 0]
        nmax, rsum, rinv = a_(16), a_(16), a_(16)
        kpe = prob[:, 0, 0:TOK]
        ckv_raw = prob[:, 0, TOK:3 * TOK].rearrange("p (a b) -> p a b", b=TOK)
        m_sq = probT[:, 0:3 * TOK].rearrange("p (a b) -> p a b", b=TOK)
        kv_sq = prob[:, 1, 0:2 * TOK].rearrange("p (a b) -> p a b", b=TOK)
        cache_in = q_h[:, 0, 0:KV_RANK + ROPE]
        new_rows = a_(KV_RANK + ROPE)
        q_rstd, kv_rstd = q_h[:, 1], probT[:, 3 * TOK:4 * TOK]
        IN_TILES = 14
        PAIR_DMAS = (10, 1)
        MLA_IN, KEY_SLAB = 7, 2

        sems("lat_done", "lat_read", "cache_loaded", "cache_turned", "rank_squared", "rank_summed",
             "rank_rooted", "rank_ready", "new_turned", "new_copied", "new_stored",
             "q_done", "k_done", "v_done", "q_copied", "q_turned", "k_copied", "v_copied",
             "score_done", "max_done", "exp_done", "sum_done", "prob_ready",
             "probT_done", "probT_a", "probT_v", "attn_done", "attn_read",
             "y_turned", "y_copied_a", "y_copied_v")

        def mla_misc_loads(pool, r):
            pool.dma_start(rope_tab[2 * ROPE:4 * ROPE], t["rope"]).then_inc(S["cache_loaded"], 16)
            pool.dma_start(cache_in[:, 0:KV_RANK], t["cache_mla_ckv"][0, r]).then_inc(S["cache_loaded"], 16)
            pool.dma_start(cache_in[:, KV_RANK:], t["cache_mla_kpe"][0, r]).then_inc(S["cache_loaded"], 16)

        def mla_sync(sp, r):
            w = t["mla_w_in"][r].rearrange("(k p) n -> p k n", p=P)
            for s in range(MLA_IN):
                dmas = (7, 7) if s == KEY_SLAB else HALVES
                slot, free, _, _ = slabs.take(dmas)
                sp.wait_ge(w_used, free)
                v = columns(ring, slot, 2 * P)
                if s != KEY_SLAB:
                    at = 2 * P * s if s < KEY_SLAB else Q_RANK + KV_RANK + ROPE + 2 * P * (s - KEY_SLAB - 1)
                    load_halves(sp, slot, v, w[:, :, at:at + 2 * P], KD)
                    continue
                for h in range(2):
                    k = slice(4 * h, 4 * h + 4)
                    sp.dma_start(v[:, k, 0:P], w[:, k, 512:640]).then_inc(w_loaded[slot][h], 16)
                    for c in range(2):
                        for at, src, n in ((0, 640, 32), (32, 656, 16), (48, 640, 16)):
                            at += P + 64 * c
                            sp.dma_start(v[:, k, at:at + n], w[:, k, src:src + n]).then_inc(w_loaded[slot][h], 16)
            wq = t["mla_w_uq"][r].rearrange("(k p) h d -> p k h d", p=P)
            wk = t["mla_w_uk"][r].rearrange("(k p) h d -> p k (h d)", p=P)
            wv = t["mla_w_uv"][r].rearrange("(k p) h d -> p k (h d)", p=P)
            with sp.Fori(0, PAIRS // 2) as i:
                slabs.enter(i, [PAIR_DMAS, PAIR_DMAS])
                for u in range(2):
                    slot, free, _, _ = slabs.take(PAIR_DMAS)
                    q, k, v = pair_weights(slot)
                    sp.wait_ge(w_used, free)
                    for c in range(3):
                        h = bass.ds(4 * i + 2 * u, 2)
                        for at, src, n in ((0, 0, QK), (QK, QK - 16, 16), (QK + 16, NOPE, 16)):
                            sp.dma_start(q[:, c, :, at:at + n], wq[:, c, h, src:src + n]).then_inc(w_loaded[slot][0], 16)
                    for half, (dst, src) in enumerate(((k, wk), (v, wv))):
                        sp.dma_start(dst, src[:, :, bass.ds((2 * i + u) * P, P)]).then_inc(w_loaded[slot][half], 16)
            slabs.leave(PAIRS // 2)

        def pair_weights(slot, a=None):
            a = ring if a is None else a
            q = a[:, slot, 0:768].rearrange("p (k h d) -> p k h d", k=3, h=2)
            k = a[:, slot, 768:1024].rearrange("p (k n) -> p k n", k=2)
            v = a[:, slot, 1024:1280].rearrange("p (k n) -> p k n", k=2)
            return q, k, v

        def mla_in_pe(pe, r):
            n = 0
            for s in range(MLA_IN):
                slot, _, _, split = slabs.take((7, 7) if s == KEY_SLAB else HALVES)
                hi, lo = columns(w_hi, slot, 2 * P), columns(w_lo, slot, 2 * P)
                for m in range(2):
                    c = slice(m * P, (m + 1) * P)
                    if n >= 3:
                        pe.wait_ge(S["lat_read"], IN_TILES * r + n - 2)
                    for k in range(KD):
                        if m == 0 and k % 4 == 0:
                            pe.wait_ge(w_split, split[k // 4])
                        if n == 0:
                            pe.wait_ge(h_ready, KD * 3 * r + k + 1)
                        st = dict(start=(k == 0), stop=(k == KD - 1))
                        mm = split3_tile(pe, big(n), hi[:, k, c], lo[:, k, c], h_hi[:, k], h_lo[:, k], **st)
                    if m:
                        slab_through(pe, mm, last_cols(n), S["lat_done"])
                    else:
                        mm.then_inc(S["lat_done"], 1)
                    n += 1
            pe.wait_ge(S["cache_loaded"], 48 * (r + 1))
            for c in range(2):
                pe.transpose(bank(6)[:, c * P:(c + 1) * P], cache_in[:, c * P:(c + 1) * P], ident[:])
            pe.transpose(bank(6)[0:ROPE, 2 * P:3 * P], cache_in[:, KV_RANK:], ident[:]).then_inc(S["cache_turned"], 1)
            pe.wait_ge(S["lat_read"], IN_TILES * (r + 1))
            pe.wait_ge(S["rank_squared"], RANK_TILES * (r + 1))
            for b, sq, tiles in ((0, m_sq, 3), (1, kv_sq, 2)):
                for k in range(tiles):
                    pe.matmul(big(b)[:, 0:512], ones[:], sq[:, k, 0:512], start=(k == 0), stop=(k == tiles - 1))
                    mm = pe.matmul(big(b)[:, 512:TOK], ones[:], sq[:, k, 512:TOK], start=(k == 0), stop=(k == tiles - 1))
                mm.then_inc(S["rank_summed"], 1)
            pe.wait_ge(S["rank_ready"], RANK_TILES * (r + 1))
            for c in range(2):
                pe.transpose(bank(7)[:, c * P:(c + 1) * P], keyc[:, c, LAT + PAST:], ident[:])
            pe.transpose(bank(7)[:, KV_RANK:KV_RANK + ROPE], kpe[0:ROPE, LAT:TOK], ident[0:ROPE, 0:ROPE]
                         ).then_inc(S["new_turned"], 1)

        def mla_in_act(act, r):
            for n in range(IN_TILES):
                act.wait_ge(S["lat_done"], IN_TILES * r + n + 1)
                dst, f = ((cq[:, n], ACT.Copy) if n < 3 else (ckv_raw[:, n - 3], ACT.Copy) if n < 5 else
                          (kpe, ACT.Copy) if n == 5 else (yT[:, n - 6], ACT.Silu))
                act.activation(dst, wide(big(n)), f).then_inc(S["lat_read"], 1)
            act.wait_ge(S["cache_turned"], r + 1)
            act_t.mark(act.activation(keyc[:, :, LAT:LAT + PAST], bank(6)[:, 0:2 * P].rearrange("p (a b) -> p a b", b=P),
                                      ACT.Copy))
            cached = act_t.n
            for h in range(2):
                act.activation(k_h[NOPE:QK, h, LAT:LAT + PAST], bank(6)[0:ROPE, 2 * P:3 * P], ACT.Copy)
            act.wait_ge(S["rank_summed"], 2 * r + 2)
            act.wait_ge(S["rank_rooted"], 4 * r + 2)
            for n, a in enumerate((q_rstd, kv_rstd)):
                act.activation(a, a, ACT.Sqrt).then_inc(S["rank_rooted"], 1)
            act.wait_ge(act_steps, cached)
            for n in range(RANK_TILES):
                act.wait_ge(S["rank_ready"], RANK_TILES * r + n + 1)
                x, hi = (cq[:, n], cq_hi[:, n]) if n < QT else (keyc[:, n - QT], keyc_hi[:, n - QT])
                act.activation(hi, x, ACT.Copy).then_inc(y_high, 1)
            act.wait_ge(S["new_turned"], r + 1)
            act.activation(new_rows, bank(7)[:, 0:KV_RANK + ROPE], ACT.Copy).then_inc(S["new_copied"], 1)

        def mla_in_dve(dve, r):
            for n in range(RANK_TILES):
                dve.wait_ge(S["lat_read"], IN_TILES * r + n + 1)
                src, dst = (cq[:, n], m_sq[:, n]) if n < 3 else (ckv_raw[:, n - 3], kv_sq[:, n - 3])
                dve.tensor_tensor(dst, src, src, ALU.mult).then_inc(S["rank_squared"], 1)
            dve.wait_ge(S["lat_read"], IN_TILES * r + 6)
            dve.wait_ge(S["cache_loaded"], 48 * (r + 1))
            rot = slice(NOPE, QK)
            dve_t.mark(dve.tensor_tensor(k_h[rot, 0, 0:LAT], kpe[rot, 0:LAT], rope_tab[rot, 0:LAT], ALU.mult))
            dve_t.after(dve.tensor_tensor(rope_tmp[rot, 0:LAT], kpe[QK:P, 0:LAT], rope_tab[QK:P, 0:LAT], ALU.mult))
            dve_t.after(dve.tensor_tensor(k_h[rot, 0, 0:LAT], k_h[rot, 0, 0:LAT], rope_tmp[rot, 0:LAT], ALU.add))
            dve.tensor_copy(k_h[rot, 1, 0:LAT], k_h[rot, 0, 0:LAT])
            for h in range(2):
                dve.tensor_copy(k_h[rot, h, LAT + PAST:], kpe[rot, LAT:TOK])
            dve.wait_ge(S["rank_summed"], 2 * r + 2)
            for b, a, n in ((0, q_rstd, Q_RANK), (1, kv_rstd, KV_RANK)):
                dve.tensor_scalar(a, big(b)[:, 0:TOK], 1.0 / n, EPS, ALU.mult, ALU.add).then_inc(S["rank_rooted"], 1)
            dve.wait_ge(S["rank_rooted"], 4 * r + 4)
            dve_t.mark(dve.reciprocal(q_rstd, q_rstd))
            dve_t.after(dve.reciprocal(kv_rstd, kv_rstd))
            dve_t.after(dve.tensor_scalar(q_rstd, q_rstd, MLA_SCALE, None, ALU.mult))
            for c in range(3):
                g = col("mla_q_norm_g", 3 * r + c)
                dve.scalar_tensor_tensor(out=cq[:, c], in0=cq[:, c], scalar=cols[:, g:g + 1], in1=q_rstd,
                                         op0=ALU.mult, op1=ALU.mult).then_inc(S["rank_ready"], 1)
            for c in range(2):
                g = col("mla_kv_norm_g", 2 * r + c)
                for src, dst in ((slice(0, LAT), slice(0, LAT)), (slice(LAT, TOK), slice(LAT + PAST, KEYS))):
                    ins = dve.scalar_tensor_tensor(out=keyc[:, c, dst], in0=ckv_raw[:, c, src],
                                                   scalar=cols[:, g:g + 1], in1=kv_rstd[:, src],
                                                   op0=ALU.mult, op1=ALU.mult)
                ins.then_inc(S["rank_ready"], 1)
            for n in range(RANK_TILES):
                dve.wait_ge(y_high, tiles_before(3 * r) + n + 1)
                x, hi, lo = ((cq[:, n], cq_hi[:, n], cq_lo[:, n]) if n < QT else
                             (keyc[:, n - QT], keyc_hi[:, n - QT], keyc_lo[:, n - QT]))
                dve.tensor_tensor(lo, x, hi.bitcast(F32), ALU.subtract).then_inc(y_split, 1)

        def mla_splits(pool):
            for s in range(MLA_IN):
                split_slab(pool, (7, 7) if s == KEY_SLAB else HALVES)

        def mla_new_store(pool, r):
            pool.wait_ge(S["new_copied"], r + 1)
            pool.dma_start(out["new_mla_ckv"][0, r], new_rows[:, 0:KV_RANK]).then_inc(S["new_stored"], 16)
            pool.dma_start(out["new_mla_kpe"][0, r], new_rows[:, KV_RANK:]).then_inc(S["new_stored"], 16)

        NS = 10

        def prob_tile(n):
            h, c = divmod(n, 5)
            return prob[:, h, 640 * c:640 * c + 640] if c < 4 else prob[:, h, 2560:2560 + P]

        def key_cols(b):
            return b[:, 512 - KEYS // 2:512 + KEYS // 2]

        def mla_pe(pe, r):
            with pe.Fori(0, PAIRS // 2) as i:
                slabs.enter(i, [PAIR_DMAS, PAIR_DMAS])
                for u in range(2):
                    p = PAIRS * r + u + 2 * i
                    slot, _, full, split = slabs.take(PAIR_DMAS)
                    _, _, wv = pair_weights(slot)
                    q_hi, k_hi, _ = pair_weights(slot, w_hi)
                    q_lo, k_lo, _ = pair_weights(slot, w_lo)
                    pe.wait_ge(w_split, split[0])
                    pe.wait_ge(S["exp_done"], NS * p + 10)
                    for h in range(2):
                        for k in range(QT):
                            mm = split3_tile(pe, big(h), q_hi[:, k, h], q_lo[:, k, h], cq_hi[:, k], cq_lo[:, k],
                                             start=(k == 0), stop=(k == QT - 1))
                        mm.then_inc(S["q_done"], 1)
                    pe.wait_ge(w_split, split[1])
                    pe.wait_ge(S["attn_read"], p + 1)
                    for k in range(KT):
                        for c in (slice(0, KEYS // 2), slice(KEYS // 2, KEYS)):
                            mm = split3(pe, key_cols(big(2))[:, c], k_hi[:, k], k_lo[:, k], keyc_hi[:, k, c],
                                        keyc_lo[:, k, c], start=(k == 0), stop=(k == KT - 1))
                    mm.then_inc(S["k_done"], 1)
                    pe.wait_ge(w_loaded[slot][1], full[1])
                    pe.wait_ge(S["q_copied"], 2 * p + 1)
                    pe.wait_ge(S["q_turned"], 2 * p + 1)
                    for kt in range(KEYS // P):
                        for k in range(2):
                            mm = pe.matmul(big(3)[:, kt * P:(kt + 1) * P], keyc[:, k, kt * P:(kt + 1) * P], wv[:, k],
                                           start=(k == 0), stop=(k == 1))
                    slab_through(pe, mm, last_cols(3), S["v_done"])
                    for n in range(NS):
                        h, c = divmod(n, 5)
                        b = big(4 + n)
                        if c == 0:
                            pe.wait_ge(S["q_copied"], 2 * p + h + 1)
                            pe.wait_ge(S["q_turned"], 2 * p + h + 1)
                            pe.wait_ge(S["k_copied"], 2 * p + h + 1)
                        if n == 0:
                            pe.wait_ge(S["q_copied"], 2 * p + 2)
                            pe.wait_ge(S["q_turned"], 2 * p + 2)
                        if n == 1:
                            pe.wait_ge(S["k_copied"], 2 * p + 2)
                        if n == 2:
                            pe.wait_ge(S["v_copied"], p + 1)
                        if n >= 3:
                            pe.wait_ge(S["exp_done"], NS * p + NS + n - 2)
                        if c < 4:
                            q = q_h[0:QK, h, c * P:(c + 1) * P]
                            pe.matmul(b[:, 0:512], q, k_h[0:QK, h, 0:512], start=True, stop=True)
                            pe.matmul(b[:, 512:640], q, k_h[0:QK, h, 512:640], start=True, stop=True
                                      ).then_inc(S["score_done"], 1)
                        else:
                            pe.matmul(b[:, 0:P], q_h[0:QK, h, LAT:TOK], k_h[0:QK, h, LAT + PAST:KEYS],
                                      start=True, stop=True).then_inc(S["score_done"], 1)
                    for h in range(2):
                        at = slice(VDIM * h, VDIM * h + VDIM)
                        for kt in range(6):
                            pe.wait_ge(S["probT_a" if kt % 2 else "probT_v"], 6 * p + 3 * h + kt // 2 + 3)
                            if kt < 5:
                                for c in range(4):
                                    if kt == 0:
                                        pe.wait_ge(S["prob_ready"], NS * p + 5 * h + c + 1)
                                    mm = pe.transpose(bank(6 + kt % 2)[:, c * P:(c + 1) * P],
                                                      prob_tile(5 * h + c)[:, kt * P:(kt + 1) * P], ident[:])
                            else:
                                pe.wait_ge(S["prob_ready"], NS * p + 5 * h + 5)
                                mm = pe.transpose(bank(7)[:, 0:P], prob_tile(5 * h + 4), ident[:])
                            mm.then_inc(S["probT_done"], 1)
                        for kt in range(5):
                            pe.wait_ge(S["probT_a" if kt % 2 else "probT_v"], 6 * p + 3 * h + kt // 2 + 4)
                            pe.matmul(big(2)[at, 0:512], v_h[:, kt, at], probT[:, kt * LAT:(kt + 1) * LAT],
                                      start=(kt == 0), stop=(kt == 4))
                        pe.wait_ge(S["probT_a"], 6 * p + 3 * h + 6)
                        mm = pe.matmul(big(2)[at, 512:TOK], v_h[:, 5, at], probT[:, 5 * LAT:], start=True, stop=True)
                    mm.then_inc(S["attn_done"], 1)
            slabs.leave(PAIRS // 2)

        def mla_act(act, r):
            with act.Fori(0, PAIRS // 2) as i:
                for u in range(2):
                    p = PAIRS * r + u + 2 * i
                    for h in range(2):
                        act.wait_ge(S["q_done"], 2 * p + h + 1)
                        act.activation(q_h[0:NOPE, h], wide(big(h))[0:NOPE], ACT.Copy).then_inc(S["q_copied"], 1)
                    act.wait_ge(S["k_done"], p + 1)
                    for h in range(2):
                        act.activation(k_h[0:NOPE, h], key_cols(big(2))[NOPE * h:NOPE * h + NOPE], ACT.Copy
                                       ).then_inc(S["k_copied"], 1)
                    act.wait_ge(S["v_done"], p + 1)
                    act.activation(v_h, big(3)[:, 0:KEYS].rearrange("p (a b) -> p a b", b=P), ACT.Copy
                                   ).then_inc(S["v_copied"], 1)
                    for n in range(NS):
                        act.wait_ge(S["max_done"], NS * p + n + 1)
                        a = prob_tile(n)
                        act.activation(a, big(4 + n)[:, 0:a.shape[1]], ACT.Exp, bias=nmax[:, n:n + 1],
                                       accum_out=rsum[:, n:n + 1]).then_inc(S["exp_done"], 1)
                    for h in range(2):
                        for kt in (1, 3, 5):
                            act.wait_ge(S["probT_done"], 12 * p + 6 * h + kt + 1)
                            n = LAT if kt < 5 else P
                            act.activation(probT[:, kt * LAT:kt * LAT + n], bank(7)[:, 0:n], ACT.Copy
                                           ).then_inc(S["probT_a"], 1)

        def mla_dve(dve, r):
            rot = slice(NOPE, QK)
            with dve.Fori(0, PAIRS // 2) as i:
                dve_t.enter(i, 8)
                for u in range(2):
                    p = PAIRS * r + u + 2 * i
                    for h in range(2):
                        dve.wait_ge(S["q_done"], 2 * p + h + 1)
                        dve_t.mark(dve.tensor_tensor(q_h[rot, h], wide(big(h))[rot], rope_tab[rot], ALU.mult))
                        dve_t.after(dve.tensor_tensor(rope_tmps[rot, h], wide(big(h))[QK:P], rope_tab[QK:P], ALU.mult))
                        dve.tensor_tensor(q_h[rot, h], q_h[rot, h], rope_tmps[rot, h], ALU.add).then_inc(S["q_turned"], 1)
                    for n in range(NS + 1):
                        if n < NS:
                            dve.wait_ge(S["score_done"], NS * p + n + 1)
                            w = prob_tile(n).shape[1]
                            dve.tensor_reduce(nmax[:, n:n + 1], big(4 + n)[:, 0:w], X, ALU.max, negate=True
                                              ).then_inc(S["max_done"], 1)
                        if n:
                            dve.wait_ge(S["exp_done"], NS * p + NS + n)
                            dve.reciprocal(rinv[:, n - 1:n], rsum[:, n - 1:n]).then_inc(S["sum_done"], 1)
                    for h in range(2):
                        for kt in (0, 2, 4):
                            dve.wait_ge(S["probT_done"], 12 * p + 6 * h + kt + 1)
                            dve.tensor_copy(probT[:, kt * LAT:(kt + 1) * LAT], bank(6)).then_inc(S["probT_v"], 1)
                    dve.wait_ge(S["attn_done"], p + 1)
                    y = yT[:, bass.ds(2 * i + u, 1), :].rearrange("p a b -> p (a b)")
                    dve.tensor_tensor(y, big(2)[:, 0:TOK], y, ALU.mult).then_inc(S["attn_read"], 1)
            dve_t.leave(PAIRS // 2)

        def split_pair(pool):
            slot, _, full, _ = slabs.take(PAIR_DMAS)
            pool.wait_ge(w_loaded[slot][0], full[0])
            for part in (slice(0, 768), slice(768, HALF)):
                raw, hi, lo = (a[:, slot, part] for a in (ring, w_hi, w_lo))
                pool_t.after(pool.tensor_tensor(hi, raw, ones[:, 0:1].broadcast_to(raw.shape), ALU.mult))
                pool.tensor_tensor(lo, raw, hi.bitcast(F32), ALU.subtract).then_inc(w_split, 1)

        def mla_pool(pool, r):
            with pool.Fori(0, PAIRS // 2) as i:
                slabs.enter(i, [PAIR_DMAS, PAIR_DMAS])
                pool_t.enter(i, 4)
                for u in range(2):
                    split_pair(pool)
                    p = PAIRS * r + u + 2 * i
                    for n in range(NS):
                        pool.wait_ge(S["sum_done"], NS * p + n + 1)
                        a = prob_tile(n)
                        pool.tensor_tensor(a, a, rinv[:, n:n + 1].broadcast_to([P, a.shape[1]]), ALU.mult).then_inc(S["prob_ready"], 1)
            pool_t.leave(PAIRS // 2)
            slabs.leave(PAIRS // 2)
            pool.wait_ge(S["new_stored"], 32 * (r + 1))

        def mla_credits_act(act):
            act.sem_inc(S["exp_done"], NS)
            act.sem_inc(S["probT_a"], 3)

        def credits_dve(dve):
            dve.sem_inc(S["probT_v"], 3)
            dve.sem_inc(S["attn_read"], 1)
            dve.sem_inc(ada_read, 2)
            dve.sem_inc(out_read, 2)

        LC = LAT // P
        b_ = Room()
        s_dt, s_nacs, s_eacs = b_(NT, 2 * SH), b_(NT, 2 * SH), b_(NT, 2 * SH)
        s_etot, s_wend = b_(NT, 2 * SH), b_(NT, 2 * SH)
        s_a, s_bias, s_d = b_(2 * SH), b_(2 * SH), b_(SH)
        s_ssq, s_one = b_(NT, GROUPS), b_(NT)
        s_raw, s_xc = b_(4, RAW), b_(4, CONV)
        s_xb = b_(NT, 3 * P)
        s_xe, s_xd = b_(NT, 2, GX), b_(2, 2, GX)
        s_m = b_(3, 8, P)
        s_h = b_(LC, 2, GX)
        s_y, s_t = b_(NT, GX), b_(2, 2 * GX)
        s_cb, s_in, s_fin = b_(TOK), b_(4, P), b_(4, P)
        s_z = room[:, ROOM - NT * GX:].rearrange("p (a b) -> p a b", b=GX)
        assert b_.at <= ROOM - NT * GX
        s_rstd, s_tmp = room[:, ROOM - TOK:], room[:, 2 * KI * TOK:2 * (KI + 1) * TOK].rearrange("p (a b) -> p a b", b=TOK)
        s_t2 = s_in.rearrange("p (a b) n -> p a (b n)", a=2)
        s_dump = s_z
        s_dtmp = s_m[:, 0].rearrange("p a b -> p (a b)")
        s_dA = s_m[:, 1].rearrange("p a b -> p (a b)")[:, 0:NT * 2 * SH].rearrange("p (a b) -> p a b", b=2 * SH)
        s_rows = s_h.rearrange("p a b c -> p (a b c)")[0:SH, 0:2 * TOK].rearrange("p (d n) -> p d n", d=2)
        s_v, s_e = s_dtmp[:, 0:320], s_dtmp[:, 320:640]

        sems("s_small_loaded", "s_dt_summed", "s_v_ready", "s_abs", "s_dA_ready", "s_acs_done", "s_acs_read",
             "s_rows_copied", "s_rows_stored", "s_cols_ready", "s_cols_exp", "s_zeroed",
             "s_pj_done", "s_pj_read", "s_tap0", "s_conved", "s_x_ready", "s_state_loaded", "s_state_turned",
             "s_state_copied", "s_in_turned", "s_in_copied", "s_cb_done", "s_cb_copied", "s_xe_ready", "s_upd_done",
             "s_h_ready", "s_fin_done", "s_fin_copied", "s_fin_stored", "s_xd_ready", "s_m_ready",
             "s_y_done", "s_y_read", "s_y_ready", "s_y_squared", "s_y_turned", "s_y_copied",
             "s_rows_loaded0", "s_rows_loaded1", "s_rows_loaded2", "s_masked", "s_decayed", "s_rms_done", "s_rms_diag",
             "s_rms_root")

        GROUP_SLABS = [HALVES, HALVES, HALVES, WHOLE, (2, 0), WHOLE]
        ADA_TILES = 24 // GROUPS

        def ssd_sync(sp):
            w = t["ssd_w_in"][0].rearrange("(k p) n -> p k n", p=P)
            slot, free, _, _ = slabs.take(HALVES)
            sp.wait_ge(w_used, free)
            load_halves(sp, slot, columns(ring, slot, 2 * P)[:, :, 0:2 * SH], w[:, :, 3 * INNER:3 * INNER + 2 * SH], KD)
            with sp.Fori(0, GROUPS) as g:
                slabs.enter(g, GROUP_SLABS)
                slot, free, _, _ = slabs.take(HALVES)
                sp.wait_ge(w_used, free)
                apart(sp)
                load_halves(sp, slot, columns(ring, slot, 2 * P), w[:, :, bass.ds(INNER + GX * g, GX)], KD)
                slot, free, _, _ = slabs.take(HALVES)
                sp.wait_ge(w_used, free)
                apart(sp)
                for c in range(2):
                    sp.dma_start(ring[:, slot, c * HALF:(c + 1) * HALF].rearrange("p (k n) -> p k n", n=P),
                                 w[:, :, bass.ds(2 * INNER + c * GROUPS * STATE + P * g, P)]
                                 ).then_inc(w_loaded[slot][c], 16)
                slot, free, _, _ = slabs.take(HALVES)
                sp.wait_ge(w_used, free)
                apart(sp)
                load_halves(sp, slot, columns(ring, slot, 2 * P), w[:, :, bass.ds(GX * g, GX)], KD)
                wa = [t["ada_w"][l].rearrange("(k p) n -> p k n", p=P) for l in (2, 3)]
                first, rest = bass.ds(ADA_TILES * P * g, 2 * P), bass.ds(ADA_TILES * P * g + 2 * P, P)
                for parts in (((0, first, 0, 2),), ((0, rest, 0, 1), (1, rest, 1, 1)), ((1, first, 0, 2),)):
                    slot, free, _, _ = slabs.take((len(parts), 0))
                    sp.wait_ge(w_used, free)
                    apart(sp)
                    for l, c, m, n in parts:
                        sp.dma_start(columns(ring, slot, 2 * P)[:, :, m * P:(m + n) * P], wa[l][:, :, c]
                                     ).then_inc(w_loaded[slot][0], 16)
            slabs.leave(GROUPS)

        def ssd_in_pe(pe):
            slot, _, _, split = slabs.take(HALVES)
            hi, lo = columns(w_hi, slot, 2 * P), columns(w_lo, slot, 2 * P)
            pe.wait_ge(w_split, split[1])
            for tt in range(NT):
                c = slice(tt * P, (tt + 1) * P)
                for k in range(KD):
                    if tt == 0:
                        pe.wait_ge(h_ready, KD * 1 + k + 1)
                    mm = split3(pe, bank(6)[:, tt * 64:(tt + 1) * 64], h_hi[:, k, c], h_lo[:, k, c],
                                hi[:, k, 0:2 * SH], lo[:, k, 0:2 * SH], start=(k == 0), stop=(k == KD - 1))
            slab_through(pe, mm, bank(6)[0:2, 510:512], S["s_dt_summed"])
            pe.wait_ge(S["s_dA_ready"], 1)
            for tt in range(NT):
                for d in range(2):
                    pe.matmul(bank(7)[:, tt * 64 + d * SH:tt * 64 + d * SH + SH], tri[:, d],
                              s_dA[:, tt, d * SH:(d + 1) * SH], start=True, stop=True)
            for d in range(2):
                for tt in range(NT):
                    pe.matmul(big(d)[0:SH, tt * P:(tt + 1) * P], s_dA[:, tt, d * SH:(d + 1) * SH], tri[:, d],
                              start=True, stop=True)
            pe.matmul(bank(6)[:, 0:320], ones[:], s_dA.rearrange("p a b -> p (a b)"), start=True, stop=True
                      ).then_inc(S["s_acs_done"], 1)
            pe.wait_ge(S["s_rows_copied"], 2)
            pe.wait_ge(S["s_acs_read"], 1)

        def ssd_in_dve(dve):
            dve.wait_ge(S["s_small_loaded"], 48)
            dve.wait_ge(S["s_dt_summed"], 1)
            bias = s_bias.unsqueeze(1).broadcast_to([P, NT, 2 * SH])
            dve.tensor_tensor(s_v.rearrange("p (a b) -> p a b", b=64),
                              bank(6)[:, 0:320].rearrange("p (a b) -> p a b", b=64), bias, ALU.add
                              ).then_inc(S["s_v_ready"], 1)
            dve.wait_ge(S["s_abs"], 4)
            dt2 = s_dt.rearrange("p a b -> p (a b)")
            dve_t.after(dve.scalar_tensor_tensor(out=dt2, in0=s_v, scalar=0.0, in1=s_e, op0=ALU.max, op1=ALU.add))
            dve.scalar_tensor_tensor(out=s_dA, in0=s_dt, scalar=-1.0, in1=s_a.unsqueeze(1).broadcast_to([P, NT, 2 * SH]),
                                     op0=ALU.mult, op1=ALU.mult).then_inc(S["s_dA_ready"], 1)
            dve.wait_ge(S["s_acs_done"], 1)
            acs, tot = bank(7)[:, 0:320], bank(6)[:, 0:320]
            fl = lambda a: a.rearrange("p a b -> p (a b)")
            dve_t.mark(dve.tensor_scalar(fl(s_nacs), acs, -1.0, None, ALU.mult))
            dve_t.after(dve.tensor_copy(fl(s_etot), tot))
            dve.tensor_tensor(fl(s_wend), fl(s_etot), fl(s_nacs), ALU.add).then_inc(S["s_acs_read"], 1)
            dve.wait_ge(S["s_cols_exp"], 3)
            dve.tensor_tensor(fl(s_wend), fl(s_wend), fl(s_dt), ALU.mult).then_inc(S["s_cols_ready"], 1)
            dve.wait_ge(S["s_cols_ready"], 1)

        def ssd_in_act(act):
            act.wait_ge(S["s_zeroed"], 1)
            act.wait_ge(S["s_small_loaded"], 48)
            act.activation(s_a, s_a, ACT.Exp).then_inc(S["s_abs"], 1)
            act.wait_ge(S["s_v_ready"], 1)
            act.activation(s_e, s_v, ACT.Abs).then_inc(S["s_abs"], 1)
            act.wait_ge(S["s_abs"], 2)
            act.activation(s_e, s_e, ACT.Exp, scale=-1.0).then_inc(S["s_abs"], 1)
            act.wait_ge(S["s_abs"], 3)
            act.activation(s_e, s_e, ACT.Ln, bias=1.0).then_inc(S["s_abs"], 1)
            act.wait_ge(S["s_acs_done"], 1)
            for d in range(2):
                act.activation(s_rows[:, d], big(d)[0:SH, 0:TOK], ACT.Copy).then_inc(S["s_rows_copied"], 1)
            act.wait_ge(S["s_acs_read"], 1)
            act.activation(s_eacs, s_nacs, ACT.Exp, scale=-1.0).then_inc(S["s_cols_exp"], 1)
            act.activation(s_etot, s_etot, ACT.Exp).then_inc(S["s_cols_exp"], 1)
            act.activation(s_wend, s_wend, ACT.Exp).then_inc(S["s_cols_exp"], 1)

        def conv_tile(n, g):
            return 2 * g + n if n < 2 else (16 + g if n == 2 else 24 + g)

        def pcol(c):
            return cols[:, bass.ds(c, 1)]

        def y_banks(tt):
            return (bank(0), bank(1)) if tt % 2 else (bank(6), bank(7))

        def xc_tile(n, tt):
            at = tt * P if tt < LC else C_CTX
            return s_xc[:, n, at:at + P]

        def ssd_pe(pe):
            with pe.Fori(0, GROUPS) as g:
                slabs.enter(g, GROUP_SLABS)
                for n in range(9):
                    first = n in (0, 2, 4)
                    if first:
                        slot, _, _, split = slabs.take(HALVES)
                        hi, lo = columns(w_hi, slot, 2 * P), columns(w_lo, slot, 2 * P)
                    if n in (2, 3):
                        first = True
                        hi, lo = (a[:, slot, (n - 2) * HALF:(n - 1) * HALF].rearrange("p (k n) -> p k n", n=P)
                                  for a in (w_hi, w_lo))
                    pe.wait_ge(S["s_pj_read"], 9 * g + 9 + max(n - 1, 0))
                    if n == 1:
                        pe.wait_ge(ada_read, ADA * ADA_AHEAD + 2 + g)
                    b = big(n % 2)
                    for k in range(KD):
                        if first and k % 4 == 0:
                            pe.wait_ge(w_split, split[n - 2 if n in (2, 3) else k // 4])
                        st = dict(start=(k == 0), stop=(k == KD - 1))
                        if n < 4:
                            c = slice(n * P, (n + 1) * P) if n < 2 else slice(0, P)
                            mm = split3_tile(pe, b, hi[:, k, c], lo[:, k, c], h_hi[:, k], h_lo[:, k], **st)
                        else:
                            c = slice((n - 4) * P, (n - 3) * P)
                            mm = split3(pe, b[:, 0:GX], h_hi[:, k, c], h_lo[:, k, c], hi[:, k], lo[:, k], **st)
                    if n in (1, 3, 8):
                        slab_through(pe, mm, big(n % 2)[0:2, 1020:1022] if n < 4 else b[0:2, 510:512], S["s_pj_done"])
                    else:
                        mm.then_inc(S["s_pj_done"], 1)
                pe.wait_ge(S["s_state_loaded"], 32 * g + 32)
                pe.wait_ge(S["s_y_copied"], 2 * g + 2)
                for c in range(4):
                    mm = pe.transpose(bank(5)[:, c * P:(c + 1) * P], s_in[:, c], ident[:])
                mm.then_inc(S["s_state_turned"], 1)
                pe.wait_ge(S["s_x_ready"], 4 * g + 4)
                for tt in range(NT):
                    if tt == 1:
                        pe.wait_ge(S["s_state_copied"], g + 1)
                    if tt >= 2:
                        pe.wait_ge(S["s_in_copied"], NT * g + tt - 1)
                    for n in range(3):
                        mm = pe.transpose(bank(4 + tt % 2)[:, n * P:(n + 1) * P], xc_tile(n, tt), ident[:])
                    mm.then_inc(S["s_in_turned"], 1)
                pe.wait_ge(S["s_y_read"], NT * g + NT)
                for tt in range(NT):
                    b = bank(6)[:, tt * P:(tt + 1) * P] if tt < LC else bank(7)[:, 0:P]
                    mm = pe.matmul(b, xc_tile(2, tt), xc_tile(3, tt), start=True, stop=True)
                mm.then_inc(S["s_cb_done"], 1)
                pe.wait_ge(S["s_in_copied"], NT * g + NT)
                pe.wait_ge(S["s_xe_ready"], NT * g + NT)
                for s in range(LC - 1):
                    if s == 2:
                        pe.wait_ge(S["s_h_ready"], 3 * g + 1)
                    for d, tt in ((0, s), (1, LC - 1 - s)):
                        mm = pe.matmul(bank(4 + s % 2)[:, d * GX:(d + 1) * GX], s_xb[:, tt, 2 * P:], s_xe[:, tt, d],
                                       start=True, stop=True)
                    mm.then_inc(S["s_upd_done"], 1)
                pe.wait_ge(S["s_h_ready"], 3 * g + 2)
                for d in range(2):
                    for c in range(2):
                        mm = pe.matmul(bank(5)[:, (2 * d + c) * P:(2 * d + c + 1) * P], s_xe[:, LC, d, c * P:(c + 1) * P],
                                       s_xb[:, LC, 2 * P:], start=True, stop=True)
                mm.then_inc(S["s_fin_done"], 1)
                ada_slab = None

                def ada_tile(n):
                    nonlocal ada_slab
                    if n % 2 == 0:
                        slot, _, full, _ = slabs.take(GROUP_SLABS[3 + n // 2])
                        ada_slab = columns(ring, slot, 2 * P)
                        pe.wait_ge(w_loaded[slot][0], full[0])
                    at = 2 * (0, 1, 2, 5, 3, 4)[n]
                    for k in range(KD):
                        mm = pe.matmul(bank(2)[:, at:at + 2], ada_slab[:, k, n % 2 * P:(n % 2 + 1) * P], cond[:, k, :],
                                       start=(k == 0), stop=(k == KD - 1))
                    if n % 2:
                        slab_through(pe, mm, bank(2)[0:2, 510:512], ada_done)

                ada_tile(0)
                pe.wait_ge(S["s_cb_copied"], g + 1)
                for tt in range(NT):
                    pe.wait_ge(S["s_xd_ready"], NT * g + tt + 1)
                    pe.wait_ge(S["s_m_ready"], NT * g + tt + 1)
                    if tt >= 2:
                        pe.wait_ge(S["s_y_read"], NT * g + tt - 1 + NT)
                    inner, outer = y_banks(tt)
                    for h in range(GH):
                        for d in range(2):
                            mm = pe.matmul(inner[:, h * HD:(h + 1) * HD], s_m[:, tt % 3, d * GH + h],
                                           s_xd[:, tt % 2, d, h * HD:(h + 1) * HD], start=(d == 0), stop=(d == 1))
                    if tt < LC:
                        if tt == 0:
                            pe.wait_ge(S["s_h_ready"], 3 * g + 3)
                        mm = pe.matmul(outer, xc_tile(3, tt), s_h[:, tt].rearrange("p a b -> p (a b)"),
                                       start=True, stop=True)
                    mm.then_inc(S["s_y_done"], 1)
                    ada_tile(tt + 1)
                for c in range(2):
                    if c == 0:
                        pe.wait_ge(S["s_y_ready"], NT * g + NT)
                        pe.wait_ge(S["s_fin_copied"], g + 1)
                    else:
                        pe.wait_ge(S["s_y_copied"], 2 * g + 3)
                    for tt in range(NT):
                        mm = pe.transpose(big(2)[:, tt * P:(tt + 1) * P], s_y[:, tt, c * P:(c + 1) * P], ident[:])
                    mm.then_inc(S["s_y_turned"], 1)
            slabs.leave(GROUPS)
            pe.wait_ge(S["s_rms_diag"], 1)
            for tt in range(NT):
                mm = pe.matmul(big(0)[:, tt * P:(tt + 1) * P], ones[:], s_m[:, 0:2].rearrange("p a b c -> p (a b) c")[:, tt],
                               start=True, stop=True)
            mm.then_inc(S["s_rms_done"], 1)

        def ssd_act(act):
            def exps(g, tt):
                act.wait_ge(S["s_masked"], NT * g + tt + 1)
                for c in range(8):
                    d, h = divmod(c, GH)
                    nac = s_nacs[:, tt, bass.ds(d * SH + GH * g + h, 1)]
                    ins = act.activation(s_m[:, tt % 3, c], s_m[:, tt % 3, c], ACT.Exp, bias=nac)
                ins.then_inc(S["s_decayed"], 1)

            with act.Fori(0, GROUPS) as g:
                act_t.enter(g, 4)
                for n in range(9):
                    act.wait_ge(S["s_pj_done"], 9 * g + n + 1)
                    if n < 4:
                        if n == 0:
                            act.wait_ge(S["s_conved"], 4 * g + 4)
                            act.wait_ge(S["s_y_done"], NT * g + NT)
                        b = wide(big(n % 2))
                        act_t.mark(act.activation(s_raw[:, n, RAW_LAT:RAW_LAT + LAT], b[:, 0:LAT], ACT.Copy))
                        act.activation(s_raw[:, n, RAW_CTX:RAW_CTX + CTX], b[:, LAT:TOK], ACT.Copy
                                       ).then_inc(S["s_pj_read"], 1)
                        act.wait_ge(S["s_pj_read"], 9 * g + 9 + n + 1)
                        act.activation(s_xc[:, n], s_raw[:, n, 0:CONV], ACT.Identity,
                                       bias=pcol(col("ssd_conv_b") + conv_tile(n, g)),
                                       scale=pcol(col("ssd_conv_w") + conv_tile(n, g))).then_inc(S["s_tap0"], 1)
                    else:
                        act.activation(s_z[:, n - 4], big(n % 2)[:, 0:GX], ACT.Silu).then_inc(S["s_pj_read"], 1)
                        if n < 8:
                            act.wait_ge(S["s_conved"], 4 * g + 4 + n - 3)
                            act.activation(s_xc[:, n - 4], s_xc[:, n - 4], ACT.Silu).then_inc(S["s_x_ready"], 1)
                act.wait_ge(S["s_state_turned"], g + 1)
                act.activation(s_h[:, 0, 0], bank(5)[:, 0:GX], ACT.Copy)
                act.activation(s_h[:, LC - 1, 1], bank(5)[:, GX:2 * GX], ACT.Copy).then_inc(S["s_state_copied"], 1)
                for tt in range(NT):
                    act.wait_ge(S["s_in_turned"], NT * g + tt + 1)
                    act.activation(s_xb[:, tt], bank(4 + tt % 2)[:, 0:3 * P], ACT.Copy).then_inc(S["s_in_copied"], 1)
                act.wait_ge(S["s_cb_done"], g + 1)
                act.activation(s_cb[:, 0:LAT], bank(6), ACT.Copy)
                act.activation(s_cb[:, LAT:TOK], bank(7)[:, 0:P], ACT.Copy).then_inc(S["s_cb_copied"], 1)
                for tt in range(3):
                    exps(g, tt)
                act.wait_ge(S["s_fin_done"], g + 1)
                act.activation(s_fin, bank(5).rearrange("p (a b) -> p a b", b=P), ACT.Copy).then_inc(S["s_fin_copied"], 1)
                for tt in range(3, NT):
                    exps(g, tt)
                for tt in range(NT):
                    act.wait_ge(S["s_y_ready"], NT * g + tt + 1)
                    act.activation(s_dump[:, tt], s_y[:, tt], ACT.Square,
                                   accum_out=s_ssq[:, tt, bass.ds(g, 1)]).then_inc(S["s_y_squared"], 1)
                for c in range(2):
                    act.wait_ge(S["s_y_turned"], 2 * g + c + 1)
                    act.activation(yT[:, bass.ds(2 * g + c, 1), :].rearrange("p a b -> p (a b)"), big(2)[:, 0:TOK],
                                   ACT.Copy, scale=pcol(col("ssd_norm_g") + 2 * g + c)).then_inc(S["s_y_copied"], 1)
            act_t.leave(GROUPS)
            act.wait_ge(S["s_rms_root"], 1)
            act.activation(s_rstd, s_rstd, ACT.Sqrt).then_inc(S["s_rms_root"], 1)

        def ssd_dve(dve):
            with dve.Fori(0, GROUPS) as g:
                dve_t.enter(g, 26)
                for n in range(4):
                    dve.wait_ge(S["s_tap0"], 4 * g + n + 1)
                    for k in range(1, CW):
                        ins = dve.scalar_tensor_tensor(out=s_xc[:, n], in0=s_raw[:, n, k:k + CONV],
                                                       scalar=pcol(col("ssd_conv_w", 32 * k) + conv_tile(n, g)),
                                                       in1=s_xc[:, n], op0=ALU.mult, op1=ALU.add)
                        if k < CW - 1:
                            dve_t.after(ins)
                        else:
                            ins.then_inc(S["s_conved"], 1)

                def weigh(dst, tt, by):
                    x = s_xb[:, tt, 0:GX].rearrange("p (h w) -> p h w", w=HD).unsqueeze(1).broadcast_to([P, 2, GH, HD])
                    f = by[:, tt].rearrange("p (d h) -> p d h", d=2)[:, :, bass.ds(GH * g, GH)]
                    return dve.tensor_tensor(dst.rearrange("p d (h w) -> p d h w", w=HD), x,
                                             f.unsqueeze(3).broadcast_to([P, 2, GH, HD]), ALU.mult)

                for tt in range(NT):
                    dve.wait_ge(S["s_in_copied"], NT * g + tt + 1)
                    weigh(s_xe[:, tt], tt, s_wend).then_inc(S["s_xe_ready"], 1)

                for s in range(LC - 1):
                    for d, tt, nx in ((0, s, s + 1), (1, LC - 1 - s, LC - 2 - s)):
                        f = s_etot[:, tt, bass.ds(d * SH + GH * g, GH)].unsqueeze(2).broadcast_to([P, GH, HD])
                        ins = dve.tensor_tensor(s_h[:, nx, d].rearrange("p (h w) -> p h w", w=HD),
                                                s_h[:, tt, d].rearrange("p (h w) -> p h w", w=HD), f, ALU.mult)
                        if d:
                            dve_t.after(ins)
                        else:
                            dve_t.mark(ins)
                    dve.wait_ge(S["s_upd_done"], 3 * g + s + 1)
                    for d, nx in ((0, s + 1), (1, LC - 2 - s)):
                        ins = dve.tensor_tensor(s_h[:, nx, d], s_h[:, nx, d], bank(4 + s % 2)[:, d * GX:(d + 1) * GX],
                                                ALU.add)
                        if d:
                            ins.then_inc(S["s_h_ready"], 1)
                        else:
                            dve_t.mark(ins)
                    dve.wait_ge(S["s_h_ready"], 3 * g + s + 1)
                dve.wait_ge(S["s_cb_copied"], g + 1)

                def chunk_weights(tt):
                    weigh(s_xd[:, tt % 2], tt, s_dt).then_inc(S["s_xd_ready"], 1)
                    dve.wait_ge(S["s_decayed"], NT * g + tt + 1)
                    m = s_m[:, tt % 3]
                    dve.tensor_tensor(m, m, s_cb[:, tt * P:(tt + 1) * P].unsqueeze(1).broadcast_to([P, 8, P]), ALU.mult
                                      ).then_inc(S["s_m_ready"], 1)

                chunk_weights(0)
                for tt in range(NT):
                    if tt < NT - 1:
                        chunk_weights(tt + 1)
                    dve.wait_ge(S["s_y_done"], NT * g + tt + 1 + NT)
                    y = s_y[:, tt]
                    inner, outer = y_banks(tt)
                    if tt < LC:
                        tmp = s_t[:, tt % 2]
                        f = s_eacs[:, tt].rearrange("p (d h) -> p d h", d=2)[:, :, bass.ds(GH * g, GH)]
                        dve_t.after(dve.tensor_tensor(tmp.rearrange("p (d h w) -> p d h w", d=2, w=HD),
                                                      outer.rearrange("p (d h w) -> p d h w", d=2, w=HD),
                                                      f.unsqueeze(3).broadcast_to([P, 2, GH, HD]), ALU.mult))
                        dve_t.after(dve.tensor_tensor(y, inner[:, 0:GX], tmp[:, 0:GX], ALU.add))
                        dve.tensor_tensor(y, y, tmp[:, GX:], ALU.add).then_inc(S["s_y_read"], 1)
                    else:
                        dve.tensor_copy(y, inner[:, 0:GX]).then_inc(S["s_y_read"], 1)
                dve.wait_ge(ada_done, ADA * ADA_AHEAD + 3 * g + 3)
                for n in range(2):
                    ins = dve.tensor_tensor(mod[:, 2 + n, bass.ds(ADA_TILES * g, ADA_TILES), :],
                                            bank(2)[:, 6 * n:6 * n + 6].rearrange("p (m c) -> p m c", c=2),
                                            bcast(cols[:, bass.ds(col("ada_b", 24 * (2 + n)) + ADA_TILES * g, ADA_TILES)],
                                                  2), ALU.add)
                    if n == 0:
                        dve_t.mark(ins)
                ins.then_inc(ada_read, 1)
            dve_t.leave(GROUPS)
            dve.wait_ge(S["s_y_squared"], NT * GROUPS)
            dve_t.after(dve.tensor_reduce(s_one, s_ssq, X, ALU.add))
            diag = s_m[:, 0:2].rearrange("p a b c -> p (a b) c")
            for tt in range(NT):
                ins = dve.tensor_scalar(diag[:, tt], ident[:], s_one[:, tt:tt + 1], None, ALU.mult)
            ins.then_inc(S["s_rms_diag"], 1)
            dve.wait_ge(S["s_rms_done"], 1)
            dve.tensor_scalar(s_rstd, big(0)[:, 0:TOK], 1.0 / INNER, EPS, ALU.mult, ALU.add).then_inc(S["s_rms_root"], 1)

        def ssd_out_scale(dve):
            dve.wait_ge(S["s_rms_root"], 2)
            dve_t.after(dve.reciprocal(s_rstd, s_rstd))

        def ssd_pool(pool):
            for n, (dst, src) in enumerate(((s_bias, t["ssd_dt_bias"]), (s_a, t["ssd_a_log"]), (s_d, t["ssd_d"]))):
                v = src.rearrange("a d h -> a (d h)") if len(src.shape) == 3 else src
                pool.dma_start(dst, v.broadcast_to([P, v.shape[1]])).then_inc(S["s_small_loaded"], 16)
            pool.memset(s_raw, 0.0).then_inc(S["s_zeroed"], 1)
            split_slab(pool, n=2 * SH)
            pool.wait_ge(S["s_rows_copied"], 2)
            for d in range(2):
                pool.dma_start(acs_rows[d * SH:(d + 1) * SH], s_rows[:, d]).then_inc(S["s_rows_stored"], 16)
            pool.wait_ge(S["s_rows_stored"], 32)
            rows = acs_rows.rearrange("(d h) n -> d h n", d=2)

            def load_rows(g, tt):
                for d in range(2):
                    src = rows[d, bass.ds(GH * g, GH), tt * P:(tt + 1) * P].unsqueeze(0)
                    pool.dma_start(s_m[:, tt % 3, d * GH:(d + 1) * GH], src.broadcast_to([P, GH, P])
                                   ).then_inc(S[f"s_rows_loaded{tt % 3}"], 16)

            def mask(g, tt):
                per = 64 if tt % 3 < 2 else 32
                pool.wait_ge(S[f"s_rows_loaded{tt % 3}"], per * g + 32 * (tt // 3) + 32)
                m = s_m[:, tt % 3].rearrange("p (d h) i -> p d h i", d=2)
                for d in range(2):
                    ins = pool.tensor_tensor(m[:, d], m[:, d], neg[:, d].unsqueeze(1).broadcast_to([P, GH, P]), ALU.add)
                    if d == 0:
                        pool_t.mark(ins)
                ins.then_inc(S["s_masked"], 1)

            split_slab(pool)
            split_slab(pool)
            with pool.Fori(0, GROUPS) as g:
                pool_t.enter(g, 15 + 6)
                slabs.enter(g, GROUP_SLABS[2:] + GROUP_SLABS[:2])
                pool.wait_ge(S["s_y_done"], NT * g + NT)
                apart(pool)
                for d in range(2):
                    src = t["state_ssd"][0, 0, d, bass.ds(GH * g, GH)].rearrange("(a h) w n -> (h w) a n", a=2)
                    pool.dma_start(s_in[:, 2 * d:2 * d + 2], src).then_inc(S["s_state_loaded"], 16)
                for tt in range(3):
                    load_rows(g, tt)
                split_slab(pool)
                for n in range(3):
                    slabs.take(GROUP_SLABS[3 + n])
                for tt in range(3):
                    mask(g, tt)
                pool.wait_ge(S["s_fin_copied"], g + 1)
                apart(pool)
                for d in range(2):
                    dst = out["new_ssd"][0, 0, d, bass.ds(GH * g, GH)].rearrange("(a h) w n -> (h w) a n", a=2)
                    pool.dma_start(dst, s_fin[:, 2 * d:2 * d + 2]).then_inc(S["s_fin_stored"], 16)
                for tt in range(NT):
                    pool.wait_ge(S["s_y_read"], NT * g + NT + tt + 1)
                    apart(pool)
                    if tt < 2:
                        load_rows(g, tt + 3)
                    y, x = s_y[:, tt], s_xb[:, tt, 0:GX]
                    xd = s_t2[:, tt % 2]
                    f = s_d[:, bass.ds(GH * g, GH)].unsqueeze(2).broadcast_to([P, GH, HD])
                    pool_t.after(pool.tensor_tensor(xd.rearrange("p (h w) -> p h w", w=HD),
                                                    x.rearrange("p (h w) -> p h w", w=HD), f, ALU.mult))
                    pool_t.after(pool.tensor_tensor(y, y, xd, ALU.add))
                    pool.tensor_tensor(y, y, s_z[:, tt], ALU.mult).then_inc(S["s_y_ready"], 1)
                    if tt < 2:
                        mask(g, tt + 3)
                    if tt == LC - 1:
                        slot, _, full, _ = slabs.take(HALVES)
                        split_half(pool, slot, full, 0)
                    if tt == LC:
                        split_half(pool, slot, full, 1)
                        split_slab(pool)
                pool.wait_ge(S["s_fin_stored"], 32 * g + 32)
            pool_t.leave(GROUPS)
            slabs.leave(GROUPS)

        def ssd_credits_act(act):
            act.sem_inc(S["s_pj_read"], 9)
            act.sem_inc(S["s_y_copied"], 2)

        def ssd_credits_dve(dve):
            dve.sem_inc(S["s_conved"], 4)
            dve.sem_inc(S["s_y_read"], 5)

        def ssd_credits_pe(pe):
            pe.sem_inc(S["s_y_done"], 5)


        c_ = Room()
        m_raw, m_xc = c_(KH, RAW), c_(KH, CONV)
        m_wide = c_(16, TOK)
        m_q = m_wide[:, 0:4]
        m_k = m_wide[:, 4:8]
        m_v = m_wide[:, 8:12].rearrange("p a b -> p (a b)").rearrange("p (t n) -> p t n", n=DH)
        m_hh = m_wide[:, 12:16].rearrange("p a b -> p (a b)").rearrange("p (t n) -> p t n", n=DH)
        xc_lo = room_r[:, c_.at:c_.at + KH * TOK].rearrange("p (k n) -> p k n", n=TOK)
        m_sw, m_swc = c_(LC, TOK), c_(2, P)
        xc_hi = room_r[:, c_.at:c_.at + KH * TOK].rearrange("p (k n) -> p k n", n=TOK)
        XC = tiles_before(2)
        m_row, m_diag = c_(2, TOK), c_(2, TOK)
        m_t = c_(2, DH)
        m_gt, m_lf, m_gb = c_(NT, 16), c_(NT, 16), c_(16)
        m_c = c_(P)
        m_den, m_r, m_rg = c_(8), c_(2, 2), c_(2, 2)
        m_stat, m_mv, m_sd = c_(NT, 6), c_(NT, 2), c_(NT)
        m_m0, m_new = c_(2), c_(2)
        m_kw = m_sw.rearrange("p a b -> p (a b)")[:, 0:2 * DH].rearrange("p (d n) -> p d n", d=2)
        q_place, sw_place = (a.rearrange("p a b -> p (a b)") for a in (m_q, m_sw))
        m_cst = [q_place[:, n * DH:(n + 1) * DH] if n < 5 else sw_place[:, (n - 3) * DH:(n - 2) * DH] for n in range(8)]
        m_nst = m_diag.rearrange("p a b -> p (a b)")[0:1, 0:2 * DH]
        m_zero = m_raw[0:ML_HEADS, 0, 0:LAT]
        R_IG, R_LF, R_BC, R_G, R_M, R_GI, R_EN, R_WE = range(0, 16, 2)
        kinds = ["xm"] * 4 + ["o"] * 2 * NT + ["z"] * 4 + ["q"] * 4 + ["k"] * 4 + ["v"] * NT
        per_slab = dict(xm=2, o=NT, z=2, q=4, k=4, v=NT)
        PJ = len(kinds)
        HEAD_SLABS = [HALVES] * 8 + [WHOLE] * 3 + [None]
        by_dve = [k in ("q", "v") for k in kinds]
        N_V = sum(by_dve)
        N_A = PJ - N_V

        sems("m_small_loaded", "m_zeroed", "m_gates_done", "m_gates_read", "m_softplus", "m_lf_ready", "m_rows_turned", "m_rows_copied",
             "m_scanned", "m_rows_exp", "m_rows_stored", "m_cols_turned",
             "m_pj_done", "m_rd_a", "m_rd_v", "m_tap0", "m_conved", "m_x_ready", "m_row_loaded", "m_masked", "m_w_ready",
             "m_s_done", "m_sw_ready", "m_den_done", "m_init_done", "m_num_done", "m_i_read", "m_r_ready", "m_t_ready", "m_h_ready",
             "m_var_ready", "m_sd_ready", "m_ln_ready", "m_kt_done", "m_kw_ready", "m_c_done", "m_c_copied_a",
             "m_c_copied_v", "m_c_stored_a", "m_c_stored_v", "m_n_done", "m_n_copied", "m_n_stored", "m_sk_ready",
             "m_h_turned", "m_a_ready", "m_y_ready")

        def pair(n):
            return ps[:, 2 * n:2 * n + 2, :].rearrange("p a b -> p (a b)")

        def ml_sync(sp):
            w = t["ml_w_in"][0].rearrange("(k p) n -> p k n", p=P)
            slot, free, _, _ = slabs.take(HALVES)
            sp.wait_ge(w_used, free)
            load_halves(sp, slot, columns(ring, slot, 2 * P)[:, :, 0:16], w[:, :, 3 * INNER:3 * INNER + 16], KD)
            with sp.Fori(0, ML_HEADS) as h:
                slabs.enter(h, HEAD_SLABS)
                for c in range(3):
                    for half in range(2):
                        slot, free, _, _ = slabs.take(HALVES)
                        sp.wait_ge(w_used, free)
                        apart(sp)
                        load_halves(sp, slot, columns(ring, slot, 2 * P),
                                    w[:, :, bass.ds(INNER * c + DH * h + 2 * P * half, 2 * P)], KD)
                for name in ("ml_w_q", "ml_w_k", "ml_w_v", 0, 1):
                    whole = name not in ("ml_w_q", "ml_w_k")
                    slot, free, _, _ = slabs.take(WHOLE if whole else HALVES)
                    sp.wait_ge(w_used, free)
                    apart(sp)
                    src = t["state_mlstm_c"][0, 0, name] if isinstance(name, int) else t[name][0]
                    src = src[bass.ds(h, 1)].rearrange("a (k p) n -> p (a k) n", p=P)
                    if whole:
                        sp.dma_start(columns(ring, slot, DH), src).then_inc(w_loaded[slot][0], 16)
                    else:
                        load_halves(sp, slot, columns(ring, slot, DH), src, KH)
                slabs.take(None)
            slabs.leave(ML_HEADS)

        def ml_in_pe(pe):
            slot, _, _, split = slabs.take(HALVES)
            hi, lo = columns(w_hi, slot, 2 * P), columns(w_lo, slot, 2 * P)
            pe.wait_ge(w_split, split[1])
            for tt in range(NT):
                c = slice(tt * P, (tt + 1) * P)
                for k in range(KD):
                    if tt == 0:
                        pe.wait_ge(h_ready, KD * 2 + k + 1)
                    mm = split3(pe, bank(6)[:, tt * 16:(tt + 1) * 16], h_hi[:, k, c], h_lo[:, k, c],
                                hi[:, k, 0:16], lo[:, k, 0:16], start=(k == 0), stop=(k == KD - 1))
            slab_through(pe, mm, bank(6)[0:2, 510:512], S["m_gates_done"])
            pe.wait_ge(S["m_lf_ready"], 1)
            for q in range(4):
                src = m_gt if q < 2 else m_lf
                at = 8 * (q % 2) + (0 if q < 2 else 4)
                for tt in range(NT):
                    mm = pe.transpose(pair(q)[0:4, tt * P:(tt + 1) * P], src[:, tt, at:at + 4], ident[:])
            mm.then_inc(S["m_rows_turned"], 1)
            pe.wait_ge(S["m_rows_copied"], 4)
            pe.wait_ge(S["m_rows_exp"], 8)
            for tt in range(NT):
                for n, q in enumerate((R_G, R_GI, R_EN)):
                    for d in range(2):
                        at = 24 * tt + 8 * n + 4 * d
                        pe.transpose(bank(6)[:, at:at + 4], m_wide[0:4, q + d, tt * P:(tt + 1) * P], ident[0:4, 0:4])
            for d in range(2):
                mm = pe.transpose(bank(6)[:, 120 + 4 * d:124 + 4 * d], m_wide[0:4, R_WE + d, 0:P], ident[0:4, 0:4])
            mm.then_inc(S["m_cols_turned"], 1)
            fence(pe, "pe")

        def ml_in_dve(dve):
            fl = lambda a: a.rearrange("p a b -> p (a b)")
            dve.wait_ge(S["m_small_loaded"], 32)
            dve.wait_ge(S["m_zeroed"], 1)
            dve.wait_ge(S["m_gates_done"], 1)
            dve.tensor_tensor(m_gt, bank(6)[:, 0:80].rearrange("p (a b) -> p a b", b=16),
                              m_gb.unsqueeze(1).broadcast_to([P, NT, 16]), ALU.add).then_inc(S["m_gates_read"], 1)
            dve.wait_ge(S["m_softplus"], 3)
            dve.wait_ge(S["m_gates_read"], 1)
            dve.scalar_tensor_tensor(out=fl(m_lf), in0=fl(m_gt), scalar=0.0, in1=fl(m_lf), op0=ALU.min,
                                     op1=ALU.subtract).then_inc(S["m_lf_ready"], 1)
            dve.wait_ge(S["m_rows_copied"], 4)

            def run(a, d):
                return a if d == 0 else a[:, ::-1]

            last = {}
            for d in range(2):
                for s in range(2):
                    c = seg(s)
                    n = c.stop - c.start
                    lf, ig, bc, g, mx = (m_wide[0:4, q + d, c] for q in (R_LF, R_IG, R_BC, R_G, R_M))
                    dve_t.after(dve.tensor_tensor_scan(run(bc, d), run(lf, d), m_zero[:, 0:n], 0.0, ALU.add, ALU.add))
                    dve_t.after(dve.tensor_tensor(g, ig, bc, ALU.subtract))
                    dve_t.after(dve.tensor_tensor_scan(run(mx, d), run(g, d), run(g, d),
                                                       m_m0[0:4, d:d + 1] if s == 0 else 0.0, ALU.max, ALU.max))
                dve_t.mark(dve.scalar_tensor_tensor(out=m_wide[0:4, R_EN + d], in0=m_wide[0:4, R_BC + d], scalar=-1.0,
                                                    in1=m_wide[0:4, R_M + d], op0=ALU.mult, op1=ALU.subtract))
                e = TOK - 1 if d == 0 else LAT
                dve_t.mark(dve.tensor_tensor(m_new[0:4, d:d + 1], m_wide[0:4, R_BC + d, e:e + 1],
                                             m_wide[0:4, R_M + d, e:e + 1], ALU.add))
                dve.tensor_scalar(m_wide[0:4, R_WE + d, 0:P], m_wide[0:4, R_G + d, LAT:TOK],
                                  m_wide[0:4, R_M + d, e:e + 1], None, ALU.subtract).then_inc(S["m_scanned"], 1)
            fence(dve, "dve")

        def ml_in_act(act):
            act.wait_ge(S["m_gates_read"], 1)
            act.activation(m_lf, m_gt, ACT.Abs).then_inc(S["m_softplus"], 1)
            act.wait_ge(S["m_softplus"], 1)
            act.activation(m_lf, m_lf, ACT.Exp, scale=-1.0).then_inc(S["m_softplus"], 1)
            act.wait_ge(S["m_softplus"], 2)
            act.activation(m_lf, m_lf, ACT.Ln, bias=1.0).then_inc(S["m_softplus"], 1)
            act.wait_ge(S["m_rows_turned"], 1)
            for q in range(4):
                act.activation(m_wide[0:4, q], pair(q)[0:4, 0:TOK], ACT.Copy).then_inc(S["m_rows_copied"], 1)
            act.wait_ge(S["m_scanned"], 2)
            for d in range(2):
                act.activation(m_wide[0:4, R_GI + d, 0:LAT], m_wide[0:4, R_M + d, 0:LAT], ACT.Exp, scale=-1.0,
                               bias=m_m0[0:4, d:d + 1]).then_inc(S["m_rows_exp"], 1)
                act.activation(m_wide[0:4, R_GI + d, LAT:TOK], m_wide[0:4, R_M + d, LAT:TOK], ACT.Exp, scale=-1.0
                               ).then_inc(S["m_rows_exp"], 1)
                act.activation(m_wide[0:4, R_WE + d, 0:P], m_wide[0:4, R_WE + d, 0:P], ACT.Exp).then_inc(S["m_rows_exp"], 1)
            for d in range(2):
                act.activation(m_wide[0:4, R_EN + d], m_wide[0:4, R_EN + d], ACT.Exp).then_inc(S["m_rows_exp"], 1)
            act.wait_ge(S["m_cols_turned"], 1)
            act.activation(m_c, bank(6)[:, 0:P], ACT.Copy)
            fence(act, "act")

        def ml_in_pool(pool):
            pool.memset(m_raw, 0.0).then_inc(S["m_zeroed"], 1)
            pool.dma_start(m_gb, t["ml_gate_b"].rearrange("a d g h -> a (d g h)").broadcast_to([P, 16])
                           ).then_inc(S["m_small_loaded"], 16)
            pool.dma_start(m_m0[0:4], t["state_mlstm_m"][0, 0].rearrange("d h -> h d"), allow_slow_non_contiguous=True).then_inc(S["m_small_loaded"], 16)
            split_slab(pool, n=16)
            pool.wait_ge(S["m_scanned"], 2)
            pool.dma_start(max_rows, m_wide[0:4, R_M:R_M + 2].rearrange("p a b -> p (a b)")
                           ).then_inc(S["m_rows_stored"], 16)
            pool.dma_start(out["new_mlstm_m"][0, 0].rearrange("d h -> h d"), m_new[0:4],
                           allow_slow_non_contiguous=True).then_inc(S["m_rows_stored"], 16)
            pool.wait_ge(S["m_rows_stored"], 32)
            fence(pool, "pool")

        def tokens(a, k, tt, lat, ctx_at):
            at = lat + tt * P if tt < LC else ctx_at
            return a[:, k, at:at + P]

        def ml_pe(pe):
            with pe.Fori(0, ML_HEADS) as h:
                slabs.enter(h, HEAD_SLABS)
                for n, kind in enumerate(kinds):
                    i = n - kinds.index(kind)
                    j = i % per_slab[kind]
                    first, last = j == 0, j == per_slab[kind] - 1
                    is_split = kind != "v"
                    if first:
                        slot, _, full, split = slabs.take(HALVES if is_split else WHOLE)
                        if not is_split:
                            pe.wait_ge(w_loaded[slot][0], full[0])
                    kt = KD if kind in ("xm", "o", "z") else KH
                    hi, lo, w = (columns(a, slot, SLAB // kt) for a in (w_hi, w_lo, ring))
                    c = slice(j * P, (j + 1) * P)
                    if n < 2:
                        pe.wait_ge(S["m_c_copied_a"], 4 * h + 4)
                        pe.wait_ge(S["m_c_copied_v"], 4 * h + 4)
                    elif by_dve[n - 2]:
                        pe.wait_ge(S["m_rd_v"], N_V * h + sum(by_dve[:n - 1]))
                    else:
                        pe.wait_ge(S["m_rd_a"], N_A * h + (n - 1) - sum(by_dve[:n - 1]))
                    if i == 0 and kind == "q":
                        pe.wait_ge(y_split, XC + 4 * h + 4)
                    b = big(n % 2)
                    for k in range(kt):
                        st = dict(start=(k == 0), stop=(k == kt - 1))
                        if is_split and first and k % (kt // 2) == 0:
                            pe.wait_ge(w_split, split[k // (kt // 2)])
                        if kind in ("xm", "z"):
                            mm = split3_tile(pe, b, hi[:, k, c], lo[:, k, c], h_hi[:, k], h_lo[:, k], **st)
                        elif kind in ("q", "k"):
                            mm = split3_tile(pe, b, hi[:, k, c], lo[:, k, c], xc_hi[:, k], xc_lo[:, k], **st)
                        elif kind == "o":
                            mm = split3(pe, b[:, 0:2 * P], h_hi[:, k, c], h_lo[:, k, c], hi[:, k], lo[:, k], **st)
                        else:
                            mm = pe.matmul(b[:, 0:DH], tokens(m_raw, k, i, RAW_LAT, RAW_CTX), w[:, k], **st)
                    if last:
                        slab_through(pe, mm, last_cols(n % 2), S["m_pj_done"])
                    else:
                        mm.then_inc(S["m_pj_done"], 1)
                for j in range(NT):
                    if j == 0:
                        pe.wait_ge(S["m_rd_v"], N_V * h + 4)
                        pe.wait_ge(S["m_rd_a"], N_A * h + N_A)
                        pe.wait_ge(S["m_a_ready"], 4 * h + 4)
                    if j >= 2:
                        pe.wait_ge(S["m_sw_ready"], NT * h + j - 1)
                    n = LAT if j < LC else P
                    for k in range(KH):
                        mm = pe.matmul(bank(4 + j % 2)[:, 0:n], m_k[:, k, j * P:(j + 1) * P],
                                       m_q[:, k, 0:LAT] if j < LC else m_q[:, k, LAT:TOK],
                                       start=(k == 0), stop=(k == KH - 1))
                    mm.then_inc(S["m_s_done"], 1)
                pe.wait_ge(S["m_sw_ready"], NT * h + NT)
                pe.wait_ge(S["m_rd_v"], N_V * h + N_V)
                c0 = []
                for d in range(2):
                    slot, _, full, _ = slabs.take()
                    c0.append(columns(ring, slot, DH))
                    pe.wait_ge(w_loaded[slot][0], full[0])
                for i in range(NT):
                    sums = bank(6 + i % 2)
                    sets = []
                    for d in range(2):
                        js = [LC] if i == LC else (range(0, i + 1) if d == 0 else range(i, LC))
                        for j in js:
                            if i == LC:
                                a = m_swc[:, d]
                            elif d == 0:
                                a = m_sw[:, j, (i - j) * P:(i - j + 1) * P]
                            else:
                                a = m_sw[:, j, LAT - j * P + i * P:LAT - j * P + (i + 1) * P]
                            sets.append((d, a, j, j == js[0], j == js[-1]))
                    if i >= 2:
                        pe.wait_ge(S["m_r_ready"], NT * h + i - 1)
                    for d, a, j, st, sp_ in sets:
                        mm = pe.matmul(sums[:, d:d + 1], a, ones[:, 0:1], start=st, stop=sp_)
                    if i < LC:
                        for k in range(KH):
                            n0 = cols[:, bass.ds(col("state_mlstm_n", k) + KH * h, 17)][:, ::16]
                            mm = pe.matmul(sums[:, 2:4], m_q[:, k, i * P:(i + 1) * P], n0,
                                           start=(k == 0), stop=(k == KH - 1))
                    mm.then_inc(S["m_den_done"], 1)
                    if i < LC:
                        if i:
                            pe.wait_ge(S["m_t_ready"], LC * h + i)
                        for d in range(2):
                            for k in range(KH):
                                mm = pe.matmul(bank(2 + d), m_q[:, k, i * P:(i + 1) * P], c0[d][:, k],
                                               start=(k == 0), stop=(k == KH - 1))
                            if i == LC - 1 and d == 0:
                                mm.then_inc(w_used, 1)
                    if i == LC - 1:
                        slab_through(pe, mm, bank(4)[0:2, 510:512], S["m_init_done"], empty=True)
                    elif i < LC:
                        mm.then_inc(S["m_init_done"], 1)
                    if i:
                        pe.wait_ge(S["m_i_read"], NT * h + i)
                    for d, a, j, st, sp_ in sets:
                        mm = pe.matmul(bank(d), a, m_v[:, j], start=st, stop=sp_)
                    mm.then_inc(S["m_num_done"], 1)
                for k in range(KH):
                    mm = pe.transpose(bank(7)[:, k * P:(k + 1) * P], m_k[:, k, LAT:TOK], ident[:])
                mm.then_inc(S["m_kt_done"], 1)
                pe.wait_ge(S["m_i_read"], NT * h + NT)
                pe.wait_ge(S["m_kw_ready"], h + 1)
                for d in range(2):
                    mm = pe.matmul(bank(4 + d)[0:1, :], ones[:, 0:1], m_kw[:, d], start=True, stop=True)
                mm.then_inc(S["m_n_done"], 1)
                for n in range(8):
                    d, m = divmod(n, KH)
                    if n >= 4:
                        pe.wait_ge(S["m_c_copied_v" if n % 2 else "m_c_copied_a"], 4 * h + 4 + (n - 4) // 2 + 1)
                    pe.matmul(bank(n % 4), m_kw[:, d, m * P:(m + 1) * P], m_v[:, LC], start=True, stop=True
                              ).then_inc(S["m_c_done"], 1)
                pe.wait_ge(S["m_ln_ready"], h + 1)
                pe.wait_ge(S["m_n_copied"], h + 1)
                for m in range(KH):
                    if m >= 2:
                        pe.wait_ge(S["m_a_ready"], 4 * h + 4 + m - 1)
                    for tt in range(NT):
                        mm = pe.transpose(pair(2 + m % 2)[:, tt * P:(tt + 1) * P], m_hh[:, tt, m * P:(m + 1) * P], ident[:])
                    mm.then_inc(S["m_h_turned"], 1)
            slabs.leave(ML_HEADS)

        def ml_act(act):
            with act.Fori(0, ML_HEADS) as h:
                done = 0
                for n, kind in enumerate(kinds):
                    i = n - kinds.index(kind)
                    b = big(n % 2)
                    if by_dve[n]:
                        continue
                    act.wait_ge(S["m_pj_done"], PJ * h + n + 1)
                    done += 1
                    if kind == "xm":
                        if i == 0:
                            act.wait_ge(S["m_y_ready"], 4 * h + 4)
                        act.activation(m_raw[:, i, RAW_LAT:RAW_LAT + LAT], wide(b)[:, 0:LAT], ACT.Copy)
                        act.activation(m_raw[:, i, RAW_CTX:RAW_CTX + CTX], wide(b)[:, LAT:TOK], ACT.Copy
                                       ).then_inc(S["m_rd_a"], 1)
                        act.wait_ge(S["m_rd_a"], N_A * h + done)
                        act.activation(m_xc[:, i], m_raw[:, i, 0:CONV], ACT.Identity,
                                       bias=pcol(col("ml_conv_b") + KH * h + i), scale=pcol(col("ml_conv_w") + KH * h + i)
                                       ).then_inc(S["m_tap0"], 1)
                    elif kind == "o":
                        c, tt = divmod(i, NT)
                        act.activation(m_hh[:, tt, c * 2 * P:(c + 1) * 2 * P], b[:, 0:2 * P], ACT.Sigmoid
                                       ).then_inc(S["m_rd_a"], 1)
                        x = i - (2 * NT - KH)
                        if x >= 0:
                            act.wait_ge(S["m_conved"], 4 * h + x + 1)
                            act.activation(m_xc[:, x], m_xc[:, x], ACT.Silu).then_inc(S["m_x_ready"], 1)
                            act.wait_ge(S["m_x_ready"], 4 * h + x + 1)
                            act.activation(xc_hi[:, x, 0:LAT], m_xc[:, x, 0:LAT], ACT.Copy)
                            act.activation(xc_hi[:, x, LAT:], m_xc[:, x, C_CTX:], ACT.Copy).then_inc(y_high, 1)
                    elif kind == "z":
                        act.activation(yT[:, bass.ds(KH * h + i, 1), :].rearrange("p a b -> p (a b)"), wide(b), ACT.Silu
                                       ).then_inc(S["m_rd_a"], 1)
                    else:
                        act.activation(m_k[:, i], wide(b), ACT.Copy, scale=DH ** -0.5).then_inc(S["m_rd_a"], 1)
                act.wait_ge(S["m_masked"], h + 1)
                for j in range(NT):
                    for d in range(2):
                        g = m_c[:, bass.ds(24 * j + 4 * d + h, 1)]
                        if j == LC:
                            parts = [(m_swc[:, d], m_diag[:, d, LAT:TOK])]
                        elif d == 0:
                            parts = [(m_sw[:, j, 0:P], m_diag[:, 0, j * P:(j + 1) * P]),
                                     (m_sw[:, j, P:LAT - j * P], m_row[:, 0, (j + 1) * P:LAT])]
                        else:
                            parts = [(m_sw[:, j, LAT - j * P:LAT], m_row[:, 1, 0:j * P]),
                                     (m_sw[:, j, LAT:TOK], m_diag[:, 1, j * P:(j + 1) * P])]
                        for dst, src in parts:
                            if dst.shape[1]:
                                ins = act.activation(dst, src, ACT.Exp, scale=-1.0, bias=g)
                    ins.then_inc(S["m_w_ready"], 1)
                for i in range(LC):
                    act.wait_ge(S["m_r_ready"], NT * h + i + 1)
                    act.wait_ge(S["m_init_done"], LC * h + i + 1)
                    if i:
                        act.wait_ge(S["m_h_ready"], NT * h + i)
                    for d in range(2):
                        ins = act.activation(m_t[:, d], bank(2 + d), ACT.Copy, scale=m_rg[:, i % 2, d:d + 1])
                    ins.then_inc(S["m_t_ready"], 1)
                for k in range(KH):
                    act.activation(m_xc[:, k], m_xc[:, k], ACT.Copy, scale=pcol(col("ml_skip") + KH * h + k)
                                   ).then_inc(S["m_sk_ready"], 1)
                act.wait_ge(S["m_kt_done"], h + 1)
                for d in range(2):
                    ins = act.activation(m_kw[:, d], bank(7), ACT.Copy, scale=m_c[:, bass.ds(120 + 4 * d + h, 1)])
                ins.then_inc(S["m_kw_ready"], 1)
                act.wait_ge(S["m_n_done"], h + 1)
                for d in range(2):
                    ins = act.activation(m_nst[:, d * DH:(d + 1) * DH], bank(4 + d)[0:1, :], ACT.Copy)
                ins.then_inc(S["m_n_copied"], 1)
                act.wait_ge(S["m_var_ready"], h + 1)
                act.activation(m_sd, m_sd, ACT.Sqrt).then_inc(S["m_sd_ready"], 1)
                for n in range(0, 8, 2):
                    act.wait_ge(S["m_c_done"], 8 * h + n + 1)
                    act.activation(m_cst[n], bank(n % 4), ACT.Copy).then_inc(S["m_c_copied_a"], 1)

        def ml_dve(dve):
            with dve.Fori(0, ML_HEADS) as h:
                dve_t.enter(h, ML_DVE)
                for n in range(KH):
                    dve.wait_ge(S["m_tap0"], 4 * h + n + 1)
                    for k in range(1, CW):
                        ins = dve.scalar_tensor_tensor(out=m_xc[:, n], in0=m_raw[:, n, k:k + CONV],
                                                       scalar=pcol(col("ml_conv_w", KI * k) + KH * h + n),
                                                       in1=m_xc[:, n], op0=ALU.mult, op1=ALU.add)
                        if k < CW - 1:
                            dve_t.after(ins)
                        else:
                            ins.then_inc(S["m_conved"], 1)
                for n in range(KH):
                    dve.wait_ge(y_high, XC + 4 * h + n + 1)
                    dve.tensor_tensor(xc_lo[:, n, 0:LAT], m_xc[:, n, 0:LAT], xc_hi[:, n, 0:LAT].bitcast(F32),
                                      ALU.subtract)
                    dve.tensor_tensor(xc_lo[:, n, LAT:], m_xc[:, n, C_CTX:], xc_hi[:, n, LAT:].bitcast(F32),
                                      ALU.subtract).then_inc(y_split, 1)
                for n, kind in enumerate(kinds):
                    if not by_dve[n]:
                        continue
                    i = n - kinds.index(kind)
                    dve.wait_ge(S["m_pj_done"], PJ * h + n + 1)
                    if kind == "q":
                        ins = dve.tensor_copy(m_q[:, i], wide(big(n % 2)))
                    else:
                        ins = dve.tensor_copy(m_v[:, i], big(n % 2)[:, 0:DH])
                    ins.then_inc(S["m_rd_v"], 1)
                for j in range(NT):
                    dve.wait_ge(S["m_s_done"], NT * h + j + 1)
                    dve.wait_ge(S["m_w_ready"], NT * h + NT + j + 1)
                    s = bank(4 + j % 2)
                    for d in range(2):
                        if j == LC:
                            a, b = m_swc[:, d], s[:, 0:P]
                        elif d == 0:
                            a, b = m_sw[:, j, 0:LAT - j * P], s[:, j * P:LAT]
                        else:
                            a, b = m_sw[:, j, LAT - j * P:TOK], s[:, 0:(j + 1) * P]
                        ins = dve.tensor_tensor(a, a, b, ALU.mult)
                        if d == 0:
                            dve_t.mark(ins)
                    ins.then_inc(S["m_sw_ready"], 1)
                def token_stats(i):
                    dve.wait_ge(S["m_h_ready"], NT * h + i + 1)
                    ins = dve.bn_stats(m_stat[:, i], m_hh[:, i])
                    if i < NT - 1:
                        dve_t.mark(ins)
                    else:
                        dve_t.after(ins)

                for i in range(NT):
                    dve.wait_ge(S["m_den_done"], NT * h + i + 1)
                    sums = bank(6 + i % 2)
                    gi, en = (m_c[:, bass.ds(24 * i + at + h, 5)][:, ::4] for at in (8, 16))
                    den, r, rg = m_den[:, 4 * (i % 2):4 * (i % 2) + 2], m_r[:, i % 2], m_rg[:, i % 2]
                    if i < LC:
                        dve_t.after(dve.tensor_tensor(den, sums[:, 2:4], gi, ALU.mult))
                        dve_t.after(dve.tensor_tensor(den, sums[:, 0:2], den, ALU.add))
                    else:
                        dve_t.after(dve.tensor_copy(den, sums[:, 0:2]))
                    dve_t.after(dve.scalar_tensor_tensor(out=den, in0=den, scalar=-1.0, in1=den, op0=ALU.mult,
                                                         op1=ALU.max))
                    dve_t.after(dve.tensor_tensor(den, den, en, ALU.max))
                    dve_t.after(dve.reciprocal(r, den))
                    if i < LC:
                        dve.tensor_tensor(rg, r, gi, ALU.mult).then_inc(S["m_r_ready"], 1)
                        dve.wait_ge(S["m_t_ready"], LC * h + i + 1)
                        dve.wait_ge(S["m_num_done"], NT * h + i + 1)
                        for d in range(2):
                            ins = dve.scalar_tensor_tensor(out=m_t[:, d], in0=bank(d), scalar=r[:, d:d + 1],
                                                           in1=m_t[:, d], op0=ALU.mult, op1=ALU.add)
                            if d == 0:
                                dve_t.mark(ins)
                    else:
                        dve.tensor_tensor(rg, r, gi, ALU.mult).then_inc(S["m_r_ready"], 1)
                        dve.wait_ge(S["m_h_ready"], NT * h + i)
                        dve.wait_ge(S["m_num_done"], NT * h + i + 1)
                        for d in range(2):
                            ins = dve.tensor_scalar(m_t[:, d], bank(d), r[:, d:d + 1], None, ALU.mult)
                            if d == 0:
                                dve_t.mark(ins)
                    ins.then_inc(S["m_i_read"], 1)
                    if i:
                        token_stats(i - 1)
                token_stats(NT - 1)
                apart(dve)
                for i in range(NT):
                    ins = dve.bn_aggr(m_mv[:, i], m_stat[:, i])
                    if i < NT - 1:
                        dve_t.mark(ins)
                    else:
                        dve_t.after(ins)
                dve.tensor_scalar(m_sd, m_mv[:, :, 1], EPS, None, ALU.add).then_inc(S["m_var_ready"], 1)
                dve.wait_ge(S["m_sd_ready"], h + 1)
                dve_t.after(dve.reciprocal(m_sd, m_sd))
                for i in range(NT):
                    ins = dve.tensor_scalar(m_hh[:, i], m_hh[:, i], m_mv[:, i, 0:1], m_sd[:, i:i + 1], ALU.subtract,
                                            ALU.mult)
                    if i < NT - 1:
                        dve_t.mark(ins)
                ins.then_inc(S["m_ln_ready"], 1)
                for n in range(1, 8, 2):
                    dve.wait_ge(S["m_c_done"], 8 * h + n + 1)
                    dve.tensor_copy(m_cst[n], bank(n % 4)).then_inc(S["m_c_copied_v"], 1)
                for m in range(KH):
                    dve.wait_ge(S["m_h_turned"], 4 * h + m + 1)
                    dve.wait_ge(S["m_sk_ready"], 4 * h + m + 1)
                    for s, c in ((0, slice(0, LAT)), (1, slice(C_CTX, CONV))):
                        ins = dve.scalar_tensor_tensor(out=m_xc[:, m, c], in0=pair(2 + m % 2)[:, seg(s)],
                                                       scalar=pcol(col("ml_norm_g") + KH * h + m), in1=m_xc[:, m, c],
                                                       op0=ALU.mult, op1=ALU.add)
                        if s == 0:
                            dve_t.mark(ins)
                    ins.then_inc(S["m_a_ready"], 1)
            dve_t.leave(ML_HEADS)

        ML_DVE = 8 + 5 + 4 * 5 + 4 + 5 + 10 + 1 + 4 + 4

        def ml_pool(pool):
            ml_in_pool(pool)
            split_slab(pool)
            split_slab(pool)
            with pool.Fori(0, ML_HEADS) as h:
                pool_t.enter(h, 1 + NT + KH + 16)
                slabs.enter(h, HEAD_SLABS[2:] + HEAD_SLABS[:2])
                for _ in range(6):
                    split_slab(pool)
                for _ in range(3):
                    slabs.take()
                slabs.take(None)
                pool.wait_ge(S["m_rd_a"], N_A * h + N_A)
                apart(pool)
                pool.dma_start(m_row.rearrange("p a b -> p (a b)"), max_rows[bass.ds(h, 1)].broadcast_to([P, 2 * TOK])
                               ).then_inc(S["m_row_loaded"], 16)
                pool.wait_ge(S["m_row_loaded"], 16 * h + 16)
                for d in range(2):
                    ins = pool.tensor_tensor(m_diag[:, d].rearrange("p (t i) -> p t i", i=P),
                                             m_row[:, d].rearrange("p (t i) -> p t i", i=P),
                                             neg[:, d].unsqueeze(1).broadcast_to([P, NT, P]), ALU.subtract)
                    if d == 0:
                        pool_t.mark(ins)
                ins.then_inc(S["m_masked"], 1)
                for i in range(NT):
                    pool.wait_ge(S["m_i_read"], NT * h + i + 1)
                    pool_t.after(pool.tensor_tensor(m_t[:, 0], m_t[:, 0], m_t[:, 1], ALU.add))
                    pool.tensor_tensor(m_hh[:, i], m_hh[:, i], m_t[:, 0], ALU.mult).then_inc(S["m_h_ready"], 1)
                pool.wait_ge(S["m_n_copied"], h + 1)
                apart(pool)
                for d in range(2):
                    pool.dma_start(out["new_mlstm_n"][0, 0, d, bass.ds(h, 1)], m_nst[:, d * DH:(d + 1) * DH]
                                   ).then_inc(S["m_n_stored"], 16)
                for n in range(8):
                    d, m = divmod(n, KH)
                    odd = n % 2
                    pool.wait_ge(S["m_c_copied_v" if odd else "m_c_copied_a"], 4 * h + 4 + n // 2 + 1)
                    apart(pool)
                    dst = out["new_mlstm_c"][0, 0, d, bass.ds(h, 1), m * P:(m + 1) * P].rearrange("a p n -> p (a n)")
                    pool.dma_start(dst, m_cst[n]).then_inc(S["m_c_stored_v" if odd else "m_c_stored_a"], 16)
                split_slab(pool)
                split_slab(pool)
                for m in range(KH):
                    pool.wait_ge(S["m_a_ready"], 4 * h + 4 + m + 1)
                    apart(pool)
                    for s, c in ((0, slice(0, LAT)), (1, slice(C_CTX, CONV))):
                        y = yT[:, bass.ds(KH * h + m, 1), seg(s)].rearrange("p a b -> p (a b)")
                        ins = pool.tensor_tensor(y, y, m_xc[:, m, c], ALU.mult)
                        if s == 0:
                            pool_t.mark(ins)
                    ins.then_inc(S["m_y_ready"], 1)
                pool.wait_ge(S["m_n_stored"], 32 * h + 32)
                pool.wait_ge(S["m_c_stored_a"], 64 * h + 64)
                pool.wait_ge(S["m_c_stored_v"], 64 * h + 64)
            pool_t.leave(ML_HEADS)
            slabs.leave(ML_HEADS)

        slabs = None
        act_t = dve_t = pool_t = None
        block = ctx.enter_context(nc.Block())

        @block.sync
        def _(sp):
            nonlocal slabs
            slabs = Slabs()
            setup_sync(sp)
            for l in range(layers):
                if l < ADA_AHEAD:
                    ada_sync(sp, l)
                if l % 3 == 0:
                    mla_sync(sp, l // 3)
                    out_sync(sp, t["mla_w_out"][l // 3], KD)
                elif l % 3 == 1:
                    ssd_sync(sp)
                    out_sync(sp, t["ssd_w_out"][0], KI)
                else:
                    ml_sync(sp)
                    out_sync(sp, t["ml_w_out"][0], KI)
            final_sync(sp)
            sp.wait_ge(stored, 16 * NT)

        @block.tensor
        def _(pe):
            nonlocal slabs
            slabs = Slabs()
            pe.sem_inc(w_used, 2)
            ssd_credits_pe(pe)
            setup_pe(pe)
            for l in range(layers):
                if l < ADA_AHEAD:
                    ada_pe(pe, l)
                norm_pe(pe, l)
                fence(pe, "pe")
                if l % 3 == 0:
                    mla_in_pe(pe, l // 3)
                    fence(pe, "pe")
                    mla_pe(pe, l // 3)
                    fence(pe, "pe")
                    out_pe(pe, l, KD)
                elif l % 3 == 1:
                    ssd_in_pe(pe)
                    ssd_pe(pe)
                    fence(pe, "pe")
                    out_pe(pe, l, KI)
                else:
                    ml_in_pe(pe)
                    ml_pe(pe)
                    fence(pe, "pe")
                    out_pe(pe, l, KI)
            norm_pe(pe, layers)
            fence(pe, "pe")
            final_pe(pe)

        @block.scalar
        def _(act):
            nonlocal act_t
            act_t = Tally(act, act_steps)
            setup_act_loads(act)
            mla_credits_act(act)
            ssd_credits_act(act)
            act.sem_inc(S["m_c_copied_a"], 4)
            act.sem_inc(S["m_w_ready"], NT)
            setup_act(act)
            for l in range(layers):
                norm_squares(act, l)
                fence(act, "act")
                norm_act(act, l)
                if l % 3 == 0:
                    mla_in_act(act, l // 3)
                    fence(act, "act")
                    mla_act(act, l // 3)
                elif l % 3 == 1:
                    ssd_in_act(act)
                    ssd_act(act)
                else:
                    ml_in_act(act)
                    ml_act(act)
                fence(act, "act")
                out_act(act, l, KD if l % 3 == 0 else KI)
            norm_squares(act, layers)
            fence(act, "act")
            norm_act(act, layers)
            final_copy(act, 0)

        @block.vector
        def _(dve):
            nonlocal dve_t
            dve_t = Tally(dve, dve_steps)
            credits_dve(dve)
            ssd_credits_dve(dve)
            dve.sem_inc(S["m_c_copied_v"], 4)
            dve.sem_inc(S["m_a_ready"], 4)
            setup_dve(dve)
            for l in range(layers):
                ada_dve(dve, l)
                fence(dve, "dve")
                norm_dve(dve, l)
                if l % 3 == 0:
                    mla_in_dve(dve, l // 3)
                    fence(dve, "dve")
                    mla_dve(dve, l // 3)
                    fence(dve, "dve")
                    out_dve(dve, l, KD)
                elif l % 3 == 1:
                    ssd_in_dve(dve)
                    ssd_dve(dve)
                    fence(dve, "dve")
                    out_dve(dve, l, KI, s_rstd, s_tmp)
                else:
                    ml_in_dve(dve)
                    ml_dve(dve)
                    fence(dve, "dve")
                    out_dve(dve, l, KI)
            fence(dve, "dve")
            norm_dve(dve, layers)
            final_copy(dve, 1)

        @block.gpsimd
        def _(pool):
            nonlocal pool_t, slabs
            slabs = Slabs()
            pool_t = Tally(pool, pool_steps)
            pool.sem_inc(S["m_y_ready"], 4)
            setup_pool(pool)
            for l in range(layers):
                fence(pool, "pool")
                for _ in range(ADA if l < ADA_AHEAD else 0):
                    slabs.take()
                if l % 3 == 0:
                    mla_misc_loads(pool, l // 3)
                    mla_splits(pool)
                    mla_new_store(pool, l // 3)
                    fence(pool, "pool")
                    mla_pool(pool, l // 3)
                elif l % 3 == 1:
                    ssd_pool(pool)
                else:
                    ml_pool(pool)
                fence(pool, "pool")
                out_pool(pool, KD if l % 3 == 0 else KI, l % 3)
            fence(pool, "pool")


_INS = ['x_prompt', 'x_sample', 'cache_mla_ckv', 'cache_mla_kpe', 'state_ssd', 'state_mlstm_c', 'state_mlstm_n',
        'state_mlstm_m', 'c', 'c_ctx', 'ada_w', 'ada_b', 'norm_g', 'final_norm_g', 'mla_w_in', 'mla_q_norm_g',
        'mla_kv_norm_g', 'mla_w_uq', 'mla_w_uk', 'mla_w_uv', 'mla_w_out', 'ssd_w_in', 'ssd_conv_w', 'ssd_conv_b',
        'ssd_dt_bias', 'ssd_a_log', 'ssd_d', 'ssd_norm_g', 'ssd_w_out', 'ml_w_in', 'ml_gate_b', 'ml_conv_w',
        'ml_conv_b', 'ml_w_q', 'ml_w_k', 'ml_w_v', 'ml_norm_g', 'ml_skip', 'ml_w_out']
_OUTS = [('y_prompt', (1, 128, 1024)), ('y_sample', (1, 512, 1024)), ('new_mla_ckv', (1, 2, 128, 256)),
         ('new_mla_kpe', (1, 2, 128, 32)), ('new_ssd', (1, 1, 2, 32, 64, 128)),
         ('new_mlstm_c', (1, 1, 2, 4, 512, 512)), ('new_mlstm_n', (1, 1, 2, 4, 512)), ('new_mlstm_m', (1, 1, 2, 4))]


def kernel(**inputs):
    import numpy as _np
    import concourse.bacc as _bacc
    from concourse import mybir as _mybir
    from concourse.bass_utils import run_bass_kernel_spmd as _run

    nc = _bacc.Bacc("TRN2", target_bir_lowering=False, num_devices=1)
    arrays, ins, outs = {}, {}, {}
    for name in _INS:
        a = _np.ascontiguousarray(inputs[name])
        arrays[f"in_{name}_dram"] = a
        ins[name] = nc.dram_tensor(f"in_{name}_dram", a.shape, _mybir.dt.from_np(a.dtype), kind="ExternalInput").ap()
    ins["rope"] = nc.inline_tensor(rope_table(), "rope_table").ap()
    for name, shape in _OUTS:
        outs[name] = nc.dram_tensor(f"out_{name}_dram", shape, _mybir.dt.float32, kind="ExternalOutput").ap()
    hybrid_flow_step(nc, ins, outs)
    r = _run(nc, [arrays], core_ids=[0])
    return tuple(r.results[0][f"out_{name}_dram"] for name, _ in _OUTS)
```
